# Optimizing a Trainium2 kernel written in Bass

```python
import math
import jax, jax.numpy as jnp
from jax import lax
import numpy as np

D_MODEL = 2048
BATCH = 1
SEQ = 256
DEPTH = 1

A_HEADS = 16
A_KV_HEADS = 4
A_HEAD_DIM = 64
A_GROUP = A_HEADS // A_KV_HEADS
WINDOW = 128
A_BLOCK = 128
A_Q_WIDTH = A_HEADS * A_HEAD_DIM
A_KV_WIDTH = A_KV_HEADS * A_HEAD_DIM
N_BUCKETS = 32
MAX_DISTANCE = 128
B_HEADS = 4
B_KEY_DIM = 128
B_VAL_DIM = 256
B_QK_WIDTH = B_HEADS * B_KEY_DIM
B_V_WIDTH = B_HEADS * B_VAL_DIM
B_GATE_RANK = 16
B_GATE_TAU = 16.0
B_CHUNK = 64
D_FF = -(-(8 * D_MODEL) // (3 * 256)) * 256
EPS = 1e-6
NEG_INF = -1e30

IN_SPLITS = (A_Q_WIDTH, A_KV_WIDTH, A_KV_WIDTH,
             B_QK_WIDTH, B_QK_WIDTH, B_V_WIDTH, B_GATE_RANK, B_V_WIDTH,
             D_MODEL, D_MODEL)
IN_WIDTH = sum(IN_SPLITS)


def rmsnorm(x, g):
    xf = x.astype(jnp.float32)
    y = xf * lax.rsqrt(jnp.mean(xf * xf, axis=-1, keepdims=True) + EPS)
    return (y * g.astype(jnp.float32)).astype(x.dtype)

def t5_causal_bucket(dist):
    max_exact = N_BUCKETS // 2
    d = jnp.maximum(dist, 0)
    large = max_exact + (jnp.log(jnp.maximum(d, 1).astype(jnp.float32) / max_exact)
                         / math.log(MAX_DISTANCE / max_exact)
                         * (N_BUCKETS - max_exact)).astype(jnp.int32)
    large = jnp.minimum(large, N_BUCKETS - 1)
    return jnp.where(d < max_exact, d, large)

def sliding_window_attention(q, k, v, sinks, rel_bias):
    B, S = q.shape[0], q.shape[1]
    nb = S // A_BLOCK
    qb = (q * (A_HEAD_DIM ** -0.5)).reshape(B, nb, A_BLOCK, A_KV_HEADS, A_GROUP, A_HEAD_DIM)
    pad = ((0, 0), (A_BLOCK, 0), (0, 0), (0, 0))
    kp = jnp.pad(k, pad).reshape(B, nb + 1, A_BLOCK, A_KV_HEADS, A_HEAD_DIM)
    vp = jnp.pad(v, pad).reshape(B, nb + 1, A_BLOCK, A_KV_HEADS, A_HEAD_DIM)
    kb = jnp.concatenate([kp[:, :-1], kp[:, 1:]], axis=2)
    vb = jnp.concatenate([vp[:, :-1], vp[:, 1:]], axis=2)
    s = jnp.einsum('bnqkgd,bnskd->bnkgqs', qb, kb).astype(jnp.float32)
    q_loc = jnp.arange(A_BLOCK)[:, None] + A_BLOCK
    k_loc = jnp.arange(2 * A_BLOCK)[None, :]
    dist = q_loc - k_loc
    band = (dist >= 0) & (dist < WINDOW)
    k_abs = jnp.arange(nb)[:, None, None] * A_BLOCK + k_loc[None] - A_BLOCK
    mask = band[None] & (k_abs >= 0)
    bias = rel_bias.astype(jnp.float32)[t5_causal_bucket(dist)]
    bias = bias.transpose(2, 0, 1).reshape(A_KV_HEADS, A_GROUP, A_BLOCK, 2 * A_BLOCK)
    s = jnp.where(mask[None, :, None, None], s + bias[None, None], NEG_INF)
    sink = sinks.astype(jnp.float32).reshape(A_KV_HEADS, A_GROUP)[None, None, :, :, None, None]
    m = jnp.maximum(jnp.max(s, axis=-1, keepdims=True), sink)
    p = jnp.exp(s - m)
    denom = jnp.sum(p, axis=-1, keepdims=True) + jnp.exp(sink - m)
    o = jnp.einsum('bnkgqs,bnskd->bnqkgd', (p / denom).astype(v.dtype), vb)
    return o.reshape(B, S, A_Q_WIDTH)

def gated_linear_attention(q, k, v, log_a):
    B, S = q.shape[0], q.shape[1]
    nc = S // B_CHUNK

    def chunks(t):
        return t.astype(jnp.float32).reshape(B, nc, B_CHUNK, B_HEADS, -1).transpose(0, 3, 1, 2, 4)

    qc = chunks(q) * (B_KEY_DIM ** -0.5)
    kc, vc, gc = chunks(k), chunks(v), chunks(log_a)
    b = jnp.cumsum(gc, axis=3)
    b_last = b[:, :, :, -1:, :]
    q_dec = qc * jnp.exp(b)
    k_dec = kc * jnp.exp(-b)
    k_state = kc * jnp.exp(b_last - b)
    causal = jnp.tril(jnp.ones((B_CHUNK, B_CHUNK), dtype=bool))
    att = jnp.where(causal, jnp.einsum('bhncd,bhnsd->bhncs', q_dec, k_dec), 0.0)
    o_intra = jnp.einsum('bhncs,bhnsv->bhncv', att, vc)
    dS = jnp.einsum('bhncd,bhncv->bhndv', k_state, vc)
    decay = jnp.exp(b_last[:, :, :, 0, :])

    def step(state, inp):
        dS_n, decay_n = inp
        return decay_n[..., None] * state + dS_n, state

    s0 = jnp.zeros((B, B_HEADS, B_KEY_DIM, B_VAL_DIM), jnp.float32)
    _, s_prev = lax.scan(step, s0, (dS.transpose(2, 0, 1, 3, 4), decay.transpose(2, 0, 1, 3)))
    s_prev = s_prev.transpose(1, 2, 0, 3, 4)
    o_inter = jnp.einsum('bhncd,bhndv->bhncv', q_dec, s_prev)
    o = o_intra + o_inter
    return o.transpose(0, 2, 3, 1, 4).reshape(B, S, B_HEADS, B_VAL_DIM)

def first_inputs(seed: int = 0) -> dict:
    key = jax.random.key(seed)
    ks = jax.random.split(key, 20)
    L = DEPTH

    def w(k, shape, fan_in):
        return jax.random.normal(k, shape, jnp.float32) * (fan_in ** -0.5)

    def gain(k, shape):
        return 1.0 + 0.02 * jax.random.normal(k, shape, jnp.float32)

    return {
        "x": jax.random.normal(ks[0], (BATCH, SEQ, D_MODEL), jnp.float32),
        "norm_mix_g": gain(ks[1], (L, D_MODEL)),
        "w_in": w(ks[2], (L, D_MODEL, IN_WIDTH), D_MODEL),
        "sinks": 0.5 * jax.random.normal(ks[3], (L, A_HEADS), jnp.float32),
        "rel_bias": 0.5 * jax.random.normal(ks[4], (N_BUCKETS, A_HEADS), jnp.float32),
        "w_gate_up": w(ks[5], (L, B_GATE_RANK, B_QK_WIDTH), B_GATE_RANK),
        "b_gate": 0.1 * jax.random.normal(ks[6], (L, B_QK_WIDTH), jnp.float32),
        "gla_norm_g": gain(ks[7], (L, B_VAL_DIM)),
        "w_proj_a": w(ks[8], (L, A_Q_WIDTH, D_MODEL), A_Q_WIDTH),
        "w_proj_b": w(ks[9], (L, B_V_WIDTH, D_MODEL), B_V_WIDTH),
        "w_out": w(ks[10], (L, D_MODEL, D_MODEL), D_MODEL),
        "norm_ffn_g": gain(ks[11], (L, D_MODEL)),
        "w_ffn_gate": w(ks[12], (L, D_MODEL, D_FF), D_MODEL),
        "w_ffn_up": w(ks[13], (L, D_MODEL, D_FF), D_MODEL),
        "w_ffn_down": w(ks[14], (L, D_FF, D_MODEL), D_FF),
        "norm_final_g": gain(ks[15], (D_MODEL,)),
    }

def first_block(x, norm_mix_g, w_in, sinks, rel_bias, w_gate_up, b_gate, gla_norm_g,
              w_proj_a, w_proj_b, w_out, norm_ffn_g, w_ffn_gate, w_ffn_up, w_ffn_down,
              norm_final_g):
    B, S = x.shape[0], x.shape[1]
    split_idx = [int(i) for i in np.cumsum(IN_SPLITS)[:-1]]
    h = x
    for l in range(DEPTH):
        u = rmsnorm(h, norm_mix_g[l])
        proj = u @ w_in[l]
        qa, ka, va, qb, kb, vb, g_low, ob_gate, gate_a, gate_b = jnp.split(proj, split_idx, axis=-1)
        ya = sliding_window_attention(
            qa.reshape(B, S, A_HEADS, A_HEAD_DIM),
            ka.reshape(B, S, A_KV_HEADS, A_HEAD_DIM),
            va.reshape(B, S, A_KV_HEADS, A_HEAD_DIM),
            sinks[l], rel_bias)
        ya = ya @ w_proj_a[l]
        log_a = jax.nn.log_sigmoid((g_low @ w_gate_up[l] + b_gate[l]).astype(jnp.float32)) / B_GATE_TAU
        ob = gated_linear_attention(
            qb.reshape(B, S, B_HEADS, B_KEY_DIM),
            kb.reshape(B, S, B_HEADS, B_KEY_DIM),
            vb.reshape(B, S, B_HEADS, B_VAL_DIM),
            log_a.reshape(B, S, B_HEADS, B_KEY_DIM))
        ob = rmsnorm(ob, gla_norm_g[l]).reshape(B, S, B_V_WIDTH).astype(x.dtype)
        yb = (ob * jax.nn.silu(ob_gate)) @ w_proj_b[l]
        merged = jax.nn.sigmoid(gate_a) * ya + jax.nn.sigmoid(gate_b) * yb
        h = h + (merged @ w_out[l]).astype(h.dtype)
        z = rmsnorm(h, norm_ffn_g[l])
        ff = (jax.nn.silu(z @ w_ffn_gate[l]) * (z @ w_ffn_up[l])) @ w_ffn_down[l]
        h = h + ff.astype(h.dtype)
    return rmsnorm(h, norm_final_g)


CHUNK = 64
Q_BLOCK = 128
ROPE_THETA = 500000.0
N_MEM = 256

MLA_HEADS = 8
MLA_NOPE = 128
MLA_ROPE = 64
MLA_V = 128
MLA_Q_LORA = 512
MLA_KV_LORA = 256
DSA_HEADS = 8
DSA_HEAD_DIM = 128
DSA_ROT = DSA_HEAD_DIM // 4
IDX_HEADS = 16
IDX_DIM = 64
IDX_ROT = IDX_DIM // 4
TOPK_MAX = 256
X_HEADS = 4
X_HEAD_DIM = 128
D_FF_2 = 4 * D_MODEL

MIX_WIDTH = MLA_HEADS * MLA_V + DSA_HEADS * DSA_HEAD_DIM
IN_SPLITS_2 = (
    MLA_Q_LORA,
    MLA_KV_LORA,
    MLA_ROPE,
    DSA_HEADS * DSA_HEAD_DIM,
    DSA_HEADS * DSA_HEAD_DIM,
    DSA_HEADS * DSA_HEAD_DIM,
    IDX_HEADS * IDX_DIM,
    IDX_DIM,
    IDX_HEADS,
)
D_IN = int(sum(IN_SPLITS_2))


def rmsnorm_2(x, g):
    xf = x.astype(jnp.float32)
    y = xf * lax.rsqrt(jnp.mean(xf * xf, axis=-1, keepdims=True) + EPS)
    return (y * g.astype(jnp.float32)).astype(x.dtype)

def rope(x, pos, rot_dim):
    half = rot_dim // 2
    inv_freq = ROPE_THETA ** (-jnp.arange(half, dtype=jnp.float32) / half)
    ang = pos.astype(jnp.float32)[..., None] * inv_freq
    ang = ang.reshape(ang.shape[:2] + (1,) * (x.ndim - 3) + (half,))
    cos, sin = jnp.cos(ang), jnp.sin(ang)
    xf = x.astype(jnp.float32)
    x1, x2, rest = xf[..., :half], xf[..., half:rot_dim], xf[..., rot_dim:]
    out = jnp.concatenate([x1 * cos - x2 * sin, x2 * cos + x1 * sin, rest], axis=-1)
    return out.astype(x.dtype)

def to_blocks(a):
    b, s = a.shape[:2]
    a = a.reshape((b, s // Q_BLOCK, Q_BLOCK) + a.shape[2:])
    return jnp.moveaxis(a, 1, 0)

def from_blocks(a):
    a = jnp.moveaxis(a, 0, 1)
    return a.reshape((a.shape[0], a.shape[1] * a.shape[2]) + a.shape[3:])

def query_chunks(i):
    return (i * Q_BLOCK + jnp.arange(Q_BLOCK)) // CHUNK

def mla_mixer(c_q, c_kv, k_rope, pos, g_cq, g_ckv, w_qb, w_kvb):
    b, s, _ = c_q.shape
    q = (rmsnorm_2(c_q, g_cq) @ w_qb).reshape(b, s, MLA_HEADS, MLA_NOPE + MLA_ROPE)
    q_nope = q[..., :MLA_NOPE]
    q_rope = rope(q[..., MLA_NOPE:], pos, MLA_ROPE)
    kv = (rmsnorm_2(c_kv, g_ckv) @ w_kvb).reshape(b, s, MLA_HEADS, MLA_NOPE + MLA_V)
    k_nope, v = kv[..., :MLA_NOPE], kv[..., MLA_NOPE:]
    k_rope = rope(k_rope, pos, MLA_ROPE)
    scale = (MLA_NOPE + MLA_ROPE) ** -0.5
    key_chunk = jnp.arange(s) // CHUNK

    def block(args):
        i, qn, qr = args
        sc = (jnp.einsum('bqhd,bkhd->bhqk', qn, k_nope)
              + jnp.einsum('bqhr,bkr->bhqk', qr, k_rope)).astype(jnp.float32) * scale
        allowed = key_chunk[None, :] <= query_chunks(i)[:, None]
        sc = jnp.where(allowed[None, None], sc, -jnp.inf)
        p = jax.nn.softmax(sc, axis=-1).astype(v.dtype)
        return jnp.einsum('bhqk,bkhd->bqhd', p, v)

    o = lax.map(block, (jnp.arange(s // Q_BLOCK), to_blocks(q_nope), to_blocks(q_rope)))
    return from_blocks(o).reshape(b, s, MLA_HEADS * MLA_V)

def dsa_mixer(q, k, v, q_idx, k_idx, w_idx, pos):
    b, s, _ = q.shape
    q = rope(q.reshape(b, s, DSA_HEADS, DSA_HEAD_DIM), pos, DSA_ROT)
    k = rope(k.reshape(b, s, DSA_HEADS, DSA_HEAD_DIM), pos, DSA_ROT)
    v = v.reshape(b, s, DSA_HEADS, DSA_HEAD_DIM)
    q_idx = rope(q_idx.reshape(b, s, IDX_HEADS, IDX_DIM), pos, IDX_ROT)
    k_idx = rope(k_idx, pos, IDX_ROT)
    w_idx = w_idx * (IDX_HEADS ** -0.5)
    n_sel = min(TOPK_MAX, s // 4)
    key_chunk = jnp.arange(s) // CHUNK
    gather = jax.vmap(lambda arr, idx: arr[idx])

    def block(args):
        i, qb, qib, wb = args
        qc = query_chunks(i)
        logits = jax.nn.relu(jnp.einsum('bqhd,bkd->bqhk', qib, k_idx).astype(jnp.float32) * (IDX_DIM ** -0.5))
        score = jnp.einsum('bqhk,bqh->bqk', logits, wb.astype(jnp.float32))
        allowed = key_chunk[None, :] <= qc[:, None]
        score = jnp.where(allowed[None], score, -jnp.inf)
        _, sel = lax.top_k(score, n_sel)
        sel_ok = (sel // CHUNK) <= qc[None, :, None]
        k_sel = gather(k, sel)
        v_sel = gather(v, sel)
        sc = jnp.einsum('bqhd,bqnhd->bhqn', qb, k_sel).astype(jnp.float32) * (DSA_HEAD_DIM ** -0.5)
        sc = jnp.where(sel_ok[:, None], sc, -jnp.inf)
        p = jax.nn.softmax(sc, axis=-1).astype(v.dtype)
        return jnp.einsum('bhqn,bqnhd->bqhd', p, v_sel)

    o = lax.map(block, (jnp.arange(s // Q_BLOCK), to_blocks(q), to_blocks(q_idx), to_blocks(w_idx)))
    return from_blocks(o).reshape(b, s, DSA_HEADS * DSA_HEAD_DIM)

def memory_cross_attention(h, mem_n, wq, wk, wv, wo):
    b, s, _ = h.shape
    m = mem_n.shape[1]
    q = (h @ wq).reshape(b, s, X_HEADS, X_HEAD_DIM)
    k = (mem_n @ wk).reshape(b, m, X_HEADS, X_HEAD_DIM)
    v = (mem_n @ wv).reshape(b, m, X_HEADS, X_HEAD_DIM)
    sc = jnp.einsum('bshd,bmhd->bhsm', q, k).astype(jnp.float32) * (X_HEAD_DIM ** -0.5)
    p = jax.nn.softmax(sc, axis=-1).astype(v.dtype)
    o = jnp.einsum('bhsm,bmhd->bshd', p, v).reshape(b, s, X_HEADS * X_HEAD_DIM)
    return o @ wo

def second_inputs(seed: int = 0) -> dict:
    key = jax.random.key(seed)
    ks = jax.random.split(key, 24)
    f32 = jnp.float32

    def w(k, shape, fan_in):
        return jax.random.normal(k, (DEPTH,) + shape, f32) * (fan_in ** -0.5)

    def gain(k, n):
        return 1.0 + 0.02 * jax.random.normal(k, (DEPTH, n), f32)

    x = jax.random.normal(ks[0], (BATCH, SEQ, D_MODEL), f32)
    mem = jax.random.normal(ks[1], (BATCH, N_MEM, D_MODEL), f32)
    offset = jax.random.randint(ks[2], (BATCH, 1), 0, 16, dtype=jnp.int32) * CHUNK
    positions = (offset + jnp.arange(SEQ, dtype=jnp.int32)[None, :]).astype(jnp.int32)
    return {
        "x": x,
        "mem": mem,
        "positions": positions,
        "g_mix": gain(ks[3], D_MODEL),
        "w_in": w(ks[4], (D_MODEL, D_IN), D_MODEL),
        "g_cq": gain(ks[5], MLA_Q_LORA),
        "g_ckv": gain(ks[6], MLA_KV_LORA),
        "w_qb": w(ks[7], (MLA_Q_LORA, MLA_HEADS * (MLA_NOPE + MLA_ROPE)), MLA_Q_LORA),
        "w_kvb": w(ks[8], (MLA_KV_LORA, MLA_HEADS * (MLA_NOPE + MLA_V)), MLA_KV_LORA),
        "w_out": w(ks[9], (MIX_WIDTH, D_MODEL), MIX_WIDTH),
        "g_cross": gain(ks[10], D_MODEL),
        "g_mem": gain(ks[11], D_MODEL),
        "w_q_cross": w(ks[12], (D_MODEL, X_HEADS * X_HEAD_DIM), D_MODEL),
        "w_k_cross": w(ks[13], (D_MODEL, X_HEADS * X_HEAD_DIM), D_MODEL),
        "w_v_cross": w(ks[14], (D_MODEL, X_HEADS * X_HEAD_DIM), D_MODEL),
        "w_o_cross": w(ks[15], (X_HEADS * X_HEAD_DIM, D_MODEL), X_HEADS * X_HEAD_DIM),
        "g_mlp": gain(ks[16], D_MODEL),
        "w_up": w(ks[17], (D_MODEL, D_FF_2), D_MODEL),
        "w_down": w(ks[18], (D_FF_2, D_MODEL), D_FF_2),
        "g_final": 1.0 + 0.02 * jax.random.normal(ks[19], (D_MODEL,), f32),
    }

def second_block(x, mem, positions, g_mix, w_in, g_cq, g_ckv, w_qb, w_kvb, w_out,
              g_cross, g_mem, w_q_cross, w_k_cross, w_v_cross, w_o_cross,
              g_mlp, w_up, w_down, g_final):
    offsets = np.cumsum(np.array(IN_SPLITS_2))[:-1].tolist()
    for l in range(DEPTH):
        h = rmsnorm_2(x, g_mix[l])
        c_q, c_kv, k_rope, q_d, k_d, v_d, q_idx, k_idx, w_idx = jnp.split(h @ w_in[l], offsets, axis=-1)
        a = mla_mixer(c_q, c_kv, k_rope, positions, g_cq[l], g_ckv[l], w_qb[l], w_kvb[l])
        bb = dsa_mixer(q_d, k_d, v_d, q_idx, k_idx, w_idx, positions)
        x = x + jnp.concatenate([a, bb], axis=-1) @ w_out[l]
        hc = rmsnorm_2(x, g_cross[l])
        mem_n = rmsnorm_2(mem, g_mem[l])
        x = x + memory_cross_attention(hc, mem_n, w_q_cross[l], w_k_cross[l], w_v_cross[l], w_o_cross[l])
        hm = rmsnorm_2(x, g_mlp[l])
        x = x + jnp.square(jax.nn.relu(hm @ w_up[l])) @ w_down[l]
    return rmsnorm_2(x, g_final)


def setup_inputs(seed=0):
    out = dict(first_inputs(seed))
    for name, value in second_inputs(seed + 1).items():
        if name != "x":
            out[name + "_2"] = value
    return out


def reference(
    x, norm_mix_g, w_in, sinks, rel_bias, w_gate_up, b_gate, gla_norm_g, w_proj_a, w_proj_b,
    w_out, norm_ffn_g, w_ffn_gate, w_ffn_up, w_ffn_down, norm_final_g, mem_2, positions_2,
    g_mix_2, w_in_2, g_cq_2, g_ckv_2, w_qb_2, w_kvb_2, w_out_2, g_cross_2, g_mem_2, w_q_cross_2,
    w_k_cross_2, w_v_cross_2, w_o_cross_2, g_mlp_2, w_up_2, w_down_2, g_final_2,
):
    x = first_block(
        x, norm_mix_g, w_in, sinks, rel_bias, w_gate_up, b_gate, gla_norm_g, w_proj_a, w_proj_b,
        w_out, norm_ffn_g, w_ffn_gate, w_ffn_up, w_ffn_down, norm_final_g,
    )
    return second_block(
        x, mem_2, positions_2, g_mix_2, w_in_2, g_cq_2, g_ckv_2, w_qb_2, w_kvb_2, w_out_2,
        g_cross_2, g_mem_2, w_q_cross_2, w_k_cross_2, w_v_cross_2, w_o_cross_2, g_mlp_2, w_up_2,
        w_down_2, g_final_2,
    )


_drawn_inputs = setup_inputs


def setup_inputs(seed=0):
    import zlib

    import numpy as np

    out = dict(_drawn_inputs(seed))
    spreads = {}
    factors = {'sinks': 4.952,
     'gla_norm_g': 3.458,
     'g_cq_2': 8.0,
     'g_ckv_2': 8.0,
     'g_cross_2': 8.0,
     'g_mem_2': 8.0,
     'g_mlp_2': 9.563,
     'g_final_2': 7.934}
    for name, (base, spread) in spreads.items():
        noise = np.random.default_rng([zlib.crc32(name.encode()), seed]).standard_normal(out[name].shape)
        drawn = base * np.exp(spread * noise) if base else spread * noise
        out[name] = __import__('jax').numpy.asarray(drawn.astype(out[name].dtype))
    for name, factor in factors.items():
        out[name] = (out[name] * factor).astype(out[name].dtype)
    return out
```

```python
from contextlib import ExitStack

import numpy as np

import concourse.bass as bass
from concourse import mybir

F32 = mybir.dt.float32
F32R = mybir.dt.float32r
I32 = mybir.dt.int32
ALU = mybir.AluOpType
ACT = mybir.ActivationFunctionType
X = mybir.AxisListType.X

P = 128
SEQ, D = 256, 2048
NT = SEQ // P
DC = D // P
EPS = 1e-6
NEG = -1e30
RING = 4
LEAD = RING - 1
CK = 2
COLS = 512

A_HEADS, A_KV, A_DIM = 16, 4, 64
G_HEADS, G_KEY, G_VAL, G_RANK, CHUNK = 4, 128, 256, 16, 64
M_HEADS, M_NOPE, M_ROPE, M_VAL = 8, 128, 64, 128
S_HEADS, S_DIM, S_ROT = 8, 128, 32
I_HEADS, I_DIM, I_ROT = 16, 64, 16
TOPK = 64
TWO_PI = 2 * np.pi
TWO_PI_PARTS = (6.28125, float(np.float16(TWO_PI - 6.28125)), float(TWO_PI - 6.28125 - float(np.float16(TWO_PI - 6.28125))))
PI_BELOW = float(np.nextafter(np.float32(np.pi), np.float32(0)))
ROUND = 1.5 * 2.0 ** 23
C_HEADS, C_DIM = 4, 128
D_FF1, D_FF2 = 5632, 8192

IN1_GLOW = 3 * COLS + 4 * COLS
IN1_OBG = IN1_GLOW + G_RANK
IN1_GA = IN1_OBG + G_HEADS * G_VAL
IN1_GB = IN1_GA + D
IN2_CQ, IN2_CKV, IN2_QD = 0, 512, 832
IN2_QI = IN2_QD + 3 * S_HEADS * S_DIM
IN2_KI = IN2_QI + I_HEADS * I_DIM
IN2_END = IN2_KI + I_DIM + I_HEADS

C_IDENT, C_TRI, C_REST, C_CAUSAL, C_ZERO, C_CMASK, C_IND, C_FREQ, C_HOT = 0, 128, 256, 384, 512, 640, 768, 770, 802
C_BIASW = 384
C_END = C_HOT + C_BIASW


def constants():
    c = np.zeros((P, C_END), np.float32)
    s, t = np.arange(P)[:, None], np.arange(P)[None, :]
    same = s // CHUNK == t // CHUNK
    c[:, C_IDENT:C_IDENT + P] = s == t
    c[:, C_TRI:C_TRI + P] = (same & (s <= t)) / 16.0
    c[:, C_REST:C_REST + P] = (same & (s > t)) / 16.0
    c[:, C_CAUSAL:C_CAUSAL + P] = same & (s <= t)
    c[:, C_CMASK:C_CMASK + P] = np.where(t // CHUNK <= s // CHUNK, 0.0, NEG)
    c[:, C_IND:C_IND + 2] = (s // CHUNK == np.arange(2)[None]) / 16.0
    half = M_ROPE // 2
    c[:, C_FREQ:C_FREQ + half] = (500000.0 ** (-np.arange(half) / half)).astype(np.float32)
    dist = 255 - np.arange(C_BIASW)
    d = np.maximum(dist, 0)
    large = 16 + (np.log(np.maximum(d, 1).astype(np.float32) / 16) / np.float32(np.log(8.0)) * 16).astype(np.int32)
    bucket = np.where(d < 16, d, np.minimum(large, 31))
    seen = (dist >= 0) & (dist < 128)
    for m in range(C_BIASW):
        if seen[m]:
            c[bucket[m], C_HOT + m] = 1.0
        else:
            c[32, C_HOT + m] = NEG
    return c


TRANSPOSES = {
}


def xp(name, src, col, width, n, dst, idx, mode):
    TRANSPOSES[name] = (src, col, width, n, dst, idx, mode)


for j in range(4):
    xp(f"mem{j}", "u_mem", 512 * j, 128, 4, "memT", 4 * j, "split")
    xp(f"u{j}", "u", 512 * j, 128, 4, "xT", 4 * j, "split")
    xp(f"aq{j}", "qkva", 256 * j, 64, 4, "aqT", 4 * j, "act" if j % 2 else "dve")
    xp(f"merged{j}", "merged", 512 * j, 128, 4, "xT", 4 * j, "split")
xp("ak", "qkva", 1024, 64, 4, "akT", 0, "act")
for j in range(2):
    xp(f"ya{j}", "qkva", 512 * j, 128, 4, "yT", 4 * j, "split")
    xp(f"yb{j}", "gla", 512 * j, 128, 4, "yT", 8 + 4 * j, "split")
xp("glow", "glow", 0, 16, 1, "glowT", 0, "dve")
xp("gq", "gla", 0, 128, 4, "gqT", 0, "act")
xp("gk", "gla", 512, 128, 4, "gkT", 0, "act")
for j in range(4):
    xp(f"iq{j}", "idx", 256 * j, 64, 4, "iqT", 4 * j, "act" if j % 2 else "dve")
xp("ik", "idx", 1024, 64, 1, "ikT", 0, "act")
xp("cq", "c", 0, 128, 4, "cT", 0, "split")
xp("ckv", "c", 512, 128, 2, "cT", 4, "split")
xp("kr", "c", 768, 64, 1, "krT", 0, "act")
for j in range(2):
    xp(f"mq{j}", "mq", j, 128, 4, "mqT", 4 * j, "act")
    xp(f"mr{j}", "mr", j, 64, 4, "mrT", 4 * j, "dve")
    xp(f"mk{j}", "mkv", j, 128, 4, "mkT", 4 * j, "act")
    xp(f"a{j}", "mout", 512 * j, 128, 4, "xT", 4 * j, "split")
    xp(f"sq{j}", "dsa", 512 * j, 128, 4, "sqT", 4 * j, "act")
    xp(f"sk{j}", "dsa", 1024 + 512 * j, 128, 4, "skT", 4 * j, "dve")
    xp(f"s{j}", "dsa", 512 * j, 128, 4, "xT", 8 + 4 * j, "split")
xp("ck", "ckv", 0, 128, 4, "ckT", 0, "act")
xp("cqq", "cqo", 0, 128, 4, "cqT", 0, "dve")
xp("co", "cqo", 0, 128, 4, "coT", 0, "split")


def attention_groups():
    groups = []
    for kind, heads in (("A", A_HEADS), ("M", M_HEADS), ("S", S_HEADS), ("C", C_HEADS)):
        for t in range(NT):
            for h in range(0, heads, 2):
                groups.append((kind, t, h, SEQ if t or kind == "C" else P))
    return groups


GROUPS = attention_groups()
GROUP0 = {k: [g[0] for g in GROUPS].index(k) for k in "AMSC"}
NGROUPS = {k: sum(g[0] == k for g in GROUPS) for k in "AMSC"}


def attention_slots(kind):
    a, n = GROUP0[kind], NGROUPS[kind]
    slots = []
    for j in range(n + 2):
        slot = []
        if 0 <= j - 1 < n:
            slot.append(("probs_T", a + j - 1))
        if 0 <= j - 2 < n:
            slot.append(("output", a + j - 2))
        if j < n:
            slot.append(("scores", a + j))
        slots.append(slot)
    return slots


def block_steps(w, k0, kc, c0, nc_, lhs, l0, evac, arg=0, first_unit=None):
    n = -(-kc // CK)
    b = dict(w=w, k0=k0, kc=kc, c0=c0, n=nc_, lhs=lhs, l0=l0, evac=evac, arg=arg, need=first_unit)
    return [("tile", b, k) for k in range(n)] + [("evac", b)]


def both(name, slots=False):
    return [("T", name, t) for t in range(NT)]


def weave(dense, slots, every):
    out, slots, n = [], list(slots), 0
    for s in dense:
        out.append(s)
        if s[0] == "tile":
            n += 1
            if n % every == 0 and slots:
                out += slots.pop(0)
    for s in slots:
        out += s
    return out


def schedule():
    S = []
    S += [("norm", 0, "mem"), ("prime",)] + [("T", f"mem{j}", t) for t in range(NT) for j in range(4)]
    S += [("norm", 1, "x")]
    xu = [[("T", f"u{j}", t)] for t in range(NT) for j in range(4)]
    S += weave(block_steps("w_k_cross_2", 0, DC, 0, 512, "memT", 0, "ckv", 0, "mem3")
               + block_steps("w_v_cross_2", 0, DC, 0, 512, "memT", 0, "ckv", 1), [[], []] + xu, 1)
    S += [("keep_ckv",), ("bias_row",)]
    w = lambda c0, n, evac, arg=0, need=None: block_steps("w_in", 0, DC, c0, n, "xT", 0, evac, arg, need)
    S += w(0, 512, "qkva", 0, "u3") + w(512, 512, "qkva", 512) + w(1024, 512, "qkva", 1024)
    dense = []
    for j in range(4):
        dense += w(1536 + 512 * j, 512, "gla", 512 * j)
    dense += w(IN1_GLOW, G_RANK, "glow")
    dense += w(IN1_OBG, 512, "obg", 0) + w(IN1_OBG + 512, 512, "obg", 512)
    for j in range(4):
        dense += w(IN1_GA + 512 * j, 512, "sigA", 512 * j)
    for j in range(4):
        dense += w(IN1_GB + 512 * j, 512, "sigB", 512 * j)
    a_slots = [both(f"aq{j}") for j in range(4)] + [both("ak")] + attention_slots("A")
    g_slots = a_slots + [
        both("glow"), [("gate_z", t) for t in range(NT)], [("gate_sum", t) for t in range(NT)],
        [("gate_rest", t) for t in range(NT)], [("gate_decay",)], both("gq"), both("gk")]
    g_slots += [[("state", n, h)] for n in range(3) for h in (0, 2)]
    g_slots += [[("gla_att", t)] for t in range(NT)]
    g_slots += [[("gla_out", t, h)] for t in range(NT) for h in (0, 2)]
    g_slots += [[("gla_norm",)]]
    g_slots += [both(f"ya{j}") for j in range(2)] + [both(f"yb{j}") for j in range(2)]
    S += weave(dense, g_slots, 2)
    for j in range(4):
        S += block_steps("w_proj_a", 0, 8, 512 * j, 512, "yT", 0, "none", 0, "yb1" if not j else None)
        S += block_steps("w_proj_b", 0, 8, 512 * j, 512, "yT", 8, "merge", 512 * j)
    S += [("load_x",)] + [("T", f"merged{j}", t) for j in range(4) for t in range(NT)]
    for j in range(4):
        S += block_steps("w_out", 0, DC, 512 * j, 512, "xT", 0, "add", 512 * j, "merged3" if not j else None)
    S += [("norm", 2, "x")] + [("T", f"u{j}", t) for t in range(NT) for j in range(4)]
    g0 = 0
    for n in (6, 5):
        S += [("swiglu_up", g0, n), ("down", "w_ffn_down", 4 * g0, 4 * n)]
        g0 += n
    S += [("norm", 3, "final1")]
    S += [("norm", 4, "x")] + [("T", f"u{j}", t) for t in range(NT) for j in range(4)]
    w = lambda c0, n, evac, arg=0, need=None: block_steps("w_in_2", 0, DC, c0, n, "xT", 0, evac, arg, need)
    S += [("angles",)]
    S += w(IN2_QI, 512, "idx", 0, "u3") + w(IN2_QI + 512, 512, "idx", 512) + w(IN2_KI, 80, "idx", 1024)
    S += [("rope", "idx")]
    dense = w(IN2_CQ, 512, "c", 0) + w(IN2_CKV, 320, "c", 512)
    slots = [both(f"iq{j}") for j in range(4)] + [both("ik")]
    slots += [[("idx", t, h)] for t in range(NT) for h in range(0, I_HEADS, 2)]
    S += weave(dense, slots, 1)
    S += [("rope", "kr"), ("c_norm",)] + both("cq") + both("ckv") + both("kr")
    for j in range(4):
        S += block_steps("w_qb_2", 0, 4, 384 * j, 384, "cT", 0, "mq", 384 * j, "kr" if not j else None)
    for j in range(4):
        S += block_steps("w_kvb_2", 0, 2, 512 * j, 512, "cT", 4, "mkv", 512 * j)
    S += [("rope", "mq")]
    dense = []
    for j in range(6):
        dense += w(IN2_QD + 512 * j, 512, "dsa", 512 * j)
    slots = [both(f"mk{j}") for j in range(2)] + [both(f"mq{j}") for j in range(2)] + [both(f"mr{j}") for j in range(2)]
    m_slots = attention_slots("M")
    rounds = [("topk", t, r) for t in range(NT) for r in range(TOPK // 8)]
    slots += [m + rounds[2 * i:2 * i + 2] for i, m in enumerate(m_slots)]
    S += weave(dense, slots, 2)
    S += [("rope", "dsa")] + both("a0") + both("a1")
    dense = []
    for j in range(4):
        dense += block_steps("w_out_2", 0, 8, 512 * j, 512, "xT", 0, "add", 512 * j, "a1" if not j else None)
    slots = [both("sq0") + both("sk0")] + [both("sq1") + both("sk1")] + attention_slots("S")
    S += weave(dense, slots, 1)
    S += both("s0") + both("s1")
    for j in range(4):
        S += block_steps("w_out_2", 8, 8, 512 * j, 512, "xT", 8, "add", 512 * j, "s1" if not j else None)
    S += [("norm", 5, "x")] + [("T", f"u{j}", t) for t in range(NT) for j in range(4)]
    S += weave(block_steps("w_q_cross_2", 0, DC, 0, 512, "xT", 0, "cqo", 0, "u3"), [both("ck")], 2)
    S += both("cqq")
    for s in attention_slots("C"):
        S += s
    S += both("co")
    for j in range(4):
        S += block_steps("w_o_cross_2", 0, 4, 512 * j, 512, "coT", 0, "add", 512 * j, "co" if not j else None)
    S += [("norm", 6, "x")] + [("T", f"u{j}", t) for t in range(NT) for j in range(4)]
    g0 = 0
    for n in (6, 6, 4):
        S += [("relu2_up", g0, n), ("down", "w_down_2", 4 * g0, 4 * n)]
        g0 += n
    S += [("norm", 7, "out")]
    return number(S)


UNIT_STEPS = {"T": 1, "probs_T": 1, "bias_row": 1, "gate_z": 1, "gate_sum": 1, "gate_rest": 1,
              "gate_decay": 1, "state": 1, "gla_att": 1, "gla_out": 1, "idx": 1}


def number(steps):
    out, tiles, blocks, units, splits, hidden, wrote, seen = [], 0, 0, 0, 0, {}, {}, {}
    for s in steps:
        at = dict(tile=tiles, block=blocks, unit=units, split=splits, nth=seen.get(s[0], 0), h=hidden.get(s[0], 0),
                  u3=wrote.get("u3"))
        seen[s[0]] = at["nth"] + 1
        if s[0] == "tile":
            at["need"] = wrote[s[1]["need"]] if s[1]["need"] and s[2] == 0 else None
            at["last"] = s[2] == -(-s[1]["kc"] // CK) - 1
            tiles += 1
        elif s[0] == "evac":
            blocks += 1
        elif s[0] in UNIT_STEPS:
            if s[0] == "T":
                wrote[s[1]] = units
                splits += TRANSPOSES[s[1]][6] == "split"
            units += 1
        elif s[0] in ("swiglu_up", "relu2_up"):
            assert units % 2 == 0 and blocks % 2 == 0, (s, units, blocks)
            nb = 2 * s[2] if s[0] == "swiglu_up" else s[2]
            tiles += 8 * nb
            blocks += nb
            units += 2 * s[2]
            splits += 2 * s[2]
            hidden[s[0]] = at["h"] + 2 * s[2]
            assert tiles % RING == 0
        elif s[0] == "down":
            assert blocks % 2 == 0
            tiles += 4 * (s[3] // CK)
            blocks += 4
        out.append((s, at))
    return out, tiles, wrote


def build(nc, t_in, out):
    SCHEDULE, TILES, LAST_UNIT = schedule()
    ctx = ExitStack()
    with ctx:
        def sem(name):
            return ctx.enter_context(nc.semaphore(name))

        base = (nc.sbuf_base + 63) // 64 * 64
        top = [base]

        def put(name, shape, dt=F32, at=None):
            size = 4 * int(np.prod(shape[1:]))
            off = top[0] if at is None else at
            if at is None:
                top[0] += (size + 63) // 64 * 64
            assert off + size <= nc.sbuf_usable_end, (name, off + size - nc.sbuf_usable_end)
            return nc.alloc_sbuf_tensor_at(name, shape, dt, offset=off)

        w_raw = put("w_raw", [P, RING, CK, COLS])
        w_hi = put("w_hi", [P, RING, CK, COLS], F32R)
        w_lo = put("w_lo", [P, RING, CK, COLS], F32R)
        xT = (put("xT_hi", [P, DC, SEQ], F32R), put("xT_lo", [P, DC, SEQ], F32R))
        cst = put("cst", [P, C_END])
        stat = put("stat", [P, 128])
        X0 = top[0]
        x_sb = put("x_sb", [P, NT, D])
        ARENA = top[0]
        K = 1024

        def arena(name, shape, at, dt=F32):
            return put(name, shape, dt, at=ARENA + int(at * K))

        sigB = put("sigB", [P, NT, D], at=X0)
        sigA = arena("sigA", [P, NT, D], 0)
        u_mem = arena("u_mem", [P, NT, D], 0)
        obg = arena("obg", [P, NT, 1024], 16)
        gain_mem = arena("gain_mem", [P, D], 16)
        gain_x = arena("gain_x", [P, D], 40)
        qkva = arena("qkva", [P, NT, 1536], 24)
        gla = arena("gla", [P, NT, 2048], 36)
        SH = 52
        mem_sb = arena("mem_sb", [P, NT, D], 24)
        u_x = arena("u_x", [P, NT, D], 24)
        ckv1 = arena("ckv1", [P, 2, NT, 512], SH + 32)
        memT = (arena("memT_hi", [P, DC, SEQ], SH, F32R), arena("memT_lo", [P, DC, SEQ], SH + 16, F32R))
        bias = arena("bias", [P, A_HEADS, SEQ], SH)
        aqT = arena("aqT", [64, A_HEADS, SEQ], SH + 16)
        akT = arena("akT", [64, A_KV, SEQ], SH + 32)
        s1 = arena("s1", [P, 2, 2, 258], SH + 36)
        p1 = arena("p1", [P, 2, 2, 258], SH + 40.25)
        pT1 = arena("pT1", [P, 2, 4, P], SH + 44.5)
        la = arena("la", [P, NT, 512], SH)
        eb = arena("eb", [P, NT, 512], SH + 4)
        enb = arena("enb", [P, NT, 512], SH + 8)
        kst = arena("kst", [P, NT, 512], SH + 12)
        gqT = arena("gqT", [P, G_HEADS, SEQ], SH + 16)
        gkT = arena("gkT", [P, G_HEADS, SEQ], SH + 20)
        attT = arena("attT", [P, NT, G_HEADS, P], SH + 24)
        state = arena("state", [P, 3, G_HEADS, G_VAL], SH + 28)
        glowT = arena("glowT", [32, 1, SEQ], SH + 40)
        decay = arena("decay", [P, 16], SH + 41)
        yT = (arena("yT_hi", [P, DC, SEQ], SH, F32R), arena("yT_lo", [P, DC, SEQ], SH + 16, F32R))
        SH2 = SH + 49
        gup = arena("gup", [17, 512], SH2)
        glow = arena("glow", [P, NT, G_RANK], SH2 + 2)
        glag = arena("glag", [P, G_VAL], SH2 + 2.125)
        sinks_b = arena("sinks_b", [P, A_HEADS], SH2 + 3.125)
        relb = arena("relb", [33, A_HEADS], SH2 + 3.1875)
        brow = arena("brow", [A_HEADS, C_BIASW], SH2 + 3.25)
        hT = (arena("hT_hi", [P, 24, SEQ], 0, F32R), arena("hT_lo", [P, 24, SEQ], 24, F32R))
        hb = arena("hb", [P, 2, NT, 512], 48)
        sil = arena("sil", [P, NT, 512], 56)
        u = arena("u", [P, NT, D], 64)
        gain = arena("gain", [P, D], 96)
        idx = arena("idx", [P, NT, 1104], 0)
        iqT = arena("iqT", [64, I_HEADS, SEQ], 9)
        ikT = arena("ikT", [64, 1, SEQ], 25)
        mqT = arena("mqT", [P, M_HEADS, SEQ], 0)
        mrT = arena("mrT", [64, M_HEADS, SEQ], 8)
        mkT = arena("mkT", [P, M_HEADS, SEQ], 16)
        krT = arena("krT", [64, 1, SEQ], 26)
        sqT = arena("sqT", [P, S_HEADS, SEQ], 0)
        skT = arena("skT", [P, S_HEADS, SEQ], 8)
        mq = arena("mq", [P, NT, 1536], 27)
        mout = arena("mout", [P, NT, 1024], 27)
        mkv = arena("mkv", [P, NT, 2048], 39)
        s2 = arena("s2", [P, 2, 2, 258], 55)
        p2 = arena("p2", [P, 2, 2, 258], 59.25)
        pT2 = arena("pT2", [P, 2, 4, P], 63.5)
        rel = arena("rel", [P, 2, 2, SEQ], 55)
        work = arena("work", [P, 2, SEQ], 101)
        dsa = arena("dsa", [P, NT, 3072], 68)
        c_sb = arena("c_sb", [P, NT, 832], 68)
        cT = (arena("cT_hi", [P, 6, SEQ], 75, F32R), arena("cT_lo", [P, 6, SEQ], 81, F32R))
        gcq = arena("gcq", [P, 768], 101)
        SM = 104
        score = arena("score", [P, NT, SEQ], SM)
        sel = arena("sel", [P, NT, SEQ], SM)
        selw = arena("selw", [P, NT, SEQ], 92)
        trig = arena("trig", [P, 2, NT, 32], 94)
        rtmp = arena("rtmp", [P, 4, 256], 96)
        pos_i = arena("pos_i", [P, NT], 106, I32)
        ang = arena("ang", [P, 4, NT, 32], 100)
        ckv = arena("ckv", [P, 2, NT, 512], 0)
        ckT = arena("ckT", [P, C_HEADS, SEQ], 8)
        cqo = arena("cqo", [P, NT, 512], 12)
        cqT = arena("cqT", [P, C_HEADS, SEQ], 16)
        coT = (arena("coT_hi", [P, 4, SEQ], 20, F32R), arena("coT_lo", [P, 4, SEQ], 24, F32R))

        acc = [[ctx.enter_context(nc.psum_tensor(f"acc{p}{t}", [P, 512], F32)) for t in range(NT)] for p in range(2)]
        bank = [ctx.enter_context(nc.psum_tensor(f"unit{i}", [P, 512], F32)) for i in range(2)]
        psS = ctx.enter_context(nc.psum_tensor("psS", [P, 2, 256], F32))
        psO = ctx.enter_context(nc.psum_tensor("psO", [P, 2, 256], F32))

        keep_kv = nc.dram_tensor("keep_kv", [2, SEQ, 512], F32, kind="Internal")
        keep_bias = nc.dram_tensor("keep_bias", [A_HEADS, P, C_BIASW], F32, kind="Internal")

        w_landed = [sem(f"w_landed{i}") for i in range(RING)]
        hi_split = sem("hi_split")
        lo_split = sem("lo_split")
        tile_done = sem("tile_done")
        acc0_done = sem("acc0_done")
        acc_free = [[sem(f"acc{p}{t}_free") for t in range(NT)] for p in range(2)]
        unit_done = sem("unit_done")
        unit_hi = sem("unit_hi")
        unit_free = [sem(f"unit{i}_free") for i in range(2)]
        sc_done = sem("scores_done")
        sc_read = sem("scores_read")
        max_done = sem("max_done")
        exp_done = sem("exp_done")
        out_acc = sem("attention_out_acc")
        out_done = sem("attention_out_done")
        const_in = sem("const_in")
        mem_in = sem("mem_in")
        x_in = [sem("x_in"), sem("x_again_in")]
        gain_in = [sem(f"gain_in{i}") for i in range(8)]
        small_in = sem("small_in")
        gcq_in = sem("gcq_in")
        ckv_kept, ckv_back = sem("ckv_kept"), sem("ckv_back")
        bias_kept, bias_in = sem("bias_kept"), sem("bias_in")
        squares = sem("squares")
        u_ready = sem("u_ready")
        z_log, la_ready = sem("z_log"), sem("la_ready")
        obg_tanh = sem("obg_tanh")
        sig_ready = sem("sig_ready")
        exp_sum, gq_ready, gk_ready = sem("exp_sum"), sem("gq_ready"), sem("gk_ready")
        head_squares, ob_normed, ob_ready = sem("head_squares"), sem("ob_normed"), sem("ob_ready")
        merged_ready = sem("merged_ready")
        h2_ready = sem("h2_ready")
        angles_ready, trig_ready = sem("angles_ready"), sem("trig_ready")
        roped = {k: sem(f"roped_{k}") for k in ("idx", "kr", "mq", "dsa")}
        c_squares, c_normed = sem("c_squares"), sem("c_normed")
        rel_used = sem("rel_used")
        mean_ready, rstd_ready = sem("mean_ready"), sem("rstd_ready")
        out_stored, ttr_done = sem("out_stored"), sem("ttr_done")
        dve_step, act_step, pool_step = sem("dve_step"), sem("act_step"), sem("pool_step")

        def acc_ready(eng, b, t, last_tile):
            if t == 0:
                eng.wait_ge(acc0_done, b + 1)
            else:
                eng.wait_ge(tile_done, last_tile + 1)

        def block_read(eng, b, t):
            eng.wait_ge(acc_free[b % 2][t], b // 2 + 1)

        def units_read(eng, n):
            for i in range(2):
                if n >= i:
                    eng.wait_ge(unit_free[i], (n - i) // 2 + 1)

        BLOCK = {}
        for s, at in SCHEDULE:
            if s[0] == "evac":
                BLOCK[s[1]["evac"], s[1]["arg"]] = at["block"]

        BUF = dict(qkva=qkva, gla=gla, glow=glow, idx=idx, c=c_sb, mq=mq, mkv=mkv, dsa=dsa, cqo=cqo)
        SRC = dict(u_mem=u_mem, qkva=qkva, gla=gla, glow=glow, merged=sigA, idx=idx, c=c_sb, mout=mout, dsa=dsa, cqo=cqo)
        LHS = dict(memT=memT, xT=xT, yT=yT, cT=cT, coT=coT)
        DST = dict(aqT=aqT, akT=akT, glowT=glowT, gqT=gqT, gkT=gkT, iqT=iqT, ikT=ikT, krT=krT, mqT=mqT, mrT=mrT,
                   mkT=mkT, sqT=sqT, skT=skT, ckT=ckT, cqT=cqT)
        def piece(name, i, t, nth):
            src, col, width, _, _, _, _ = TRANSPOSES[name]
            if src == "u":
                return (u_x if nth < 16 else u)[:, t, col + i * width:col + (i + 1) * width]
            if src == "mq":
                return mq[:, t, (4 * col + i) * 192:(4 * col + i) * 192 + 128]
            if src == "mr":
                return mq[:, t, (4 * col + i) * 192 + 128:(4 * col + i + 1) * 192]
            if src == "mkv":
                return mkv[:, t, (4 * col + i) * 256:(4 * col + i) * 256 + 128]
            if src == "ckv":
                return ckv[:, 0, t, i * 128:(i + 1) * 128]
            return SRC[src][:, t, col + i * width:col + (i + 1) * width]

        def heads_view(which, t):
            if which == "idx":
                return idx[:, t, 0:1088].rearrange("p (h d) -> p h d", d=I_DIM), I_ROT // 2
            if which == "kr":
                return c_sb[:, t, 768:832].rearrange("p (h d) -> p h d", d=M_ROPE), M_ROPE // 2
            if which == "mq":
                return mq[:, t, :].rearrange("p (h d) -> p h d", d=M_NOPE + M_ROPE)[:, :, M_NOPE:], M_ROPE // 2
            return dsa[:, t, 0:2048].rearrange("p (h d) -> p h d", d=S_DIM), S_ROT // 2

        def attention(kind):
            if kind == "A":
                return s1, p1, pT1, A_DIM ** -0.5, A_DIM
            scale = {"M": (M_NOPE + M_ROPE) ** -0.5, "S": S_DIM ** -0.5, "C": C_DIM ** -0.5}[kind]
            return s2, p2, pT2, scale, 128

        def values(kind, kt, h):
            if kind == "A":
                return qkva[:, kt, 1280 + (h // 4) * 64:1280 + (h // 4 + 1) * 64]
            if kind == "M":
                return mkv[:, kt, h * 256 + 128:(h + 1) * 256]
            if kind == "S":
                return dsa[:, kt, 2048 + h * 128:2048 + (h + 1) * 128]
            return ckv[:, 1, kt, h * 128:(h + 1) * 128]

        def outputs(kind, t, h, dv):
            to = {"A": qkva, "M": mout, "S": dsa, "C": cqo}[kind]
            return to[:, t, h * dv:(h + 2) * dv].rearrange("p (i v) -> p i v", i=2)

        ident = cst[:, C_IDENT:C_IDENT + P]
        block = ctx.enter_context(nc.Block())

        @block.sync
        def _(sp):
            tok = lambda a: a.rearrange("(t p) d -> p t d", p=P)
            sp.dma_start(mem_sb[:], tok(t_in["mem_2"][0])).then_inc(mem_in, 16)
            sp.dma_start(cst[:], t_in["const"]).then_inc(const_in, 16)

            def tile(slot, free, src, kc, n):
                if free is not None:
                    sp.wait_ge(lo_split, free)
                sp.dma_start(w_raw[:, slot, 0:kc, 0:n], src.rearrange("(c p) n -> p c n", p=P)).then_inc(
                    w_landed[slot], 16)

            for s, at in SCHEDULE:
                i = at["tile"]
                if s[0] == "tile":
                    b, k = s[1], s[2]
                    kc = min(CK, b["kc"] - k * CK)
                    r = (b["k0"] + k * CK) * P
                    tile(i % RING, i - RING + 1 if i >= RING else None,
                         t_in[b["w"]][r:r + kc * P, b["c0"]:b["c0"] + b["n"]], kc, b["n"])
                    if i == RING - 1:
                        sp.dma_start(x_sb[:], tok(t_in["x"][0])).then_inc(x_in[0], 16)
                elif s[0] == "swiglu_up":
                    with sp.Fori(0, s[2]) as r:
                        for j, w in enumerate(("w_ffn_gate", "w_ffn_up")):
                            for k in range(8):
                                tile(k % RING, i + 8 * j + k - RING + 1 + r * 16,
                                     t_in[w][2 * k * P:(2 * k + 2) * P, bass.ds(r * 512 + s[1] * 512, 512)], 2, 512)
                elif s[0] == "relu2_up":
                    with sp.Fori(0, s[2] // 2) as r:
                        for j in range(2):
                            for k in range(8):
                                tile(k % RING, i + 8 * j + k - RING + 1 + r * 16,
                                     t_in["w_up_2"][2 * k * P:(2 * k + 2) * P,
                                                    bass.ds(r * 1024 + (s[1] + j) * 512, 512)], 2, 512)
                elif s[0] == "down":
                    n = s[3] // CK
                    with sp.Fori(0, 2) as r:
                        for j in range(2):
                            for k in range(n):
                                o = i + n * j + k
                                row = (s[2] + 2 * k) * P
                                tile(o % RING, o - RING + 1 + r * (2 * n),
                                     t_in[s[1]][row:row + 2 * P, bass.ds(r * 1024 + j * 512, 512)], 2, 512)
                elif s[0] == "norm" and s[2] == "out":
                    for t in range(NT):
                        sp.wait_ge(u_ready, 8 * s[1] + 4 * t + 4)
                        sp.dma_start(out[0, t * P:(t + 1) * P, :], u[:, t, :]).then_inc(out_stored, 16)
            sp.wait_ge(out_stored, 16 * NT)

        @block.gpsimd
        def _(pool):
            steps = [0]

            def after(ins):
                steps[0] += 1
                ins.then_inc(pool_step, 1)
                pool.wait_ge(pool_step, steps[0])

            def rows(dst, vec, sm):
                pool.dma_start(dst, vec.unsqueeze(0).broadcast_to([P, vec.shape[0]])).then_inc(sm, 16)

            rows(gain_mem[:], t_in["g_mem_2"][0], gain_in[0])
            rows(gain_x[:], t_in["norm_mix_g"][0], gain_in[1])
            after(pool.memset(relb[32:33, :], 1.0))
            pool.dma_start(relb[0:32, :], t_in["rel_bias"]).then_inc(small_in, 16)
            pool.dma_start(gup[0:G_RANK, :], t_in["w_gate_up"]).then_inc(small_in, 16)
            pool.dma_start(gup[G_RANK:G_RANK + 1, :], t_in["b_gate"]).then_inc(small_in, 16)
            rows(glag[:], t_in["gla_norm_g"][0], small_in)
            rows(sinks_b[:], t_in["sinks"][0], small_in)
            for t in range(NT):
                pool.dma_start(pos_i[:, t:t + 1], t_in["positions_2"][0, t * P:(t + 1) * P].unsqueeze(1)).then_inc(small_in, 16)

            roots = [0]

            after(pool.memset(stat[:, 100:108], -0.5))

            def rstd(c0, n):
                roots[0] += 1
                pool.wait_ge(mean_ready, roots[0])
                v = stat[:, c0:c0 + n]
                pool.tensor_tensor(v, v, stat[:, 100:100 + n], ALU.pow).then_inc(rstd_ready, 1)

            def rotate(which, t):
                v, half = heads_view(which, t)
                n = v.shape[1]
                x1, x2 = v[:, :, 0:half], v[:, :, half:2 * half]
                cos, sin = (trig[:, i, t, 0:32:32 // half].unsqueeze(1).broadcast_to([P, n, half]) for i in range(2))
                tmp = [rtmp[:, i, 0:n * half].rearrange("p (h f) -> p h f", f=half) for i in range(4)]
                for dst, a, b in zip(tmp, (x1, x2, x2, x1), (cos, sin, cos, sin)):
                    last = pool.tensor_tensor(dst, a, b, ALU.mult)
                after(last)
                pool.tensor_tensor(x1, tmp[0], tmp[1], ALU.subtract)
                last = pool.tensor_tensor(x2, tmp[2], tmp[3], ALU.add)
                last.then_inc(roped[which], 1)
                pool.wait_ge(roped[which], t + 1)

            for s, at in SCHEDULE:
                if s[0] == "norm" and s[1] >= 2:
                    n = s[1]
                    if n == 2:
                        pool.wait_ge(merged_ready, 8)
                    else:
                        pool.wait_ge(u_ready, 8 * n)
                    if n == 5:
                        pool.wait_ge(c_normed, 4)
                        pool.wait_ge(out_done, GROUP0["S"] + NGROUPS["S"])
                        pool.dma_start(ckv[:], keep_kv.ap().rearrange("a (t p) d -> p a t d", p=P)).then_inc(ckv_back, 16)
                    name = ["", "", "norm_ffn_g", "norm_final_g", "g_mix_2", "g_cross_2", "g_mlp_2", "g_final_2"][n]
                    vec = t_in[name]
                    rows(gain[:], vec if len(vec.shape) == 1 else vec[0], gain_in[n])
                    rstd(4 * n, 2)
                elif s[0] == "norm":
                    rstd(4 * s[1], 2)
                elif s[0] == "c_norm":
                    rstd(66, 4)
                elif s[0] == "keep_ckv":
                    for i in range(2):
                        for t in range(NT):
                            block_read(pool, BLOCK["ckv", i], t)
                    pool.dma_start(keep_kv.ap().rearrange("a (t p) d -> p a t d", p=P), ckv1[:]).then_inc(ckv_kept, 16)
                elif s[0] == "bias_row":
                    units_read(pool, at["unit"])
                    pool.dma_start(keep_bias[:, :, :], brow[:].unsqueeze(1).broadcast_to([A_HEADS, P, C_BIASW])).then_inc(
                        bias_kept, 16)
                    pool.wait_ge(bias_kept, 16)
                    pool.dma_start(bias[:], bass.AP(tensor=keep_bias, offset=P - 1,
                                                    ap=[[C_BIASW - 1, P], [P * C_BIASW, A_HEADS], [1, SEQ]])).then_inc(bias_in, 16)
                elif s[0] == "gate_z":
                    t = s[1]
                    pool.wait_ge(z_log, t + 1)
                    pool.tensor_tensor(la[:, t, :], enb[:, t, :], eb[:, t, :], ALU.subtract).then_inc(la_ready, 1)
                elif s[0] == "gate_sum":
                    t = s[1]
                    pool.wait_ge(exp_sum, t + 1)
                    pool.tensor_tensor(gla[:, t, 0:512], gla[:, t, 0:512], eb[:, t, :], ALU.mult).then_inc(gq_ready, 1)
                elif s[0] == "gate_rest":
                    t = s[1]
                    units_read(pool, at["unit"])
                    after(pool.tensor_tensor(kst[:, t, :], kst[:, t, :], gla[:, t, 512:1024], ALU.mult))
                    pool.tensor_tensor(gla[:, t, 512:1024], gla[:, t, 512:1024], enb[:, t, :], ALU.mult).then_inc(
                        gk_ready, 1)
                elif s[0] == "evac" and s[1]["evac"] in ("sigA", "sigB"):
                    buf, col = (sigA if s[1]["evac"] == "sigA" else sigB), s[1]["arg"]
                    for t in range(NT):
                        block_read(pool, at["block"], t)
                        v = buf[:, t, col:col + 512]
                        pool.tensor_scalar(v, v, 0.5, 0.5, ALU.mult, ALU.add).then_inc(sig_ready, 1)
                elif s[0] == "gla_norm":
                    rstd(50, 8)
                    for t in range(NT):
                        pool.wait_ge(ob_normed, t + 1)
                        v = gla[:, t, 0:1024]
                        pool.tensor_tensor(v, v, obg[:, t, :], ALU.mult).then_inc(ob_ready, 1)
                elif s[0] == "evac" and s[1]["evac"] == "merge":
                    j = s[1]["arg"] // 512
                    for t in range(NT):
                        block_read(pool, at["block"], t)
                        c = slice(512 * j, 512 * j + 512)
                        pool.tensor_tensor(sigA[:, t, c], sigA[:, t, c], sigB[:, t, c], ALU.add).then_inc(
                            merged_ready, 1)
                elif s[0] == "load_x":
                    pool.wait_ge(merged_ready, 8)
                    pool.dma_start(x_sb[:], t_in["x"][0].rearrange("(t p) d -> p t d", p=P)).then_inc(x_in[1], 16)
                elif s[0] == "angles":
                    pool.wait_ge(u_ready, 8 * 5)
                    rows(gcq[:, 0:512], t_in["g_cq_2"][0], gcq_in)
                    rows(gcq[:, 512:768], t_in["g_ckv_2"][0], gcq_in)
                    pool.wait_ge(trig_ready, 2)
                elif s[0] == "rope":
                    which = s[1]
                    blocks = {"idx": [("idx", 0), ("idx", 512), ("idx", 1024)], "kr": [("c", 512)],
                              "mq": [("mq", 384 * j) for j in range(4)],
                              "dsa": [("dsa", 512 * j) for j in range(4)]}[which]
                    for t in range(NT):
                        for b in blocks:
                            block_read(pool, BLOCK[b], t)
                        if which == "mq":
                            pass
                        rotate(which, t)

        @block.scalar
        def _(act):
            def split_hi(i, slot, uses, free):
                act.wait_ge(w_landed[slot], uses)
                if free is not None:
                    act.wait_ge(tile_done, free)
                act.activation(w_hi[:, slot], w_raw[:, slot], ACT.Copy).then_inc(hi_split, 1)

            def lead(i, more=0):
                if isinstance(more, int) and i + more >= TILES:
                    return
                static = isinstance(more, int) and more == 0
                split_hi(i, i % RING, 16 * (i // RING + 1) + (0 if static else more * (16 // RING)),
                         (i - RING + 1 if i >= RING else None) if static else i - RING + 1 + more)

            def inputs(n, kind, t):
                if kind == "mem":
                    act.wait_ge(mem_in, 16)
                elif n == 1:
                    act.wait_ge(x_in[0], 16)
                    act.wait_ge(u_ready, 8)
                elif n == 4:
                    act.wait_ge(u_ready, 8 * 4)

            def hi(bk, w, n, dst, i0, t):
                act.activation(dst[0][0:w, i0:i0 + n, t * P:(t + 1) * P],
                               bank[bk][0:w, 0:n * P].rearrange("p (c q) -> p c q", q=P), ACT.Copy).then_inc(unit_hi, 1)

            for s, at in SCHEDULE:
                U, B = at["unit"], at["block"]
                if s[0] == "prime":
                    for i in range(LEAD):
                        lead(i)
                elif s[0] == "tile":
                    lead(at["tile"] + LEAD)
                elif s[0] == "norm":
                    n, kind = s[1], s[2]
                    inputs(n, kind, 0)
                    if n not in (0, 1, 4):
                        for t in range(NT):
                            block_read(act, B - 2, t)
                            block_read(act, B - 1, t)
                    src = mem_sb if kind == "mem" else x_sb
                    junk = u_mem if kind == "mem" else u_x if n == 1 else u
                    act.activation(junk[:, 0, :], src[:, 0, :], ACT.Square, accum_out=stat[:, 4 * n:4 * n + 1]).then_inc(
                        squares, 1)
                elif s[0] == "T":
                    name, t = s[1], s[2]
                    _, _, w, n, dst, i0, mode = TRANSPOSES[name]
                    if mode == "split":
                        act.wait_ge(unit_done, U + 1)
                        hi(U % 2, w, n, LHS[dst], i0, t)
                    elif mode == "act":
                        if name == "ak" and t == 0:
                            act.wait_ge(ckv_kept, 16)
                        act.wait_ge(unit_done, U + 1)
                        scale = G_KEY ** -0.5 if name == "gq" else 1.0
                        act.activation(DST[dst][0:w, i0:i0 + n, t * P:(t + 1) * P],
                                       bank[U % 2][0:w, 0:n * P].rearrange("p (c q) -> p c q", q=P),
                                       ACT.Copy, scale=scale).then_inc(unit_free[U % 2], 1)
                elif s[0] == "evac":
                    b, what, arg, n = B, s[1]["evac"], s[1]["arg"], s[1]["n"]
                    last = at["tile"] - 1
                    ac = acc[b % 2]
                    if what == "ckv":
                        acc_ready(act, b, 0, last)
                        act.activation(ckv1[:, arg, 0, :], ac[0][:], ACT.Copy).then_inc(acc_free[b % 2][0], 1)
                    elif what in BUF:
                        if what == "gla" and arg == 0:
                            act.wait_ge(u_ready, 16)
                        acc_ready(act, b, 0, last)
                        act.activation(BUF[what][:, 0, arg:arg + n], ac[0][:, 0:n], ACT.Copy).then_inc(
                            acc_free[b % 2][0], 1)
                    elif what == "obg":
                        for t in range(NT):
                            acc_ready(act, b, t, last)
                            act.activation(obg[:, t, arg:arg + 512], ac[t][:], ACT.Tanh, scale=0.5).then_inc(obg_tanh, 1)
                    elif what in ("sigA", "sigB"):
                        buf = sigA if what == "sigA" else sigB
                        for t in range(NT):
                            acc_ready(act, b, t, last)
                            act.activation(buf[:, t, arg:arg + 512], ac[t][:], ACT.Tanh, scale=0.5).then_inc(
                                acc_free[b % 2][t], 1)
                elif s[0] == "scores":
                    g = s[1]
                    kind, t, h, nk = GROUPS[g]
                    _, pb, _, _, _ = attention(kind)
                    sb_ = attention(kind)[0]
                    act.wait_ge(max_done, g + 1)
                    w = nk + 1 if kind == "A" else nk
                    for i in range(2):
                        ins = act.activation(pb[:, g % 2, i, 0:w], sb_[:, g % 2, i, 0:w], ACT.Exp,
                                             bias=stat[:, 40 + 2 * (g % 2) + i:41 + 2 * (g % 2) + i],
                                             accum_out=stat[:, 44 + 2 * (g % 2) + i:45 + 2 * (g % 2) + i])
                    ins.then_inc(exp_done, 1)
                elif s[0] == "probs_T":
                    g = s[1]
                    kind, t, h, nk = GROUPS[g]
                    n = 2 * nk // P
                    act.wait_ge(unit_done, U + 1)
                    act.activation(attention(kind)[2][:, g % 2, 0:n, :],
                                   bank[U % 2][:, 0:n * P].rearrange("p (c q) -> p c q", q=P), ACT.Copy).then_inc(
                        unit_free[U % 2], 1)
                elif s[0] == "gate_z":
                    t = s[1]
                    units_read(act, U)
                    act.activation(eb[:, t, :], eb[:, t, :], ACT.Exp).then_inc(act_step, 1)
                    act.wait_ge(act_step, t + 1)
                    act.activation(eb[:, t, :], eb[:, t, :], ACT.Ln, bias=1.0).then_inc(z_log, 1)
                elif s[0] == "gate_sum":
                    t = s[1]
                    act.wait_ge(unit_done, U + 1)
                    act.activation(eb[:, t, :], bank[U % 2][:], ACT.Exp).then_inc(exp_sum, 1)
                    act.activation(enb[:, t, :], bank[U % 2][:], ACT.Exp, scale=-1.0).then_inc(unit_free[U % 2], 1)
                elif s[0] == "gate_rest":
                    t = s[1]
                    act.wait_ge(unit_done, U + 1)
                    ins = act.activation(kst[:, t, :], bank[U % 2][:], ACT.Exp)
                    ins.then_inc(unit_free[U % 2], 1)
                elif s[0] == "gate_decay":
                    act.wait_ge(unit_done, U + 1)
                    act.activation(decay[:], bank[U % 2][:, 0:16], ACT.Exp).then_inc(unit_free[U % 2], 1)
                elif s[0] == "gla_out" and s[2] == 0:
                    act.wait_ge(unit_done, U + 1)
                    act.activation(gla[:, s[1], 0:512], bank[U % 2][:], ACT.Copy).then_inc(unit_free[U % 2], 1)
                elif s[0] == "gla_norm":
                    units_read(act, U - 1)
                    for t in range(NT):
                        for h in range(G_HEADS):
                            junk = (eb, enb)[t][:, h // 2, 256 * (h % 2):256 * (h % 2) + 256]
                            act.activation(junk, gla[:, t, 256 * h:256 * h + 256], ACT.Square,
                                           accum_out=stat[:, 50 + 4 * t + h:51 + 4 * t + h]).then_inc(head_squares, 1)
                elif s[0] == "angles":
                    act.wait_ge(angles_ready, 1)
                    for i in range(2):
                        act.activation(trig[:, i], ang[:, 2 + i], ACT.Sin).then_inc(trig_ready, 1)
                elif s[0] == "idx":
                    t, n = s[1], at["nth"]
                    nk = SEQ if t else P
                    if n >= 2:
                        act.wait_ge(rel_used, n - 1)
                    act.wait_ge(unit_done, U + 1)
                    act.activation(rel[:, n % 2, :, 0:nk], bank[U % 2][:].rearrange("p (i k) -> p i k", i=2)[:, :, 0:nk],
                                   ACT.Relu, scale=1.0 / 32).then_inc(unit_free[U % 2], 1)
                elif s[0] == "c_norm":
                    for i, (c0, n) in enumerate(((0, 512), (512, 256))):
                        for t in range(NT):
                            block_read(act, BLOCK["c", c0], t)
                            act.activation(mkv[:, t, c0:c0 + n], c_sb[:, t, c0:c0 + n], ACT.Square,
                                           accum_out=stat[:, 66 + 2 * i + t:67 + 2 * i + t]).then_inc(c_squares, 1)
                elif s[0] in ("swiglu_up", "relu2_up"):
                    T0, glu = at["tile"], s[0] == "swiglu_up"

                    def body(r, prev):
                        m = r * 16
                        for k in range(8):
                            lead(T0 + k + LEAD, m)
                        for t in range(NT):
                            if t == 0:
                                act.wait_ge(acc0_done, B + 1 + r * 2)
                            else:
                                act.wait_ge(tile_done, T0 + 8 + m)
                            if glu:
                                if prev:
                                    act.wait_ge(acc_free[1][t], B // 2 + r)
                                act.activation(sil[:, t, :], acc[0][t][:], ACT.Silu).then_inc(acc_free[0][t], 1)
                            else:
                                act.activation(hb[:, 0, t, :], acc[0][t][:], ACT.Relu).then_inc(acc_free[0][t], 1)
                        if prev:
                            for t in range(NT):
                                act.wait_ge(unit_done, (U - 2 + t + 1) + r * (2 if glu else 4))
                                c = (r - 1) * 4 if glu else (r - 1) * 8 + 4
                                act.activation(hT[0][:, bass.ds(c, 4), t * P:(t + 1) * P],
                                               bank[t][:].rearrange("p (c q) -> p c q", q=P), ACT.Copy).then_inc(unit_hi, 1)
                        for k in range(8):
                            lead(T0 + 8 + k + LEAD, m)
                        if not glu:
                            for t in range(NT):
                                if t == 0:
                                    act.wait_ge(acc0_done, B + 2 + r * 2)
                                else:
                                    act.wait_ge(tile_done, T0 + 16 + m)
                                act.activation(hb[:, 1, t, :], acc[1][t][:], ACT.Relu).then_inc(acc_free[1][t], 1)
                            for t in range(NT):
                                act.wait_ge(unit_done, U + t + 1 + r * 4)
                                act.activation(hT[0][:, bass.ds(r * 8, 4), t * P:(t + 1) * P],
                                               bank[t][:].rearrange("p (c q) -> p c q", q=P), ACT.Copy).then_inc(unit_hi, 1)

                    n = s[2] if glu else s[2] // 2
                    body(0, False)
                    with act.Fori(1, n) as r:
                        body(r, True)
                    for t in range(NT):
                        act.wait_ge(unit_done, U + 2 * s[2] - 1 + t)
                        act.activation(hT[0][:, 4 * s[2] - 4:4 * s[2], t * P:(t + 1) * P],
                                       bank[t][:].rearrange("p (c q) -> p c q", q=P), ACT.Copy).then_inc(unit_hi, 1)
                elif s[0] == "down":
                    n, T0 = s[3] // CK, at["tile"]
                    if T0 + 4 * n == TILES:
                        for k in range(4 * n):
                            lead(T0 + k + LEAD)
                    else:
                        with act.Fori(0, 2) as r:
                            for k in range(2 * n):
                                lead(T0 + k + LEAD, r * (2 * n))

        @block.tensor
        def _(pe):
            def products(ac, b_lhs, l0, kc, slot, n, t, start, stop):
                hi_, lo_ = b_lhs
                for c in range(kc):
                    for m, (a, w) in enumerate(((hi_, w_hi), (lo_, w_hi), (hi_, w_lo))):
                        ins = pe.matmul(ac[t][:, 0:n], a[:, l0 + c, t * P:(t + 1) * P], w[:, slot, c, 0:n],
                                        start=start and c == 0 and m == 0, stop=stop and c == kc - 1 and m == 2)
                return ins

            def dense_tile(i, p, free, lhs, l0, kc, n, first, last, more=0):
                pe.wait_ge(lo_split, i + 1 + more)
                for t in range(NT):
                    if first and free is not None:
                        pe.wait_ge(acc_free[p][t], free)
                    ins = products(acc[p], lhs, l0, kc, i % RING, n, t, first, last)
                    if t == 0 and last:
                        ins.then_inc(acc0_done, 1)
                ins.then_inc(tile_done, 1)

            def bank_free(n):
                if n >= 2:
                    pe.wait_ge(unit_free[n % 2], n // 2)

            def transpose_pieces(bk, pieces, w):
                for i, a in enumerate(pieces):
                    ins = pe.transpose(bank[bk][0:w, i * P:(i + 1) * P], a, ident)
                ins.then_inc(unit_done, 1)

            def source_ready(name, t, nth):
                src, col, w, _, _, _, _ = TRANSPOSES[name]
                if name.startswith("mem"):
                    pe.wait_ge(u_ready, 4 * t + int(name[3:]) + 1)
                elif src == "u":
                    n = {1: 1, 2: 2, 3: 4, 4: 5, 5: 6}[nth // 8]
                    pe.wait_ge(u_ready, 8 * n + 4 * t + int(name[1:]) + 1)
                elif name[:2] in ("aq", "ak"):
                    block_read(pe, BLOCK["qkva", col // 512 * 512], t)
                elif name == "glow":
                    block_read(pe, BLOCK["glow", 0], t)
                elif name in ("gq", "gk"):
                    pe.wait_ge(gq_ready if name == "gq" else gk_ready, t + 1)
                elif name[:2] == "ya":
                    pe.wait_ge(out_done, GROUP0["A"] + NGROUPS["A"])
                elif name[:2] == "yb":
                    pe.wait_ge(ob_ready, t + 1)
                elif src == "merged":
                    pe.wait_ge(merged_ready, 2 * (col // 512) + t + 1)
                elif src == "idx":
                    pe.wait_ge(roped["idx"], t + 1)
                elif name in ("cq", "ckv"):
                    pe.wait_ge(c_normed, t + 1 if name == "cq" else t + 3)
                elif name == "kr":
                    pe.wait_ge(roped["kr"], t + 1)
                elif src == "mq":
                    for j in range(4):
                        block_read(pe, BLOCK["mq", 384 * j], t)
                    pe.wait_ge(roped["mq"], t + 1)
                elif src == "mr":
                    pe.wait_ge(roped["mq"], t + 1)
                elif src == "mkv":
                    for j in range(4):
                        block_read(pe, BLOCK["mkv", 512 * j], t)
                elif src == "mout":
                    pe.wait_ge(out_done, GROUP0["M"] + NGROUPS["M"])
                elif name[:2] in ("sq", "sk"):
                    pe.wait_ge(roped["dsa"], t + 1)
                elif name in ("s0", "s1"):
                    pe.wait_ge(out_done, GROUP0["S"] + NGROUPS["S"])
                elif name == "ck":
                    pe.wait_ge(ckv_back, 16)
                elif name == "cqq":
                    block_read(pe, BLOCK["cqo", 0], t)
                elif name == "co":
                    pe.wait_ge(out_done, GROUP0["C"] + NGROUPS["C"])

            def score_terms(kind, h, t):
                q = slice(t * P, (t + 1) * P)
                if kind == "A":
                    return [(aqT[:, h, q], akT[:, h // 4])]
                if kind == "M":
                    return [(mqT[:, h, q], mkT[:, h]), (mrT[:, h, q], krT[:, 0])]
                if kind == "S":
                    return [(sqT[:, h, q], skT[:, h])]
                return [(cqT[:, h, q], ckT[:, h])]

            LAST_T = {"A": "ak", "M": "mr1", "S": "sk1", "C": "cqq"}
            n_u = 0
            pe.wait_ge(const_in, 16)
            for s, at in SCHEDULE:
                U, B = at["unit"], at["block"]
                if s[0] in UNIT_STEPS:
                    bank_free(U)
                    ps = bank[U % 2]
                if s[0] == "tile":
                    b, k = s[1], s[2]
                    if at["need"] is not None:
                        units_read(pe, at["need"])
                    dense_tile(at["tile"], B % 2, B // 2 if B >= 2 else None, LHS[b["lhs"]], b["l0"] + CK * k,
                               min(CK, b["kc"] - CK * k), b["n"], k == 0, at["last"])
                elif s[0] == "T":
                    name, t = s[1], s[2]
                    _, _, w, n, _, _, _ = TRANSPOSES[name]
                    source_ready(name, t, n_u)
                    transpose_pieces(U % 2, [piece(name, i, t, n_u) for i in range(n)], w)
                    n_u += TRANSPOSES[name][0] in ("u", "u_mem")
                elif s[0] == "scores":
                    g = s[1]
                    kind, t, h, nk = GROUPS[g]
                    if g == GROUP0[kind]:
                        units_read(pe, LAST_UNIT[LAST_T[kind]])
                        if kind in "MSC":
                            units_read(pe, U - 1)
                    if g:
                        pe.wait_ge(sc_read, g)
                    for i in range(2):
                        terms = score_terms(kind, h + i, t)
                        for m, (q, k) in enumerate(terms):
                            ins = pe.matmul(psS[:, i, 0:nk], q, k[:, 0:nk], start=m == 0, stop=m == len(terms) - 1)
                    ins.then_inc(sc_done, 1)
                elif s[0] == "probs_T":
                    g = s[1]
                    kind, t, h, nk = GROUPS[g]
                    pb = attention(kind)[1]
                    pe.wait_ge(exp_done, g + 1)
                    transpose_pieces(U % 2, [pb[:, g % 2, i, c * P:(c + 1) * P] for i in range(2) for c in range(nk // P)], P)
                elif s[0] == "output":
                    g = s[1]
                    kind, t, h, nk = GROUPS[g]
                    _, _, pT, _, dv = attention(kind)
                    units_read(pe, U - 1)
                    if g:
                        pe.wait_ge(out_done, g)
                    if kind == "M" and g == GROUP0["M"]:
                        for j in range(4):
                            for tt in range(NT):
                                block_read(pe, BLOCK["mkv", 512 * j], tt)
                    if kind == "S" and g == GROUP0["S"]:
                        for j in range(6):
                            for tt in range(NT):
                                block_read(pe, BLOCK["dsa", 512 * j], tt)
                    for i in range(2):
                        for kt in range(nk // P):
                            ins = pe.matmul(psO[:, i, 0:dv], pT[:, g % 2, i * (nk // P) + kt, :], values(kind, kt, h + i),
                                            start=kt == 0, stop=kt == nk // P - 1)
                    ins.then_inc(out_acc, 1)
                elif s[0] == "bias_row":
                    pe.wait_ge(small_in, 16 * 7)
                    pe.matmul(ps[0:A_HEADS, 0:C_BIASW], relb[0:33, :], cst[0:33, C_HOT:C_HOT + C_BIASW],
                              start=True, stop=True).then_inc(unit_done, 1)
                elif s[0] == "gate_z":
                    t = s[1]
                    units_read(pe, LAST_UNIT["glow"])
                    pe.matmul(ps[:], glowT[0:17, 0, t * P:(t + 1) * P], gup[0:17, :], start=True, stop=True).then_inc(
                        unit_done, 1)
                elif s[0] in ("gate_sum", "gate_rest"):
                    t = s[1]
                    c0 = C_TRI if s[0] == "gate_sum" else C_REST
                    pe.wait_ge(la_ready, t + 1)
                    pe.matmul(ps[:], cst[:, c0:c0 + P], la[:, t, :], start=True, stop=True).then_inc(unit_done, 1)
                elif s[0] == "gate_decay":
                    for t in range(NT):
                        for h in range(G_HEADS):
                            c0 = 4 * h + 2 * t
                            ins = pe.matmul(ps[:, c0:c0 + 2], la[:, t, h * P:(h + 1) * P], cst[:, C_IND:C_IND + 2],
                                            start=True, stop=True)
                    ins.then_inc(unit_done, 1)
                elif s[0] == "state":
                    n, h = s[1], s[2]
                    t, r = n // 2, CHUNK * (n % 2)
                    pe.wait_ge(gk_ready, t + 1)
                    for i in range(2):
                        v0 = 1024 + (h + i) * G_VAL
                        ins = pe.matmul(ps[:, i * G_VAL:(i + 1) * G_VAL], kst[r:r + CHUNK, t, (h + i) * P:(h + i + 1) * P],
                                        gla[r:r + CHUNK, t, v0:v0 + G_VAL], start=True, stop=True)
                    ins.then_inc(unit_done, 1)
                elif s[0] == "gla_att":
                    t = s[1]
                    units_read(pe, LAST_UNIT["gk"])
                    q = slice(t * P, (t + 1) * P)
                    for h in range(G_HEADS):
                        ins = pe.matmul(ps[:, h * P:(h + 1) * P], gkT[:, h, q], gqT[:, h, q], start=True, stop=True)
                    ins.then_inc(unit_done, 1)
                elif s[0] == "gla_out":
                    t, h = s[1], s[2]
                    if s[1:] == (0, 0):
                        units_read(pe, U - 1)
                    for i in range(2):
                        o = slice(i * G_VAL, (i + 1) * G_VAL)
                        v0 = 1024 + (h + i) * G_VAL
                        ins = pe.matmul(ps[:, o], attT[:, t, h + i, :], gla[:, t, v0:v0 + G_VAL], start=True, stop=False,
                                        skip_group_check=True)
                        for j in range(2):
                            n = 2 * t + j
                            if n:
                                r = slice(CHUNK * j, CHUNK * (j + 1))
                                ins = pe.matmul(ps[r, o], gqT[:, h + i, t * P + CHUNK * j:t * P + CHUNK * (j + 1)],
                                                state[:, n - 1, h + i, :], start=False, stop=j == 1, skip_group_check=True)
                    ins.then_inc(unit_done, 1)
                elif s[0] == "idx":
                    t, h = s[1], s[2]
                    nk = SEQ if t else P
                    if at["nth"] == 0:
                        units_read(pe, LAST_UNIT["ik"])
                    for i in range(2):
                        ins = pe.matmul(ps[:, i * SEQ:i * SEQ + nk], iqT[:, h + i, t * P:(t + 1) * P], ikT[:, 0, 0:nk],
                                        start=True, stop=True)
                    ins.then_inc(unit_done, 1)
                elif s[0] in ("swiglu_up", "relu2_up"):
                    T0, glu, n = at["tile"], s[0] == "swiglu_up", s[2]

                    def pieces(j, t):
                        return [hb[:, j, t, c * P:(c + 1) * P] for c in range(4)]

                    def body(r, prev):
                        for j in range(2):
                            for k in range(8):
                                dense_tile(T0 + 8 * j + k, j, B // 2 + r, xT, CK * k, CK, 512, k == 0, k == 7, r * 16)
                            if j == 0 and prev:
                                for t in range(NT):
                                    pe.wait_ge(unit_free[t], U // 2 + (r - 1 if glu else 2 * r - 1))
                                    if glu:
                                        pe.wait_ge(acc_free[1][t], B // 2 + r)
                                    else:
                                        pe.wait_ge(h2_ready, at["h"] - 2 + t + 1 + r * 4)
                                    transpose_pieces(t, pieces(0 if glu else 1, t), P)
                            if j == 1 and not glu:
                                for t in range(NT):
                                    pe.wait_ge(unit_free[t], U // 2 + 2 * r)
                                    pe.wait_ge(h2_ready, at["h"] + t + 1 + r * 4)
                                    transpose_pieces(t, pieces(0, t), P)

                    units_read(pe, at["u3"])
                    body(0, False)
                    m = n if glu else n // 2
                    with pe.Fori(1, m) as r:
                        body(r, True)
                    for t in range(NT):
                        pe.wait_ge(unit_free[t], U // 2 + n - 1)
                        if glu:
                            pe.wait_ge(acc_free[1][t], B // 2 + n)
                        else:
                            pe.wait_ge(h2_ready, at["h"] + 2 * n - 1 + t)
                        transpose_pieces(t, pieces(0 if glu else 1, t), P)
                elif s[0] == "down":
                    n, T0 = s[3] // CK, at["tile"]

                    def body(r):
                        for j in range(2):
                            for k in range(n):
                                if j == 0 and k in (0, n - 2):
                                    for t in range(NT):
                                        pe.wait_ge(unit_free[t], U // 2 - (k == 0))
                                dense_tile(T0 + n * j + k, j, B // 2 + r, hT, CK * k, CK, 512, k == 0, k == n - 1,
                                           r * (2 * n))

                    with pe.Fori(0, 2) as r:
                        body(r)

        @block.vector
        def _(dve):
            steps = [0]

            def after(ins):
                steps[0] += 1
                ins.then_inc(dve_step, 1)
                dve.wait_ge(dve_step, steps[0])

            def lead(i, more=0):
                if isinstance(more, int) and i + more >= TILES:
                    return
                dve.wait_ge(hi_split, i + 1 + more)
                slot = i % RING
                dve.tensor_tensor(w_lo[:, slot], w_raw[:, slot], w_hi[:, slot].bitcast(F32), ALU.subtract).then_inc(
                    lo_split, 1)

            def lo(bk, w, n, dst, i0, t):
                dve.tensor_tensor(dst[1][0:w, i0:i0 + n, t * P:(t + 1) * P],
                                  bank[bk][0:w, 0:n * P].rearrange("p (c q) -> p c q", q=P),
                                  dst[0][0:w, i0:i0 + n, t * P:(t + 1) * P].bitcast(F32), ALU.subtract).then_inc(
                    unit_free[bk], 1)

            def hidden_lo(bk, c, t):
                dve.tensor_tensor(hT[1][:, bass.ds(c, 4), t * P:(t + 1) * P],
                                  bank[bk][:].rearrange("p (c q) -> p c q", q=P),
                                  hT[0][:, bass.ds(c, 4), t * P:(t + 1) * P].bitcast(F32), ALU.subtract).then_inc(
                    unit_free[bk], 1)

            roots = [0]

            def rstd(c0, n, *widths, by=1.0):
                for i, width in enumerate(widths):
                    v = stat[:, c0 + i * n:c0 + (i + 1) * n]
                    ins = dve.tensor_scalar(v, v, by / width, by * EPS, ALU.mult, ALU.add)
                ins.then_inc(mean_ready, 1)
                roots[0] += 1
                dve.wait_ge(rstd_ready, roots[0])

            dve.wait_ge(const_in, 16)
            for s, at in SCHEDULE:
                U, B = at["unit"], at["block"]
                if s[0] == "prime":
                    for i in range(LEAD):
                        lead(i)
                elif s[0] == "tile":
                    lead(at["tile"] + LEAD)
                elif s[0] == "norm":
                    n, kind = s[1], s[2]
                    if kind == "mem":
                        dve.wait_ge(mem_in, 16)
                    elif n == 1:
                        dve.wait_ge(x_in[0], 16)
                    elif n == 4:
                        dve.wait_ge(u_ready, 8 * 4)
                    else:
                        for t in range(NT):
                            block_read(dve, B - 2, t)
                            block_read(dve, B - 1, t)
                    src = mem_sb if kind == "mem" else x_sb
                    dst = {"mem": u_mem, "final1": x_sb}.get(kind, u_x if n == 1 else u)
                    junk = u if kind == "final1" else dst
                    if n == 1:
                        dve.wait_ge(u_ready, 8)
                    dve.tensor_tensor_reduce(junk[:, 1, :], src[:, 1, :], src[:, 1, :], 1.0, 0.0, ALU.mult, ALU.add,
                                             stat[:, 4 * n + 1:4 * n + 2]).then_inc(ttr_done, 1)
                    dve.wait_ge(ttr_done, n + 1)
                    dve.wait_ge(squares, n + 1)
                    rstd(4 * n, 2, D)
                    dve.wait_ge(gain_in[n], 16)
                    gb = {0: gain_mem, 1: gain_x}.get(n, gain)
                    for t in range(NT):
                        for j in range(4):
                            c = slice(512 * j, 512 * j + 512)
                            dve.scalar_tensor_tensor(out=dst[:, t, c], in0=src[:, t, c], scalar=stat[:, 4 * n + t:4 * n + t + 1],
                                                     in1=gb[:, c], op0=ALU.mult, op1=ALU.mult).then_inc(u_ready, 1)
                elif s[0] == "T":
                    name, t = s[1], s[2]
                    _, _, w, n, dst, i0, mode = TRANSPOSES[name]
                    if mode == "split":
                        dve.wait_ge(unit_hi, at["split"] + 1)
                        lo(U % 2, w, n, LHS[dst], i0, t)
                    elif mode == "dve":
                        if name == "glow" and t == 0:
                            after(dve.memset(glowT[0:32], 1.0))
                        dve.wait_ge(unit_done, U + 1)
                        dve.tensor_copy(DST[dst][0:w, i0:i0 + n, t * P:(t + 1) * P],
                                        bank[U % 2][0:w, 0:n * P].rearrange("p (c q) -> p c q", q=P)).then_inc(
                            unit_free[U % 2], 1)
                elif s[0] == "evac":
                    b, what, arg, n = B, s[1]["evac"], s[1]["arg"], s[1]["n"]
                    last = at["tile"] - 1
                    ac = acc[b % 2]
                    if what == "ckv":
                        acc_ready(dve, b, 1, last)
                        dve.tensor_copy(ckv1[:, arg, 1, :], ac[1][:]).then_inc(acc_free[b % 2][1], 1)
                    elif what in BUF:
                        acc_ready(dve, b, 1, last)
                        dve.tensor_copy(BUF[what][:, 1, arg:arg + n], ac[1][:, 0:n]).then_inc(acc_free[b % 2][1], 1)
                    elif what == "obg":
                        for t in range(NT):
                            dve.wait_ge(obg_tanh, 2 * (arg // 512) + t + 1)
                            v = obg[:, t, arg:arg + 512]
                            dve.scalar_tensor_tensor(out=v, in0=v, scalar=1.0, in1=ac[t][:], op0=ALU.add,
                                                     op1=ALU.mult).then_inc(acc_free[b % 2][t], 1)
                    elif what == "merge":
                        c = slice(arg, arg + 512)
                        if arg == 0:
                            dve.wait_ge(sig_ready, 16)
                        for t in range(NT):
                            acc_ready(dve, b, t, last)
                            dve.tensor_tensor(sigA[:, t, c], sigA[:, t, c], acc[(b - 1) % 2][t][:], ALU.mult).then_inc(
                                acc_free[(b - 1) % 2][t], 1)
                            dve.tensor_tensor(sigB[:, t, c], sigB[:, t, c], ac[t][:], ALU.mult).then_inc(
                                acc_free[b % 2][t], 1)
                    elif what == "add":
                        if arg == 0 and s[1]["w"] == "w_out":
                            dve.wait_ge(x_in[1], 16)
                        for t in range(NT):
                            acc_ready(dve, b, t, last)
                            v = x_sb[:, t, arg:arg + 512]
                            dve.tensor_tensor(v, v, ac[t][:], ALU.add).then_inc(acc_free[b % 2][t], 1)
                elif s[0] == "scores":
                    g = s[1]
                    kind, t, h, nk = GROUPS[g]
                    sb_, _, _, scale, _ = attention(kind)
                    if g == GROUP0["A"]:
                        dve.wait_ge(bias_in, 16)
                        dve.wait_ge(ckv_kept, 16)
                    if g >= 2:
                        dve.wait_ge(exp_done, g - 1)
                    dve.wait_ge(sc_done, g + 1)
                    dst, src = sb_[:, g % 2, :, 0:nk], psS[:, :, 0:nk]
                    if kind == "C":
                        ins = dve.tensor_scalar(dst, src, scale, None, ALU.mult)
                    else:
                        if kind == "A":
                            mask = bias[:, h:h + 2, SEQ - nk:SEQ]
                        elif kind == "M":
                            mask = cst[:, C_CMASK + P - nk:C_CMASK + P].unsqueeze(1).broadcast_to([P, 2, nk])
                        else:
                            mask = sel[:, t, 0:nk].unsqueeze(1).broadcast_to([P, 2, nk])
                        ins = dve.scalar_tensor_tensor(out=dst, in0=src, scalar=scale, in1=mask, op0=ALU.mult, op1=ALU.add)
                    ins.then_inc(sc_read, 1)
                    w = nk
                    if kind == "A":
                        after(dve.tensor_copy(sb_[:, g % 2, :, nk:nk + 1], sinks_b[:, h:h + 2].unsqueeze(2)))
                        w = nk + 1
                    dve.wait_ge(sc_read, g + 1)
                    dve.tensor_reduce(stat[:, 40 + 2 * (g % 2):42 + 2 * (g % 2)], sb_[:, g % 2, :, 0:w], X, ALU.max,
                                      negate=True).then_inc(max_done, 1)
                elif s[0] == "output":
                    g = s[1]
                    kind, t, h, nk = GROUPS[g]
                    dv = attention(kind)[4]
                    dve.wait_ge(exp_done, g + 1)
                    if g:
                        dve.wait_ge(out_done, g)
                    after(dve.reciprocal(stat[:, 48:50], stat[:, 44 + 2 * (g % 2):46 + 2 * (g % 2)]))
                    dve.wait_ge(out_acc, g + 1)
                    dve.tensor_tensor(outputs(kind, t, h, dv), psO[:, :, 0:dv],
                                      stat[:, 48:50].unsqueeze(2).broadcast_to([P, 2, dv]), ALU.mult).then_inc(out_done, 1)
                elif s[0] == "bias_row":
                    dve.wait_ge(unit_done, U + 1)
                    dve.tensor_copy(brow[:], bank[U % 2][0:A_HEADS, 0:C_BIASW]).then_inc(unit_free[U % 2], 1)
                elif s[0] == "gate_z":
                    t = s[1]
                    dve.wait_ge(unit_done, U + 1)
                    after(dve.tensor_scalar(enb[:, t, :], bank[U % 2][:], 0.0, None, ALU.min))
                    dve.scalar_tensor_tensor(out=eb[:, t, :], in0=enb[:, t, :], scalar=2.0, in1=bank[U % 2][:],
                                             op0=ALU.mult, op1=ALU.subtract).then_inc(unit_free[U % 2], 1)
                elif s[0] == "state":
                    n, h = s[1], s[2]
                    dve.wait_ge(unit_done, U + 1)
                    if n:
                        units_read(dve, U - 1)
                    for i in range(2):
                        dS = bank[U % 2][:, i * G_VAL:(i + 1) * G_VAL]
                        c = 4 * (h + i) + n
                        if n == 0:
                            ins = dve.tensor_copy(state[:, n, h + i, :], dS)
                        else:
                            ins = dve.scalar_tensor_tensor(out=state[:, n, h + i, :], in0=state[:, n - 1, h + i, :],
                                                           scalar=decay[:, c:c + 1], in1=dS, op0=ALU.mult, op1=ALU.add)
                    ins.then_inc(unit_free[U % 2], 1)
                elif s[0] == "gla_att":
                    t = s[1]
                    dve.wait_ge(unit_done, U + 1)
                    dve.scalar_tensor_tensor(out=attT[:, t], in0=bank[U % 2][:].rearrange("p (h c) -> p h c", h=G_HEADS),
                                             scalar=3e38,
                                             in1=cst[:, C_CAUSAL:C_CAUSAL + P].unsqueeze(1).broadcast_to([P, G_HEADS, P]),
                                             op0=ALU.min, op1=ALU.mult).then_inc(unit_free[U % 2], 1)
                elif s[0] == "gla_out" and s[2] == 2:
                    dve.wait_ge(unit_done, U + 1)
                    dve.tensor_copy(gla[:, s[1], 512:1024], bank[U % 2][:]).then_inc(unit_free[U % 2], 1)
                elif s[0] == "gla_norm":
                    dve.wait_ge(head_squares, 8)
                    rstd(50, 8, G_VAL, by=4.0)
                    for t in range(NT):
                        for h in range(G_HEADS):
                            v = gla[:, t, G_VAL * h:G_VAL * (h + 1)]
                            c = 50 + 4 * t + h
                            ins = dve.scalar_tensor_tensor(out=v, in0=v, scalar=stat[:, c:c + 1], in1=glag[:],
                                                           op0=ALU.mult, op1=ALU.mult)
                        ins.then_inc(ob_normed, 1)
                elif s[0] == "angles":
                    after(dve.tensor_copy(stat[:, 88:90], pos_i[:]))
                    for t in range(NT):
                        ins = dve.tensor_scalar(ang[:, 0, t, :], cst[:, C_FREQ:C_FREQ + 32], stat[:, 88 + t:89 + t], None,
                                                ALU.mult)
                    after(ins)
                    after(dve.tensor_scalar(ang[:, 1], ang[:, 0], 1.0 / TWO_PI, 0.25, ALU.mult, ALU.add))
                    after(dve.tensor_scalar(ang[:, 2], ang[:, 1], ROUND, -ROUND, ALU.add, ALU.add))
                    after(dve.tensor_scalar(ang[:, 1], ang[:, 0], 1.0 / TWO_PI, None, ALU.mult))
                    after(dve.tensor_scalar(ang[:, 3], ang[:, 1], ROUND, -ROUND, ALU.add, ALU.add))
                    for i, shift in ((2, TWO_PI / 4), (3, 0.0)):
                        src = ang[:, 0]
                        for part in TWO_PI_PARTS:
                            after(dve.scalar_tensor_tensor(out=ang[:, 1], in0=ang[:, i], scalar=-part, in1=src,
                                                           op0=ALU.mult, op1=ALU.add))
                            src = ang[:, 1]
                        after(dve.tensor_scalar(ang[:, i], ang[:, 1], shift, PI_BELOW, ALU.add, ALU.min))
                    dve.tensor_scalar(ang[:, 2:4], ang[:, 2:4], -PI_BELOW, None, ALU.max).then_inc(angles_ready, 1)
                elif s[0] == "idx":
                    t, h, q = s[1], s[2], at["nth"]
                    nk = SEQ if t else P
                    units_read(dve, U)
                    for i in range(2):
                        w = idx[:, t, 1088 + h + i:1089 + h + i]
                        sc = score[:, t, 0:nk]
                        if h + i == 0:
                            ins = dve.tensor_scalar(sc, rel[:, q % 2, i, 0:nk], w, None, ALU.mult)
                        else:
                            ins = dve.scalar_tensor_tensor(out=sc, in0=rel[:, q % 2, i, 0:nk], scalar=w, in1=sc,
                                                           op0=ALU.mult, op1=ALU.add)
                        if i == 0:
                            after(ins)
                    ins.then_inc(rel_used, 1)
                    dve.wait_ge(rel_used, q + 1)
                elif s[0] == "topk":
                    t, r = s[1], s[2]
                    nk = SEQ if t else P
                    sc, wk = score[:, t, 0:nk], work[:, t, 0:nk]
                    if r == 0:
                        dve.wait_ge(c_normed, 4)
                        after(dve.tensor_tensor(sc, sc, cst[:, C_CMASK + P - nk:C_CMASK + P], ALU.add))
                    src = sc if r == 0 else wk
                    after(dve.max(stat[:, 80:88], src))
                    after(dve.match_replace(out=wk, in_to_replace=stat[:, 80:88], in_values=src, imm_value=-3e38))
                    if r == TOPK // 8 - 1:
                        after(dve.tensor_scalar(sel[:, t, 0:nk], wk, -2e38, NEG, ALU.is_gt, ALU.mult))
                elif s[0] == "c_norm":
                    dve.wait_ge(c_squares, 4)
                    rstd(66, 2, 512, 256)
                    dve.wait_ge(gcq_in, 32)
                    for i, (c0, n) in enumerate(((0, 512), (512, 256))):
                        for t in range(NT):
                            v = c_sb[:, t, c0:c0 + n]
                            dve.scalar_tensor_tensor(out=v, in0=v, scalar=stat[:, 66 + 2 * i + t:67 + 2 * i + t],
                                                     in1=gcq[:, c0:c0 + n], op0=ALU.mult, op1=ALU.mult).then_inc(c_normed, 1)
                elif s[0] in ("swiglu_up", "relu2_up"):
                    T0, glu, n, S0 = at["tile"], s[0] == "swiglu_up", s[2], at["split"]

                    def body(r, prev):
                        for k in range(8):
                            lead(T0 + k + LEAD, r * 16)
                        if not glu:
                            for t in range(NT):
                                dve.wait_ge(acc_free[0][t], B // 2 + 1 + r)
                                dve.tensor_tensor(hb[:, 0, t, :], hb[:, 0, t, :], hb[:, 0, t, :], ALU.mult).then_inc(h2_ready, 1)
                        if prev:
                            for t in range(NT):
                                dve.wait_ge(unit_hi, S0 - 2 + t + 1 + r * (2 if glu else 4))
                                hidden_lo(t, (r - 1) * 4 if glu else (r - 1) * 8 + 4, t)
                        for k in range(8):
                            lead(T0 + 8 + k + LEAD, r * 16)
                        for t in range(NT):
                            if glu:
                                if t == 0:
                                    dve.wait_ge(acc0_done, B + 2 + r * 2)
                                else:
                                    dve.wait_ge(tile_done, T0 + 16 + r * 16)
                                dve.wait_ge(acc_free[0][t], B // 2 + 1 + r)
                                dve.tensor_tensor(hb[:, 0, t, :], sil[:, t, :], acc[1][t][:], ALU.mult).then_inc(
                                    acc_free[1][t], 1)
                            else:
                                dve.wait_ge(acc_free[1][t], B // 2 + 1 + r)
                                dve.tensor_tensor(hb[:, 1, t, :], hb[:, 1, t, :], hb[:, 1, t, :], ALU.mult).then_inc(h2_ready, 1)
                        if not glu:
                            for t in range(NT):
                                dve.wait_ge(unit_hi, S0 + t + 1 + r * 4)
                                hidden_lo(t, r * 8, t)

                    body(0, False)
                    with dve.Fori(1, n if glu else n // 2) as r:
                        body(r, True)
                    for t in range(NT):
                        dve.wait_ge(unit_hi, S0 + 2 * n - 1 + t)
                        hidden_lo(t, 4 * n - 4, t)
                elif s[0] == "down":
                    n, T0 = s[3] // CK, at["tile"]

                    def body(r):
                        for j in range(2):
                            for k in range(n):
                                lead(T0 + n * j + k + LEAD, r * (2 * n))
                            for t in range(NT):
                                if t == 0:
                                    dve.wait_ge(acc0_done, B + j + 1 + r * 2)
                                else:
                                    dve.wait_ge(tile_done, T0 + n * (j + 1) + r * (2 * n))
                                v = x_sb[:, t, bass.ds(r * 1024 + 512 * j, 512)]
                                dve.tensor_tensor(v, v, acc[j][t][:], ALU.add).then_inc(acc_free[j][t], 1)

                    if T0 + 4 * n == TILES:
                        body(0)
                        body(1)
                    else:
                        with dve.Fori(0, 2) as r:
                            body(r)


def kernel(**inputs):
    import numpy as _np
    import concourse.bacc as _bacc
    from concourse import mybir as _mybir
    from concourse.bass_utils import run_bass_kernel_spmd as _run

    nc = _bacc.Bacc("TRN2", target_bir_lowering=False, num_devices=1)
    arrays, t_in = {}, {}
    for name, a in [*inputs.items(), ("const", constants())]:
        a = _np.ascontiguousarray(a)
        arrays[f"in_{name}"] = a
        t_in[name] = nc.dram_tensor(f"in_{name}", a.shape, _mybir.dt.from_np(a.dtype), kind="ExternalInput").ap()
        if name.startswith("w_"):
            t_in[name] = t_in[name][0]
    out = nc.dram_tensor("out_0", (1, SEQ, D), _mybir.dt.float32, kind="ExternalOutput").ap()
    build(nc, t_in, out)
    r = _run(nc, [arrays], core_ids=[0])
    return r.results[0]["out_0"]
```

```python
from contextlib import ExitStack

import numpy as np

import concourse.bass as bass
from concourse import mybir

F32 = mybir.dt.float32
F32R = mybir.dt.float32r
I32 = mybir.dt.int32
ALU = mybir.AluOpType
ACT = mybir.ActivationFunctionType
X = mybir.AxisListType.X

P = 128
SEQ, D = 256, 2048
NT = SEQ // P
DC = D // P
EPS = 1e-6
NEG = -1e30
RING = 4
LEAD = RING - 1
CK = 2
COLS = 512

A_HEADS, A_KV, A_DIM = 16, 4, 64
G_HEADS, G_KEY, G_VAL, G_RANK, CHUNK = 4, 128, 256, 16, 64
M_HEADS, M_NOPE, M_ROPE, M_VAL = 8, 128, 64, 128
S_HEADS, S_DIM, S_ROT = 8, 128, 32
I_HEADS, I_DIM, I_ROT = 16, 64, 16
TOPK = 64
TWO_PI = 2 * np.pi
TWO_PI_PARTS = (6.28125, float(np.float16(TWO_PI - 6.28125)), float(TWO_PI - 6.28125 - float(np.float16(TWO_PI - 6.28125))))
PI_BELOW = float(np.nextafter(np.float32(np.pi), np.float32(0)))
ROUND = 1.5 * 2.0 ** 23
C_HEADS, C_DIM = 4, 128
D_FF1, D_FF2 = 5632, 8192

IN1_GLOW = 3 * COLS + 4 * COLS
IN1_OBG = IN1_GLOW + G_RANK
IN1_GA = IN1_OBG + G_HEADS * G_VAL
IN1_GB = IN1_GA + D
IN2_CQ, IN2_CKV, IN2_QD = 0, 512, 832
IN2_QI = IN2_QD + 3 * S_HEADS * S_DIM
IN2_KI = IN2_QI + I_HEADS * I_DIM
IN2_END = IN2_KI + I_DIM + I_HEADS

C_IDENT, C_TRI, C_REST, C_CAUSAL, C_ZERO, C_CMASK, C_IND, C_FREQ, C_HOT = 0, 128, 256, 384, 512, 640, 768, 770, 802
C_BIASW = 384
C_END = C_HOT + C_BIASW


def constants():
    c = np.zeros((P, C_END), np.float32)
    s, t = np.arange(P)[:, None], np.arange(P)[None, :]
    same = s // CHUNK == t // CHUNK
    c[:, C_IDENT:C_IDENT + P] = s == t
    c[:, C_TRI:C_TRI + P] = (same & (s <= t)) / 16.0
    c[:, C_REST:C_REST + P] = (same & (s > t)) / 16.0
    c[:, C_CAUSAL:C_CAUSAL + P] = same & (s <= t)
    c[:, C_CMASK:C_CMASK + P] = np.where(t // CHUNK <= s // CHUNK, 0.0, NEG)
    c[:, C_IND:C_IND + 2] = (s // CHUNK == np.arange(2)[None]) / 16.0
    half = M_ROPE // 2
    c[:, C_FREQ:C_FREQ + half] = (500000.0 ** (-np.arange(half) / half)).astype(np.float32)
    dist = 255 - np.arange(C_BIASW)
    d = np.maximum(dist, 0)
    large = 16 + (np.log(np.maximum(d, 1).astype(np.float32) / 16) / np.float32(np.log(8.0)) * 16).astype(np.int32)
    bucket = np.where(d < 16, d, np.minimum(large, 31))
    seen = (dist >= 0) & (dist < 128)
    for m in range(C_BIASW):
        if seen[m]:
            c[bucket[m], C_HOT + m] = 1.0
        else:
            c[32, C_HOT + m] = NEG
    return c


TRANSPOSES = {
}


def xp(name, src, col, width, n, dst, idx, mode):
    TRANSPOSES[name] = (src, col, width, n, dst, idx, mode)


for j in range(4):
    xp(f"mem{j}", "u_mem", 512 * j, 128, 4, "memT", 4 * j, "split")
    xp(f"u{j}", "u", 512 * j, 128, 4, "xT", 4 * j, "split")
    xp(f"aq{j}", "qkva", 256 * j, 64, 4, "aqT", 4 * j, "act" if j % 2 else "dve")
    xp(f"merged{j}", "merged", 512 * j, 128, 4, "xT", 4 * j, "split")
xp("ak", "qkva", 1024, 64, 4, "akT", 0, "act")
for j in range(2):
    xp(f"ya{j}", "qkva", 512 * j, 128, 4, "yT", 4 * j, "split")
    xp(f"yb{j}", "gla", 512 * j, 128, 4, "yT", 8 + 4 * j, "split")
xp("glow", "glow", 0, 16, 1, "glowT", 0, "dve")
xp("gq", "gla", 0, 128, 4, "gqT", 0, "act")
xp("gk", "gla", 512, 128, 4, "gkT", 0, "act")
for j in range(4):
    xp(f"iq{j}", "idx", 256 * j, 64, 4, "iqT", 4 * j, "act" if j % 2 else "dve")
xp("ik", "idx", 1024, 64, 1, "ikT", 0, "act")
xp("cq", "c", 0, 128, 4, "cT", 0, "split")
xp("ckv", "c", 512, 128, 2, "cT", 4, "split")
xp("kr", "c", 768, 64, 1, "krT", 0, "act")
for j in range(2):
    xp(f"mq{j}", "mq", j, 128, 4, "mqT", 4 * j, "act")
    xp(f"mr{j}", "mr", j, 64, 4, "mrT", 4 * j, "dve")
    xp(f"mk{j}", "mkv", j, 128, 4, "mkT", 4 * j, "act")
    xp(f"a{j}", "mout", 512 * j, 128, 4, "xT", 4 * j, "split")
    xp(f"sq{j}", "dsa", 512 * j, 128, 4, "sqT", 4 * j, "act")
    xp(f"sk{j}", "dsa", 1024 + 512 * j, 128, 4, "skT", 4 * j, "dve")
    xp(f"s{j}", "dsa", 512 * j, 128, 4, "xT", 8 + 4 * j, "split")
xp("ck", "ckv", 0, 128, 4, "ckT", 0, "act")
xp("cqq", "cqo", 0, 128, 4, "cqT", 0, "dve")
for name, src, i0 in (("hid0", "hb0", 0), ("glu6", "hb0", 20), ("glu5", "hb0", 16), ("relu6", "hb1", 20),
                      ("relu4", "hb1", 12)):
    xp(name, src, 0, 128, 4, "hT", i0, "split")
xp("co", "cqo", 0, 128, 4, "coT", 0, "split")


def attention_groups():
    groups = []
    for kind, heads in (("A", A_HEADS), ("M", M_HEADS), ("S", S_HEADS), ("C", C_HEADS)):
        for t in range(NT):
            for h in range(0, heads, 2):
                groups.append((kind, t, h, SEQ if t or kind == "C" else P))
    return groups


GROUPS = attention_groups()
GROUP0 = {k: [g[0] for g in GROUPS].index(k) for k in "AMSC"}
NGROUPS = {k: sum(g[0] == k for g in GROUPS) for k in "AMSC"}


def attention_slots(kind):
    a, n = GROUP0[kind], NGROUPS[kind]
    slots = []
    for j in range(n + 2):
        slot = []
        if 0 <= j - 1 < n:
            slot.append(("probs_T", a + j - 1))
        if 0 <= j - 2 < n:
            slot.append(("output", a + j - 2))
        if j < n:
            slot.append(("scores", a + j))
        slots.append(slot)
    return slots


def make_block(w, k0, kc, c0, n, lhs, l0, evac, arg=0, needs=()):
    return dict(w=w, k0=k0, kc=kc, c0=c0, n=n, lhs=lhs, l0=l0, evac=evac, arg=arg, needs=needs)


def tiles_in(b):
    return -(-b["kc"] // CK)


def block_steps(*args, **kw):
    b = make_block(*args, **kw)
    return [("tile", b, k) for k in range(tiles_in(b))] + [("evac", b, (0, 1))]


def both(name):
    return [("T", name, t) for t in range(NT)]


def weave(dense, slots, every):
    out, slots, n = [], list(slots), 0
    for s in dense:
        out.append(s)
        if s[0] == "tile":
            n += 1
            if n % every == 0 and slots:
                out += slots.pop(0)
    for s in slots:
        out += s
    return out


def pieces_of_norm(n, j, ts=(0, 1)):
    return [s for t in ts for s in (("ssq", n, j, t), ("gained", n, j, t))]


def through_norm(last, n, first, m=None):
    m = n if m is None else m
    k = tiles_in(last)
    a = min(LEAD, k)
    scaled = lambda j, t: ("scaled", m, j, t)
    T = lambda j, t: ("T", f"u{j}", t)
    out = [("tile", last, i) for i in range(k - a)] + [("part", last, i, 0) for i in range(k - a, k)]
    second = [("part", last, i, 1) for i in range(k - a, k)]
    out += [("evac", last, (0,)), ("ssq", n, 3, 0), second[0], ("rstd", n, 0), ("gained", n, 3, 0), scaled(0, 0)]
    out += second[1:-1] + [scaled(1, 0), T(0, 0), scaled(2, 0), second[-1], T(1, 0), scaled(3, 0)]
    out += [("evac", last, (1,)), ("ssq", n, 3, 1), ("rstd", n, 1), ("gained", n, 3, 1)]
    out += [("part", first, i, 0) for i in range(LEAD)] + [scaled(0, 1), scaled(1, 1), T(2, 0), T(3, 0)]
    out += [scaled(2, 1), scaled(3, 1), T(0, 1), T(1, 1)] + [("part", first, i, 1) for i in range(LEAD)]
    out += [T(2, 1), T(3, 1)] + [("tile", first, i) for i in range(LEAD, tiles_in(first))] + [("evac", first, (0, 1))]
    return out


U_NEEDS = ("u0", "u1", "u2", "u3")


def schedule():
    S = []
    mem_k = make_block("w_k_cross_2", 0, DC, 0, 512, "memT", 0, "ckv", 0, ("mem0", "mem1", "mem2", "mem3"))
    for t in range(NT):
        S += [("ssq", 0, j, t) for j in range(4)] + [("rstd", 0, t)] + [("scaled", 0, j, t) for j in range(4)]
        S += [("lead", 0)] * (t == 0) + [("T", "mem0", t), ("T", "mem1", t)] + [("lead", 1)] * (t == 0)
        S += [("T", "mem2", t), ("T", "mem3", t)] + [("lead", 2)] * (t == 0)
        S += [("part", mem_k, i, t) for i in range(LEAD)]
    mem_dense = [("tile", mem_k, i) for i in range(LEAD, DC // CK)] + [("evac", mem_k, (0, 1))]
    mem_dense += block_steps("w_v_cross_2", 0, DC, 0, 512, "memT", 0, "ckv", 1)
    xs = [[], pieces_of_norm(1, 0), pieces_of_norm(1, 1), pieces_of_norm(1, 2),
          pieces_of_norm(1, 3) + [("rstd", 1, 0), ("rstd", 1, 1)]]
    xs += [[("scaled", 1, j, t), ("T", f"u{j}", t)] for j in range(4) for t in range(NT)]
    S += weave(mem_dense, xs, 1)
    S += [("keep_ckv",), ("bias_row",)]
    w = lambda c0, n, evac, arg=0, needs=(): block_steps("w_in", 0, DC, c0, n, "xT", 0, evac, arg, needs)
    S += w(0, 512, "qkva", 0, U_NEEDS) + w(512, 512, "qkva", 512) + w(1024, 512, "qkva", 1024)
    dense = []
    for j in range(4):
        dense += w(1536 + 512 * j, 512, "gla", 512 * j)
    for c0, n, skip in ((0, 384, G_RANK), (384, 320, 0), (704, 320, 0)):
        dense += w(IN1_OBG + c0 - skip, n + skip, "obg", c0)
    for j in range(4):
        dense += w(IN1_GA + 512 * j, 512, "sigA", 512 * j)
    for j in range(4):
        dense += w(IN1_GB + 512 * j, 512, "sigB", 512 * j)
    slots = [both(f"aq{j}") for j in range(4)] + [both("ak")] + attention_slots("A")
    slots += [both("glow"), [("gate_z", 0)], [("gate_z", 1)], [], [("gate_sum", 0)], [("gate_sum", 1)],
              [("gate_rest", 0)], [("gate_rest", 1)], [("gate_decay",)], both("gq"), both("gk")]
    slots += [[("state", n, h)] for n in range(3) for h in (0, 2)]
    slots += [[("gla_att", t)] for t in range(NT)]
    slots += [[("gla_out", t, h)] for t in range(NT) for h in (0, 2)]
    slots += [[("gla_norm",)], [], both("ya0"), both("ya1"), both("yb0"), both("yb1")]
    S += weave(dense, slots, 2)
    for j in range(4):
        S += block_steps("w_proj_a", 0, 8, 512 * j, 512, "yT", 0, "none", 0, ("ya0", "ya1") if not j else ())
        S += weave(block_steps("w_proj_b", 0, 8, 512 * j, 512, "yT", 8, "merge", 512 * j, ("yb0", "yb1") if not j else ()),
                   [[], both(f"merged{j - 1}")] if j else [], 1)
    S += [("load_x",), ("gain", 2)]
    merged = tuple(f"merged{j}" for j in range(4))
    S += weave(block_steps("w_out", 0, DC, 0, 512, "xT", 0, "add", 0, merged), [[], [], both("merged3")], 1)
    S += pieces_of_norm(2, 0)
    for j in (1, 2):
        S += block_steps("w_out", 0, DC, 512 * j, 512, "xT", 0, "add", 512 * j) + pieces_of_norm(2, j)
    gate = lambda j, needs=(): ("w_ffn_gate", 0, DC, 512 * j, 512, "xT", 0, "silu", 0, needs)
    up = lambda j: block_steps("w_ffn_up", 0, DC, 512 * j, 512, "xT", 0, "glu", 0)
    S += through_norm(make_block("w_out", 0, DC, 1536, 512, "xT", 0, "add", 1536), 2, make_block(*gate(0, U_NEEDS)))
    S += [("gain", 3), ("gain", 4)] + up(0) + [("swiglu_up", 0, 6)] + both("glu6") + [("down", "w_ffn_down", 0, 24)]
    S += block_steps(*gate(6)) + up(6) + [("swiglu_up", 6, 5)]
    for j in range(3):
        b = block_steps("w_ffn_down", 24, 20, 512 * j, 512, "hT", 0, "add", 512 * j, HIDDEN_NEEDS("glu5", 5) if not j else ())
        S += (weave(b, [[], both("glu5")], 1) if not j else b) + pieces_of_norm(3, j)
    w = lambda c0, n, evac, arg=0: block_steps("w_in_2", 0, DC, c0, n, "xT", 0, evac, arg)
    S += through_norm(make_block("w_ffn_down", 24, 20, 1536, 512, "hT", 0, "add", 1536), 3,
                      make_block("w_in_2", 0, DC, IN2_CQ, 416, "xT", 0, "c", 0, U_NEEDS), 4)
    S += [("renorm_x",), ("angles",)] + w(IN2_CQ + 416, 416, "c", 416) + [("rope", "kr"), ("c_norm",)]
    dense = []
    for j in range(3):
        dense += w(IN2_QI + 368 * j, 368, "idx", 368 * j)
    S += weave(dense, [[], [], [], both("cq"), both("ckv"), both("kr")], 2)
    S += [("rope", "idx")]
    dense = []
    for j in range(4):
        dense += block_steps("w_qb_2", 0, 4, 384 * j, 384, "cT", 0, "mq", 384 * j, () if j else ("cq",))
    for j in range(4):
        dense += block_steps("w_kvb_2", 0, 2, 512 * j, 512, "cT", 4, "mkv", 512 * j, () if j else ("ckv",))
    dense += [("rope", "mq")]
    for j in range(5):
        dense += w(IN2_QD + 512 * j, 512, "dsa", 512 * j)
        dense += [("rope", "dsa")] * (j == 3)
    slots = [[], [], []] + [both(f"iq{j}") for j in range(4)] + [both("ik")]
    slots += [[("idx", t, h)] for t in range(NT) for h in range(0, I_HEADS, 2)]
    slots += [both(f"mk{j}") for j in range(2)] + [both(f"mq{j}") for j in range(2)] + [both(f"mr{j}") for j in range(2)]
    rounds = [("topk", t, r) for t in range(NT) for r in range(TOPK // 8)]
    slots += [m + rounds[2 * i:2 * i + 2] for i, m in enumerate(attention_slots("M"))]
    S += weave(dense, slots, 1)
    S += weave(w(IN2_QD + 2560, 512, "dsa", 2560), [[], [], [], [], both("a0"), both("a1")], 1)
    dense = []
    for j in range(4):
        dense += block_steps("w_out_2", 0, 8, 512 * j, 512, "xT", 0, "add", 512 * j, () if j else ("a0", "a1"))
    slots = [both("sq0") + both("sk0")] + [both("sq1") + both("sk1")] + attention_slots("S") + [both("s0"), both("s1")]
    S += weave(dense, slots, 1)
    S += [("gain", 5)]
    for j in range(3):
        S += block_steps("w_out_2", 8, 8, 512 * j, 512, "xT", 8, "add", 512 * j, () if j else ("s0", "s1"))
        S += pieces_of_norm(5, j)
    S += through_norm(make_block("w_out_2", 8, 8, 1536, 512, "xT", 8, "add", 1536), 5,
                      make_block("w_q_cross_2", 0, DC, 0, 512, "xT", 0, "cqo", 0, U_NEEDS))
    S += both("ck") + both("cqq") + [("gain", 6)]
    for s in attention_slots("C"):
        S += s[-1:] + s[:-1] if s[-1][0] == "scores" else s
    S += both("co")
    for j in range(3):
        S += block_steps("w_o_cross_2", 0, 4, 512 * j, 512, "coT", 0, "add", 512 * j, () if j else ("co",))
        S += pieces_of_norm(6, j)
    relu = lambda j, needs=(): ("w_up_2", 0, DC, 512 * j, 512, "xT", 0, "relu2", j % 2, needs)
    S += through_norm(make_block("w_o_cross_2", 0, 4, 1536, 512, "coT", 0, "add", 1536), 6, make_block(*relu(0, U_NEEDS)))
    S += [("gain", 7)] + block_steps(*relu(1)) + both("hid0")
    S += [("relu2_up", 0, 6)] + both("relu6") + [("down", "w_down_2", 0, 24)]
    S += block_steps(*relu(6)) + block_steps(*relu(7)) + both("hid0")
    S += [("relu2_up", 6, 6)] + both("relu6") + [("down", "w_down_2", 24, 24)]
    S += block_steps(*relu(12)) + block_steps(*relu(13)) + both("hid0") + [("relu2_up", 12, 4)]
    for j in range(3):
        b = block_steps("w_down_2", 48, 16, 512 * j, 512, "hT", 0, "add", 512 * j, HIDDEN_NEEDS("relu4", 4) if not j else ())
        S += (weave(b, [[], both("relu4")], 1) if not j else b) + pieces_of_norm(7, j)
    last = make_block("w_down_2", 48, 16, 1536, 512, "hT", 0, "add", 1536)
    S += [("tile", last, k) for k in range(8 - LEAD)]
    for t in range(NT):
        S += [("part", last, k, t) for k in range(8 - LEAD, 8)]
        S += [("evac", last, (t,)), ("ssq", 7, 3, t), ("rstd", 7, t), ("gained", 7, 3, t)]
        S += [s for j in range(4) for s in (("scaled", 7, j, t), ("store", 7, j, t))]
    return number(S)


def HIDDEN_NEEDS(name, n):
    return (None,) * (n - 1) + (name,)


UNIT_STEPS = ("T", "probs_T", "bias_row", "gate_z", "gate_sum", "gate_rest", "gate_decay", "state", "gla_att",
              "gla_out", "idx")


def number(steps):
    out, shapes, wrote, seen = [], {}, {}, {}
    c = dict(tile=0, block=0, unit=0, split=0, hidden=0, squares=0, root=0, gained=0, scaled=0)
    ahead = 0
    for s in steps:
        kind = s[0]
        at = dict(c, nth=seen.get(kind, 0))
        seen[kind] = at["nth"] + 1
        if kind in ("tile", "part"):
            b, k = s[1], s[2]
            name = b["needs"][CK * k // 4] if b["needs"] and k % 2 == 0 else None
            ts = (0, 1) if kind == "tile" else (s[3],)
            at["need"] = max(wrote[name, t] for t in ts) if name else None
            at["last"] = k == tiles_in(b) - 1
            if ts == (0,):
                at["tile"] += ahead
                ahead += 1
            else:
                ahead -= kind == "part"
                c["tile"] += 1
            shapes[at["tile"]] = (min(CK, b["kc"] - CK * k), b["n"])
        elif kind == "evac":
            what = s[1]["evac"]
            for t in s[2]:
                wrote[what, s[1]["arg"], t] = c["block"]
            c["block"] += 1 in s[2]
            c["hidden"] += 2 * (what == "relu2")
        elif kind == "ssq":
            at["block"] = wrote.get(("add", 512 * s[2], s[3]))
            c["squares"] += 2 if s[1] == 3 else 0 if s[1] == 0 and s[2] >= 2 else 1
        elif kind == "gained":
            at["block"] = wrote.get(("add", 512 * s[2], s[3]))
            at["u3"] = wrote.get(("u3", 1))
            wrote["gained", s[2], s[3]] = c["gained"]
            c["gained"] += 1
        elif kind in ("rstd", "c_norm", "gla_norm"):
            wrote["root", s[-1]] = c["root"]
            c["root"] += 1
        elif kind == "scaled":
            at["root"] = wrote["root", s[3]]
            at["gained"] = wrote.get(("gained", s[2], s[3]))
            wrote["scaled", s[2], s[3]] = c["scaled"]
            wrote["norm"] = s[1]
            c["scaled"] += 1
        elif kind == "store":
            at["scaled"] = wrote["scaled", s[2], s[3]]
        elif kind in UNIT_STEPS:
            if kind == "probs_T":
                wrote["probs", s[1]] = c["unit"]
            if kind == "T":
                if TRANSPOSES[s[1]][0] in ("u", "u_mem"):
                    at["scaled"] = wrote["scaled", TRANSPOSES[s[1]][1] // 512, s[2]]
                    at["norm"] = wrote["norm"]
                wrote[s[1], s[2]] = c["unit"]
                c["split"] += TRANSPOSES[s[1]][6] == "split"
            c["unit"] += 1
        elif kind in ("swiglu_up", "relu2_up"):
            n = s[2] - 1 if kind == "swiglu_up" else s[2] // 2 - 1
            assert c["unit"] % 2 == 0 and c["block"] % 2 == 0, s
            per = 2 if kind == "swiglu_up" else 4
            c["tile"] += 16 * n
            c["block"] += 2 * n
            c["unit"] += per * n
            c["split"] += per * n
            c["hidden"] += 4 * n if per == 4 else 0
            assert c["tile"] % RING == 0
        elif kind == "down":
            assert c["block"] % 2 == 0
            c["tile"] += 4 * (s[3] // CK)
            c["block"] += 4
        out.append((s, at))
    return out, c["tile"], wrote, shapes


def build(nc, t_in, out):
    SCHEDULE, TILES, LAST_UNIT, SHAPES = schedule()
    ctx = ExitStack()
    with ctx:
        def sem(name):
            return ctx.enter_context(nc.semaphore(name))

        base = (nc.sbuf_base + 63) // 64 * 64
        top = [base]

        def put(name, shape, dt=F32, at=None):
            size = 4 * int(np.prod(shape[1:]))
            off = top[0] if at is None else at
            if at is None:
                top[0] += (size + 63) // 64 * 64
            assert off + size <= nc.sbuf_usable_end, (name, off + size - nc.sbuf_usable_end)
            return nc.alloc_sbuf_tensor_at(name, shape, dt, offset=off)

        w_raw = put("w_raw", [P, RING, CK, COLS])
        w_hi = put("w_hi", [P, RING, CK, COLS], F32R)
        w_lo = put("w_lo", [P, RING, CK, COLS], F32R)
        xT = (put("xT_hi", [P, DC, SEQ], F32R), put("xT_lo", [P, DC, SEQ], F32R))
        cst = put("cst", [P, C_END])
        stat = put("stat", [P, 128])
        sums = put("sums", [P, 9, NT, 4])
        unwanted = put("unwanted", [P, 512], mybir.dt.bfloat16)
        X0 = top[0]
        x_sb = put("x_sb", [P, NT, D])
        ARENA = top[0]
        K = 1024

        def arena(name, shape, at, dt=F32):
            return put(name, shape, dt, at=ARENA + int(at * K))

        sigB = put("sigB", [P, NT, D], at=X0)
        sigA = arena("sigA", [P, NT, D], 0)
        u_mem = arena("u_mem", [P, NT, D], 0)
        obg = arena("obg", [P, NT, 1024], 16)
        gain_mem = arena("gain_mem", [P, D], 16)
        gain_x = arena("gain_x", [P, D], 40)
        qkva = arena("qkva", [P, NT, 1536], 24)
        gla = arena("gla", [P, NT, 2048], 36)
        SH = 52
        mem_sb = arena("mem_sb", [P, NT, D], 24)
        u_x = arena("u_x", [P, NT, D], 24)
        ckv1 = arena("ckv1", [P, 2, NT, 512], SH + 32)
        memT = (arena("memT_hi", [P, DC, SEQ], SH, F32R), arena("memT_lo", [P, DC, SEQ], SH + 16, F32R))
        bias = arena("bias", [P, A_HEADS, SEQ], SH)
        aqT = arena("aqT", [64, A_HEADS, SEQ], SH + 16)
        akT = arena("akT", [64, A_KV, SEQ], SH + 32)
        s1 = arena("s1", [P, 2, 2, 258], SH + 36)
        p1 = arena("p1", [P, 2, 2, 258], SH + 40.25)
        pT1 = arena("pT1", [P, 2, 4, P], SH + 44.5)
        la = arena("la", [P, NT, 512], SH)
        eb = arena("eb", [P, NT, 512], SH + 4)
        enb = arena("enb", [P, NT, 512], SH + 8)
        kst = arena("kst", [P, NT, 512], SH + 12)
        gqT = arena("gqT", [P, G_HEADS, SEQ], SH + 16)
        gkT = arena("gkT", [P, G_HEADS, SEQ], SH + 20)
        attT = arena("attT", [P, NT, G_HEADS, P], SH + 24)
        state = arena("state", [P, 3, G_HEADS, G_VAL], SH + 28)
        glowT = arena("glowT", [32, 1, SEQ], SH + 40)
        decay = arena("decay", [P, 16], SH + 41)
        yT = (arena("yT_hi", [P, DC, SEQ], SH, F32R), arena("yT_lo", [P, DC, SEQ], SH + 16, F32R))
        SH2 = SH + 49
        gup = arena("gup", [17, 512], SH2)
        glow = arena("glow", [P, NT, G_RANK], SH2 + 2)
        glag = arena("glag", [P, G_VAL], SH2 + 2.125)
        sinks_b = arena("sinks_b", [P, A_HEADS], SH2 + 3.125)
        relb = arena("relb", [33, A_HEADS], SH2 + 3.1875)
        brow = arena("brow", [A_HEADS, C_BIASW], SH + 46)
        hT = (arena("hT_hi", [P, 24, SEQ], 0, F32R), arena("hT_lo", [P, 24, SEQ], 24, F32R))
        hb = arena("hb", [P, 2, NT, 512], 48)
        sil = arena("sil", [P, NT, 512], 56)
        u = arena("u", [P, NT, D], 64)
        gain = arena("gain", [P, D], 96)
        gain4 = arena("gain4", [P, D], 80)
        idx = arena("idx", [P, NT, 1104], 0)
        iqT = arena("iqT", [64, I_HEADS, SEQ], 9)
        ikT = arena("ikT", [64, 1, SEQ], 25)
        mqT = arena("mqT", [P, M_HEADS, SEQ], 0)
        mrT = arena("mrT", [64, M_HEADS, SEQ], 8)
        mkT = arena("mkT", [P, M_HEADS, SEQ], 16)
        krT = arena("krT", [64, 1, SEQ], 26)
        sqT = arena("sqT", [P, S_HEADS, SEQ], 0)
        skT = arena("skT", [P, S_HEADS, SEQ], 8)
        mq = arena("mq", [P, NT, 1536], 27)
        mout = arena("mout", [P, NT, 1024], 27)
        mkv = arena("mkv", [P, NT, 2048], 39)
        s2 = arena("s2", [P, 2, 2, 258], 55)
        p2 = arena("p2", [P, 2, 2, 258], 59.25)
        pT2 = arena("pT2", [P, 2, 4, P], 63.5)
        rel = arena("rel", [P, 2, 2, SEQ], 55)
        work = arena("work", [P, 2, SEQ], 101)
        dsa = arena("dsa", [P, NT, 3072], 68)
        c_sb = arena("c_sb", [P, NT, 832], 68)
        cT = (arena("cT_hi", [P, 6, SEQ], 75, F32R), arena("cT_lo", [P, 6, SEQ], 81, F32R))
        gcq = arena("gcq", [P, 768], 101)
        SM = 92
        score = arena("score", [P, NT, SEQ], SM)
        sel = arena("sel", [P, NT, SEQ], SM)
        trig = arena("trig", [P, 2, NT, 32], 94)
        rtmp = arena("rtmp", [P, 4, 256], 96)
        pos_i = arena("pos_i", [P, NT], 104.25, I32)
        ang = arena("ang", [P, 4, NT, 32], 100)
        ckv = arena("ckv", [P, 2, NT, 512], 0)
        ckT = arena("ckT", [P, C_HEADS, SEQ], 8)
        cqo = arena("cqo", [P, NT, 512], 12)
        cqT = arena("cqT", [P, C_HEADS, SEQ], 16)
        coT = (arena("coT_hi", [P, 4, SEQ], 20, F32R), arena("coT_lo", [P, 4, SEQ], 24, F32R))

        acc = [[ctx.enter_context(nc.psum_tensor(f"acc{p}{t}", [P, 512], F32)) for t in range(NT)] for p in range(2)]
        bank = [ctx.enter_context(nc.psum_tensor(f"unit{i}", [P, 512], F32)) for i in range(2)]
        psS = ctx.enter_context(nc.psum_tensor("psS", [P, 2, 256], F32))
        psO = ctx.enter_context(nc.psum_tensor("psO", [P, 2, 256], F32))

        keep_kv = nc.dram_tensor("keep_kv", [2, SEQ, 512], F32, kind="Internal")
        keep_bias = nc.dram_tensor("keep_bias", [A_HEADS, P, C_BIASW], F32, kind="Internal")

        w_landed = [sem(f"w_landed{i}") for i in range(RING)]
        hi_split = sem("hi_split")
        lo_split = sem("lo_split")
        tile_done = sem("tile_done")
        acc0_done = sem("acc0_done")
        acc_free = [[sem(f"acc{p}{t}_free") for t in range(NT)] for p in range(2)]
        unit_done = sem("unit_done")
        unit_hi = sem("unit_hi")
        unit_free = [sem(f"unit{i}_free") for i in range(2)]
        sc_done = sem("scores_done")
        sc_read = sem("scores_read")
        max_done = sem("max_done")
        exp_done = sem("exp_done")
        out_acc = sem("attention_out_acc")
        out_done = sem("attention_out_done")
        ident_in, const_in = sem("ident_in"), sem("const_in")
        mem_in = [sem("mem0_in"), sem("mem1_in")]
        x_in = [sem("x_in"), sem("x_again_in")]
        gain_in = [sem(f"gain_in{i}") for i in range(8)]
        small_in = sem("small_in")
        gcq_in = sem("gcq_in")
        ckv_kept, ckv_back = sem("ckv_kept"), sem("ckv_back")
        bias_kept, bias_in = sem("bias_kept"), sem("bias_in")
        squares = sem("squares")
        gained = sem("gained")
        x_gained = sem("x_gained")
        u_ready = sem("u_ready")
        z_log, la_ready = sem("z_log"), sem("la_ready")
        obg_tanh = sem("obg_tanh")
        sig_ready = sem("sig_ready")
        exp_sum, gq_ready, gk_ready = sem("exp_sum"), sem("gq_ready"), sem("gk_ready")
        head_squares, ob_normed, ob_ready = sem("head_squares"), sem("ob_normed"), sem("ob_ready")
        merged_ready = sem("merged_ready")
        h2_ready = sem("h2_ready")
        angles_ready, trig_ready = sem("angles_ready"), sem("trig_ready")
        roped = {k: sem(f"roped_{k}") for k in ("idx", "kr", "mq", "dsa")}
        c_squares, c_normed = sem("c_squares"), sem("c_normed")
        rel_used = sem("rel_used")
        mean_ready, rstd_ready = sem("mean_ready"), sem("rstd_ready")
        x_renormed = sem("x_renormed")
        mem_squares = sem("mem_squares")
        out_stored, ttr_done = sem("out_stored"), sem("ttr_done")
        dve_step, act_step, pool_step = sem("dve_step"), sem("act_step"), sem("pool_step")

        def acc_ready(eng, b, t, last_tile):
            if t == 0:
                eng.wait_ge(acc0_done, b + 1)
            else:
                eng.wait_ge(tile_done, last_tile + 1)

        def block_read(eng, b, t):
            eng.wait_ge(acc_free[b % 2][t], b // 2 + 1)

        def units_read(eng, n):
            for i in range(2):
                if n >= i:
                    eng.wait_ge(unit_free[i], (n - i) // 2 + 1)

        BLOCK = {}
        for s, at in SCHEDULE:
            if s[0] == "evac":
                BLOCK[s[1]["evac"], s[1]["arg"]] = at["block"]

        BUF = dict(qkva=qkva, gla=gla, glow=glow, idx=idx, c=c_sb, mq=mq, mkv=mkv, dsa=dsa, cqo=cqo)
        SRC = dict(u_mem=u_mem, qkva=qkva, gla=gla, glow=glow, merged=sigA, idx=idx, c=c_sb, mout=mout, dsa=dsa, cqo=cqo)
        LHS = dict(memT=memT, xT=xT, yT=yT, cT=cT, coT=coT, hT=hT)
        DST = dict(aqT=aqT, akT=akT, glowT=glowT, gqT=gqT, gkT=gkT, iqT=iqT, ikT=ikT, krT=krT, mqT=mqT, mrT=mrT,
                   mkT=mkT, sqT=sqT, skT=skT, ckT=ckT, cqT=cqT)
        SRC.update(hb0=hb[:, 0], hb1=hb[:, 1])

        def piece(name, i, t, norm):
            src, col, width, _, _, _, _ = TRANSPOSES[name]
            if src == "u":
                return (u_x if norm == 1 else u)[:, t, col + i * width:col + (i + 1) * width]
            if src == "mq":
                return mq[:, t, (4 * col + i) * 192:(4 * col + i) * 192 + 128]
            if src == "mr":
                return mq[:, t, (4 * col + i) * 192 + 128:(4 * col + i + 1) * 192]
            if src == "mkv":
                return mkv[:, t, (4 * col + i) * 256:(4 * col + i) * 256 + 128]
            if src == "ckv":
                return ckv[:, 0, t, i * 128:(i + 1) * 128]
            return SRC[src][:, t, col + i * width:col + (i + 1) * width]

        def heads_view(which, t):
            if which == "idx":
                return idx[:, t, 0:1088].rearrange("p (h d) -> p h d", d=I_DIM), I_ROT // 2
            if which == "kr":
                return c_sb[:, t, 768:832].rearrange("p (h d) -> p h d", d=M_ROPE), M_ROPE // 2
            if which == "mq":
                return mq[:, t, :].rearrange("p (h d) -> p h d", d=M_NOPE + M_ROPE)[:, :, M_NOPE:], M_ROPE // 2
            return dsa[:, t, 0:2048].rearrange("p (h d) -> p h d", d=S_DIM), S_ROT // 2

        def attention(kind):
            if kind == "A":
                return s1, p1, pT1, A_DIM ** -0.5, A_DIM
            scale = {"M": (M_NOPE + M_ROPE) ** -0.5, "S": S_DIM ** -0.5, "C": C_DIM ** -0.5}[kind]
            return s2, p2, pT2, scale, 128

        def values(kind, kt, h):
            if kind == "A":
                return qkva[:, kt, 1280 + (h // 4) * 64:1280 + (h // 4 + 1) * 64]
            if kind == "M":
                return mkv[:, kt, h * 256 + 128:(h + 1) * 256]
            if kind == "S":
                return dsa[:, kt, 2048 + h * 128:2048 + (h + 1) * 128]
            return ckv[:, 1, kt, h * 128:(h + 1) * 128]

        def outputs(kind, t, h, dv):
            to = {"A": qkva, "M": mout, "S": dsa, "C": cqo}[kind]
            return to[:, t, h * dv:(h + 2) * dv].rearrange("p (i v) -> p i v", i=2)

        ident = cst[:, C_IDENT:C_IDENT + P]
        block = ctx.enter_context(nc.Block())

        @block.sync
        def _(sp):
            tok = lambda a: a.rearrange("(t p) d -> p t d", p=P)
            sp.dma_start(mem_sb[:, 0], t_in["mem_2"][0, 0:P]).then_inc(mem_in[0], 16)
            sp.dma_start(cst[:, C_IDENT:C_IDENT + P], t_in["const"][:, C_IDENT:C_IDENT + P]).then_inc(ident_in, 16)

            def tile(slot, free, src, kc, n):
                if free is not None:
                    sp.wait_ge(lo_split, free)
                sp.dma_start(w_raw[:, slot, 0:kc, 0:n], src.rearrange("(c p) n -> p c n", p=P)).then_inc(
                    w_landed[slot], 16)

            for s, at in SCHEDULE:
                i = at["tile"]
                if s[0] == "tile" or s[0] == "part" and s[3] == 0:
                    b, k = s[1], s[2]
                    kc = min(CK, b["kc"] - k * CK)
                    if i == 1:
                        sp.dma_start(mem_sb[:, 1], t_in["mem_2"][0, P:2 * P]).then_inc(mem_in[1], 16)
                    r = (b["k0"] + k * CK) * P
                    tile(i % RING, i - RING + 1 if i >= RING else None,
                         t_in[b["w"]][r:r + kc * P, b["c0"]:b["c0"] + b["n"]], kc, b["n"])
                    if i == RING - 1:
                        sp.dma_start(x_sb[:], tok(t_in["x"][0])).then_inc(x_in[0], 16)
                        sp.dma_start(cst[:, P:], t_in["const"][:, P:]).then_inc(const_in, 16)
                elif s[0] == "swiglu_up":
                    with sp.Fori(1, s[2]) as r:
                        for j, w in enumerate(("w_ffn_gate", "w_ffn_up")):
                            for k in range(8):
                                tile(k % RING, i - 16 + 8 * j + k - RING + 1 + r * 16,
                                     t_in[w][2 * k * P:(2 * k + 2) * P, bass.ds(r * 512 + s[1] * 512, 512)], 2, 512)
                elif s[0] == "relu2_up":
                    with sp.Fori(1, s[2] // 2) as r:
                        for j in range(2):
                            for k in range(8):
                                tile(k % RING, i - 16 + 8 * j + k - RING + 1 + r * 16,
                                     t_in["w_up_2"][2 * k * P:(2 * k + 2) * P,
                                                    bass.ds(r * 1024 + (s[1] + j) * 512, 512)], 2, 512)
                elif s[0] == "down":
                    n = s[3] // CK
                    with sp.Fori(0, 2) as r:
                        for j in range(2):
                            for k in range(n):
                                o = i + n * j + k
                                row = (s[2] + 2 * k) * P
                                tile(o % RING, o - RING + 1 + r * (2 * n),
                                     t_in[s[1]][row:row + 2 * P, bass.ds(r * 1024 + j * 512, 512)], 2, 512)
                elif s[0] == "store":
                    _, n, j, t = s
                    c = slice(512 * j, 512 * j + 512)
                    sp.wait_ge(u_ready, at["scaled"] + 1)
                    sp.dma_start(out[0, t * P:(t + 1) * P, c], u[:, t, c]).then_inc(out_stored, 16)
            sp.wait_ge(out_stored, 16 * NT * 4)

        @block.gpsimd
        def _(pool):
            steps = [0]

            def after(ins):
                steps[0] += 1
                ins.then_inc(pool_step, 1)
                pool.wait_ge(pool_step, steps[0])

            def rows(dst, vec, sm):
                pool.dma_start(dst, vec.unsqueeze(0).broadcast_to([P, vec.shape[0]])).then_inc(sm, 16)

            rows(gain_x[:], t_in["norm_mix_g"][0], gain_in[1])
            after(pool.memset(relb[32:33, :], 1.0))
            pool.dma_start(relb[0:32, :], t_in["rel_bias"]).then_inc(small_in, 16)
            pool.dma_start(gup[0:G_RANK, :], t_in["w_gate_up"]).then_inc(small_in, 16)
            pool.dma_start(gup[G_RANK:G_RANK + 1, :], t_in["b_gate"]).then_inc(small_in, 16)
            rows(glag[:], t_in["gla_norm_g"][0], small_in)
            rows(sinks_b[:], t_in["sinks"][0], small_in)
            for t in range(NT):
                pool.dma_start(pos_i[:, t:t + 1], t_in["positions_2"][0, t * P:(t + 1) * P].unsqueeze(1)).then_inc(small_in, 16)

            roots = [0]

            after(pool.memset(stat[:, 100:108], -0.5))

            def rstd(c0, n):
                roots[0] += 1
                pool.wait_ge(mean_ready, roots[0])
                v = stat[:, c0:c0 + n]
                pool.tensor_tensor(v, v, stat[:, 100:100 + n], ALU.pow).then_inc(rstd_ready, 1)

            def rotate(which, t):
                v, half = heads_view(which, t)
                n = v.shape[1]
                x1, x2 = v[:, :, 0:half], v[:, :, half:2 * half]
                cos, sin = (trig[:, i, t, 0:32:32 // half].unsqueeze(1).broadcast_to([P, n, half]) for i in range(2))
                tmp = [rtmp[:, i, 0:n * half].rearrange("p (h f) -> p h f", f=half) for i in range(4)]
                for dst, a, b in zip(tmp, (x1, x2, x2, x1), (cos, sin, cos, sin)):
                    last = pool.tensor_tensor(dst, a, b, ALU.mult)
                after(last)
                pool.tensor_tensor(x1, tmp[0], tmp[1], ALU.subtract)
                last = pool.tensor_tensor(x2, tmp[2], tmp[3], ALU.add)
                last.then_inc(roped[which], 1)
                pool.wait_ge(roped[which], t + 1)

            for s, at in SCHEDULE:
                if s[0] == "gain":
                    n = s[1]
                    if n == 2:
                        pool.wait_ge(merged_ready, 8)
                    elif n != 4:
                        pool.wait_ge(gained, at["gained"])
                    if n == 5:
                        pool.wait_ge(c_normed, 4)
                        pool.wait_ge(out_done, GROUP0["S"] + NGROUPS["S"])
                        pool.wait_ge(x_gained, 8)
                        pool.dma_start(ckv[:], keep_kv.ap().rearrange("a (t p) d -> p a t d", p=P)).then_inc(ckv_back, 16)
                    name = ["", "", "norm_ffn_g", "norm_final_g", "g_mix_2", "g_cross_2", "g_mlp_2", "g_final_2"][n]
                    vec = t_in[name]
                    rows((gain4 if n == 4 else gain)[:], vec if len(vec.shape) == 1 else vec[0], gain_in[n])
                elif s[0] == "gained":
                    _, n, j, t = s
                    c = slice(512 * j, 512 * j + 512)
                    if (j, t) == (0, 0):
                        pool.wait_ge(gain_in[n + (n == 3)], 16)
                        if n == 1:
                            pool.wait_ge(x_in[0], 16)
                            pool.wait_ge(u_ready, 8)
                        elif n > 2:
                            pool.wait_ge(unit_done, at["u3"] + 1)
                    if n == 3:
                        pool.wait_ge(x_gained, 2 * j + t + 1)
                    elif n > 1:
                        block_read(pool, at["block"], t)
                    dst, g = (u_x, gain_x) if n == 1 else (u, gain4 if n == 3 else gain)
                    pool.tensor_tensor(dst[:, t, c], x_sb[:, t, c], g[:, c], ALU.mult).then_inc(gained, 1)
                elif s[0] == "rstd":
                    n, t = s[1], s[2]
                    if n == 3:
                        rstd(12 + 2 * t, 2)
                    else:
                        rstd(4 * n + t, 1)
                elif s[0] == "renorm_x":
                    pool.wait_ge(squares, at["squares"])
                    pool.wait_ge(gained, at["gained"])
                    for t in range(NT):
                        pool.tensor_scalar(x_sb[:, t, :], x_sb[:, t, :], stat[:, 12 + 2 * t:13 + 2 * t], None,
                                           ALU.mult).then_inc(x_renormed, 1)
                elif s[0] == "c_norm":
                    rstd(66, 4)
                elif s[0] == "keep_ckv":
                    for i in range(2):
                        for t in range(NT):
                            block_read(pool, BLOCK["ckv", i], t)
                    pool.dma_start(keep_kv.ap().rearrange("a (t p) d -> p a t d", p=P), ckv1[:]).then_inc(ckv_kept, 16)
                elif s[0] == "bias_row":
                    units_read(pool, at["unit"])
                    pool.dma_start(keep_bias[:, :, :], brow[:].unsqueeze(1).broadcast_to([A_HEADS, P, C_BIASW])).then_inc(
                        bias_kept, 16)
                    pool.wait_ge(bias_kept, 16)
                    pool.dma_start(bias[:], bass.AP(tensor=keep_bias, offset=P - 1,
                                                    ap=[[C_BIASW - 1, P], [P * C_BIASW, A_HEADS], [1, SEQ]])).then_inc(bias_in, 16)
                elif s[0] == "gate_z":
                    t = s[1]
                    pool.wait_ge(z_log, t + 1)
                    pool.tensor_tensor(la[:, t, :], enb[:, t, :], eb[:, t, :], ALU.subtract).then_inc(la_ready, 1)
                elif s[0] == "gate_sum":
                    t = s[1]
                    pool.wait_ge(exp_sum, t + 1)
                    pool.tensor_tensor(gla[:, t, 0:512], gla[:, t, 0:512], eb[:, t, :], ALU.mult).then_inc(gq_ready, 1)
                elif s[0] == "gate_rest":
                    t = s[1]
                    units_read(pool, at["unit"])
                    after(pool.tensor_tensor(kst[:, t, :], kst[:, t, :], gla[:, t, 512:1024], ALU.mult))
                    pool.tensor_tensor(gla[:, t, 512:1024], gla[:, t, 512:1024], enb[:, t, :], ALU.mult).then_inc(
                        gk_ready, 1)
                elif s[0] == "evac" and s[1]["evac"] in ("sigA", "sigB"):
                    buf, col = (sigA if s[1]["evac"] == "sigA" else sigB), s[1]["arg"]
                    for t in range(NT):
                        block_read(pool, at["block"], t)
                        v = buf[:, t, col:col + 512]
                        pool.tensor_scalar(v, v, 0.5, 0.5, ALU.mult, ALU.add).then_inc(sig_ready, 1)
                elif s[0] == "gla_norm":
                    rstd(50, 8)
                    for t in range(NT):
                        pool.wait_ge(ob_normed, t + 1)
                        v = gla[:, t, 0:1024]
                        pool.tensor_tensor(v, v, obg[:, t, :], ALU.mult).then_inc(ob_ready, 1)
                elif s[0] == "evac" and s[1]["evac"] == "merge":
                    j = s[1]["arg"] // 512
                    for t in range(NT):
                        block_read(pool, at["block"], t)
                        c = slice(512 * j, 512 * j + 512)
                        pool.tensor_tensor(sigA[:, t, c], sigA[:, t, c], sigB[:, t, c], ALU.add).then_inc(
                            merged_ready, 1)
                elif s[0] == "load_x":
                    pool.wait_ge(merged_ready, 8)
                    pool.dma_start(x_sb[:], t_in["x"][0].rearrange("(t p) d -> p t d", p=P)).then_inc(x_in[1], 16)
                elif s[0] == "angles":
                    pool.wait_ge(u_ready, at["scaled"])
                    rows(gcq[:, 0:512], t_in["g_cq_2"][0], gcq_in)
                    rows(gcq[:, 512:768], t_in["g_ckv_2"][0], gcq_in)
                    pool.wait_ge(trig_ready, 2)
                elif s[0] == "rope":
                    which = s[1]
                    blocks = {"idx": [("idx", 368 * j) for j in range(3)], "kr": [("c", 416)],
                              "mq": [("mq", 384 * j) for j in range(4)],
                              "dsa": [("dsa", 512 * j) for j in range(4)]}[which]
                    for t in range(NT):
                        for b in blocks:
                            block_read(pool, BLOCK[b], t)
                        if which == "mq":
                            pass
                        rotate(which, t)

        @block.scalar
        def _(act):
            act.dma_start(gain_mem[:], t_in["g_mem_2"][0].unsqueeze(0).broadcast_to([P, D])).then_inc(gain_in[0], 16)

            def split_hi(i, slot, uses, free, kc=CK, n=COLS):
                act.wait_ge(w_landed[slot], uses)
                if free is not None:
                    act.wait_ge(tile_done, free)
                act.activation(w_hi[:, slot, 0:kc, 0:n], w_raw[:, slot, 0:kc, 0:n], ACT.Copy).then_inc(hi_split, 1)

            def lead(i, more=0):
                if isinstance(more, int) and i + more >= TILES:
                    return
                static = isinstance(more, int) and more == 0
                split_hi(i, i % RING, 16 * (i // RING + 1) + (0 if static else more * (16 // RING)),
                         (i - RING + 1 if i >= RING else None) if static else i - RING + 1 + more,
                         *(SHAPES.get(i, (CK, COLS)) if static else (CK, COLS)))

            def hi(bk, w, n, dst, i0, t):
                act.activation(dst[0][0:w, i0:i0 + n, t * P:(t + 1) * P],
                               bank[bk][0:w, 0:n * P].rearrange("p (c q) -> p c q", q=P), ACT.Copy).then_inc(unit_hi, 1)

            def hidden_hi(c, t, unit):
                act.wait_ge(unit_done, unit)
                act.activation(hT[0][:, bass.ds(c, 4), t * P:(t + 1) * P],
                               bank[t][:].rearrange("p (c q) -> p c q", q=P), ACT.Copy).then_inc(unit_hi, 1)

            for s, at in SCHEDULE:
                U, B = at["unit"], at["block"]
                if s[0] == "lead":
                    lead(s[1])
                elif s[0] == "tile" or s[0] == "part" and s[3] == 1:
                    lead(at["tile"] + LEAD)
                elif s[0] == "ssq":
                    _, n, j, t = s
                    if n == 0 and j >= 2:
                        continue
                    c = slice(512 * j, 512 * j + 512)
                    if n == 0:
                        act.wait_ge(mem_in[t], 16)
                    elif n == 1:
                        act.wait_ge(x_in[0], 16)
                    else:
                        block_read(act, at["block"], t)
                    src = mem_sb if n == 0 else x_sb
                    if at["squares"]:
                        act.wait_ge(squares, at["squares"])
                    act.activation(unwanted[:], src[:, t, c], ACT.Square, accum_out=sums[:, n, t, j:j + 1]).then_inc(squares, 1)
                    if n == 3:
                        act.wait_ge(x_gained, 2 * j + t + 1)
                        act.wait_ge(squares, at["squares"] + 1)
                        act.activation(unwanted[:], src[:, t, c], ACT.Square, accum_out=sums[:, 8, t, j:j + 1]).then_inc(
                            squares, 1)
                elif s[0] == "T":
                    name, t = s[1], s[2]
                    _, _, w, n, dst, i0, mode = TRANSPOSES[name]
                    if mode == "split":
                        act.wait_ge(unit_done, U + 1)
                        hi(U % 2, w, n, LHS[dst], i0, t)
                    elif mode == "act":
                        if name == "ak" and t == 0:
                            act.wait_ge(ckv_kept, 16)
                        act.wait_ge(unit_done, U + 1)
                        scale = G_KEY ** -0.5 if name == "gq" else 1.0
                        act.activation(DST[dst][0:w, i0:i0 + n, t * P:(t + 1) * P],
                                       bank[U % 2][0:w, 0:n * P].rearrange("p (c q) -> p c q", q=P),
                                       ACT.Copy, scale=scale).then_inc(unit_free[U % 2], 1)
                elif s[0] == "evac":
                    b, what, arg, n = B, s[1]["evac"], s[1]["arg"], s[1]["n"]
                    last = at["tile"] - 1
                    ac = acc[b % 2]
                    if what == "ckv":
                        acc_ready(act, b, 0, last)
                        act.activation(ckv1[:, arg, 0, :], ac[0][:], ACT.Copy).then_inc(acc_free[b % 2][0], 1)
                    elif what in BUF:
                        if what == "gla" and arg == 0:
                            act.wait_ge(u_ready, 16)
                        acc_ready(act, b, 0, last)
                        act.activation(BUF[what][:, 0, arg:arg + n], ac[0][:, 0:n], ACT.Copy).then_inc(
                            acc_free[b % 2][0], 1)
                    elif what == "obg":
                        skip = G_RANK if arg == 0 else 0
                        for t in range(NT):
                            acc_ready(act, b, t, last)
                            if skip:
                                act.activation(glow[:, t, :], ac[t][:, 0:skip], ACT.Copy)
                            act.activation(obg[:, t, arg:arg + n - skip], ac[t][:, skip:n], ACT.Tanh, scale=0.5).then_inc(
                                obg_tanh, 1)
                    elif what in ("silu", "relu2"):
                        for t in range(NT):
                            acc_ready(act, b, t, last)
                            act.activation(sil[:, t, :] if what == "silu" else hb[:, arg, t, :], ac[t][:],
                                           ACT.Silu if what == "silu" else ACT.Relu).then_inc(acc_free[b % 2][t], 1)
                    elif what in ("sigA", "sigB"):
                        buf = sigA if what == "sigA" else sigB
                        for t in range(NT):
                            acc_ready(act, b, t, last)
                            act.activation(buf[:, t, arg:arg + 512], ac[t][:], ACT.Tanh, scale=0.5).then_inc(
                                acc_free[b % 2][t], 1)
                elif s[0] == "scores":
                    g = s[1]
                    kind, t, h, nk = GROUPS[g]
                    _, pb, _, _, _ = attention(kind)
                    sb_ = attention(kind)[0]
                    act.wait_ge(max_done, g + 1)
                    w = nk + 1 if kind == "A" else nk
                    for i in range(2):
                        ins = act.activation(pb[:, g % 2, i, 0:w], sb_[:, g % 2, i, 0:w], ACT.Exp,
                                             bias=stat[:, 40 + 2 * (g % 2) + i:41 + 2 * (g % 2) + i],
                                             accum_out=stat[:, 110 + 2 * (g % 4) + i:111 + 2 * (g % 4) + i])
                    ins.then_inc(exp_done, 1)
                elif s[0] == "probs_T":
                    g = s[1]
                    kind, t, h, nk = GROUPS[g]
                    n = 2 * nk // P
                    act.wait_ge(unit_done, U + 1)
                    act.activation(attention(kind)[2][:, g % 2, 0:n, :],
                                   bank[U % 2][:, 0:n * P].rearrange("p (c q) -> p c q", q=P), ACT.Copy).then_inc(
                        unit_free[U % 2], 1)
                elif s[0] == "gate_z":
                    t = s[1]
                    units_read(act, U)
                    act.activation(eb[:, t, :], eb[:, t, :], ACT.Exp).then_inc(act_step, 1)
                    act.wait_ge(act_step, t + 1)
                    act.activation(eb[:, t, :], eb[:, t, :], ACT.Ln, bias=1.0).then_inc(z_log, 1)
                elif s[0] == "gate_sum":
                    t = s[1]
                    act.wait_ge(unit_done, U + 1)
                    act.activation(eb[:, t, :], bank[U % 2][:], ACT.Exp).then_inc(exp_sum, 1)
                    act.activation(enb[:, t, :], bank[U % 2][:], ACT.Exp, scale=-1.0).then_inc(unit_free[U % 2], 1)
                elif s[0] == "gate_rest":
                    t = s[1]
                    act.wait_ge(unit_done, U + 1)
                    ins = act.activation(kst[:, t, :], bank[U % 2][:], ACT.Exp)
                    ins.then_inc(unit_free[U % 2], 1)
                elif s[0] == "gate_decay":
                    act.wait_ge(unit_done, U + 1)
                    act.activation(decay[:], bank[U % 2][:, 0:16], ACT.Exp).then_inc(unit_free[U % 2], 1)
                elif s[0] == "gla_out" and s[2] == 0:
                    act.wait_ge(unit_done, U + 1)
                    act.activation(gla[:, s[1], 0:512], bank[U % 2][:], ACT.Copy).then_inc(unit_free[U % 2], 1)
                elif s[0] == "gla_norm":
                    units_read(act, U - 1)
                    for t in range(NT):
                        for h in range(G_HEADS):
                            junk = (eb, enb)[t][:, h // 2, 256 * (h % 2):256 * (h % 2) + 256]
                            act.activation(junk, gla[:, t, 256 * h:256 * h + 256], ACT.Square,
                                           accum_out=stat[:, 50 + 4 * t + h:51 + 4 * t + h]).then_inc(head_squares, 1)
                elif s[0] == "angles":
                    act.wait_ge(angles_ready, 1)
                    for i in range(2):
                        act.activation(trig[:, i], ang[:, 2 + i], ACT.Sin).then_inc(trig_ready, 1)
                elif s[0] == "idx":
                    t, n = s[1], at["nth"]
                    nk = SEQ if t else P
                    if n >= 2:
                        act.wait_ge(rel_used, n - 1)
                    act.wait_ge(unit_done, U + 1)
                    act.activation(rel[:, n % 2, :, 0:nk], bank[U % 2][:].rearrange("p (i k) -> p i k", i=2)[:, :, 0:nk],
                                   ACT.Relu, scale=1.0 / 32).then_inc(unit_free[U % 2], 1)
                elif s[0] == "c_norm":
                    for i, (c0, n) in enumerate(((0, 512), (512, 256))):
                        for t in range(NT):
                            block_read(act, BLOCK["c", 0], t)
                            block_read(act, BLOCK["c", 416], t)
                            act.activation(mkv[:, t, c0:c0 + n], c_sb[:, t, c0:c0 + n], ACT.Square,
                                           accum_out=stat[:, 66 + 2 * i + t:67 + 2 * i + t]).then_inc(c_squares, 1)
                elif s[0] in ("swiglu_up", "relu2_up"):
                    glu = s[0] == "swiglu_up"
                    T0, B = at["tile"] - 16, B - 2
                    U -= 0 if glu else 2

                    with act.Fori(1, s[2] if glu else s[2] // 2) as r:
                        m = r * 16
                        for k in range(8):
                            lead(T0 + k + LEAD, m)
                        for t in range(NT):
                            if t == 0:
                                act.wait_ge(acc0_done, B + 1 + r * 2)
                            else:
                                act.wait_ge(tile_done, T0 + 8 + m)
                            if glu:
                                act.wait_ge(acc_free[1][t], B // 2 + r)
                            act.activation(sil[:, t, :] if glu else hb[:, 0, t, :], acc[0][t][:],
                                           ACT.Silu if glu else ACT.Relu).then_inc(acc_free[0][t], 1)
                        for t in range(NT):
                            hidden_hi((r - 1) * 4 if glu else (r - 1) * 8 + 4, t, U - 2 + t + 1 + r * (2 if glu else 4))
                        for k in range(8):
                            lead(T0 + 8 + k + LEAD, m)
                        if not glu:
                            for t in range(NT):
                                if t == 0:
                                    act.wait_ge(acc0_done, B + 2 + r * 2)
                                else:
                                    act.wait_ge(tile_done, T0 + 16 + m)
                                act.activation(hb[:, 1, t, :], acc[1][t][:], ACT.Relu).then_inc(acc_free[1][t], 1)
                            for t in range(NT):
                                hidden_hi(r * 8, t, U + t + 1 + r * 4)
                elif s[0] == "down":
                    n, T0 = s[3] // CK, at["tile"]
                    with act.Fori(0, 2) as r:
                        for k in range(2 * n):
                            lead(T0 + k + LEAD, r * (2 * n))

        @block.tensor
        def _(pe):
            def products(ac, b_lhs, l0, kc, slot, n, t, start, stop):
                hi_, lo_ = b_lhs
                for c in range(kc):
                    for m, (a, w) in enumerate(((hi_, w_hi), (lo_, w_hi), (hi_, w_lo))):
                        ins = pe.matmul(ac[t][:, 0:n], a[:, l0 + c, t * P:(t + 1) * P], w[:, slot, c, 0:n],
                                        start=start and c == 0 and m == 0, stop=stop and c == kc - 1 and m == 2)
                return ins

            def dense_tile(i, p, free, lhs, l0, kc, n, first, last, more=0, ts=(0, 1)):
                pe.wait_ge(lo_split, i + 1 + more)
                for t in ts:
                    if first and free is not None:
                        pe.wait_ge(acc_free[p][t], free)
                    ins = products(acc[p], lhs, l0, kc, i % RING, n, t, first, last)
                    if t == 0 and last:
                        ins.then_inc(acc0_done, 1)
                if 1 in ts:
                    ins.then_inc(tile_done, 1)

            def bank_free(n):
                if n >= 2:
                    pe.wait_ge(unit_free[n % 2], n // 2)

            def transpose_pieces(bk, pieces, w):
                for i, a in enumerate(pieces):
                    ins = pe.transpose(bank[bk][0:w, i * P:(i + 1) * P], a, ident)
                ins.then_inc(unit_done, 1)

            def source_ready(name, t, at):
                src, col, w, _, _, _, _ = TRANSPOSES[name]
                if src in ("u", "u_mem"):
                    pe.wait_ge(u_ready, at["scaled"] + 1)
                elif name[:3] == "glu":
                    block_read(pe, at["block"] - 1, t)
                elif name == "hid0" or name[:4] == "relu":
                    pe.wait_ge(h2_ready, at["hidden"] - (4 if name == "hid0" else 2) + t + 1)
                elif name[:2] in ("aq", "ak"):
                    block_read(pe, BLOCK["qkva", col // 512 * 512], t)
                elif name == "glow":
                    block_read(pe, BLOCK["obg", 0], t)
                elif name in ("gq", "gk"):
                    pe.wait_ge(gq_ready if name == "gq" else gk_ready, t + 1)
                elif name[:2] == "ya":
                    pe.wait_ge(out_done, GROUP0["A"] + NGROUPS["A"])
                elif name[:2] == "yb":
                    pe.wait_ge(ob_ready, t + 1)
                elif src == "merged":
                    pe.wait_ge(merged_ready, 2 * (col // 512) + t + 1)
                elif src == "idx":
                    pe.wait_ge(roped["idx"], t + 1)
                elif name in ("cq", "ckv"):
                    pe.wait_ge(c_normed, t + 1 if name == "cq" else t + 3)
                elif name == "kr":
                    pe.wait_ge(roped["kr"], t + 1)
                elif src == "mq":
                    for j in range(4):
                        block_read(pe, BLOCK["mq", 384 * j], t)
                    pe.wait_ge(roped["mq"], t + 1)
                elif src == "mr":
                    pe.wait_ge(roped["mq"], t + 1)
                elif src == "mkv":
                    for j in range(4):
                        block_read(pe, BLOCK["mkv", 512 * j], t)
                elif src == "mout":
                    pe.wait_ge(out_done, GROUP0["M"] + NGROUPS["M"])
                elif name[:2] in ("sq", "sk"):
                    pe.wait_ge(roped["dsa"], t + 1)
                elif name in ("s0", "s1"):
                    pe.wait_ge(out_done, GROUP0["S"] + NGROUPS["S"])
                elif name == "ck":
                    pe.wait_ge(ckv_back, 16)
                elif name == "cqq":
                    block_read(pe, BLOCK["cqo", 0], t)
                elif name == "co":
                    pe.wait_ge(out_done, GROUP0["C"] + NGROUPS["C"])

            def score_terms(kind, h, t):
                q = slice(t * P, (t + 1) * P)
                if kind == "A":
                    return [(aqT[:, h, q], akT[:, h // 4])]
                if kind == "M":
                    return [(mqT[:, h, q], mkT[:, h]), (mrT[:, h, q], krT[:, 0])]
                if kind == "S":
                    return [(sqT[:, h, q], skT[:, h])]
                return [(cqT[:, h, q], ckT[:, h])]

            LAST_T = {"A": "ak", "M": "mr1", "S": "sk1", "C": "cqq"}
            pe.wait_ge(ident_in, 16)
            for s, at in SCHEDULE:
                U, B = at["unit"], at["block"]
                if s[0] in UNIT_STEPS:
                    bank_free(U)
                    ps = bank[U % 2]
                if s[0] in ("tile", "part"):
                    b, k = s[1], s[2]
                    if at["need"] is not None:
                        units_read(pe, at["need"])
                    dense_tile(at["tile"], B % 2, B // 2 if B >= 2 else None, LHS[b["lhs"]], b["l0"] + CK * k,
                               min(CK, b["kc"] - CK * k), b["n"], k == 0, at["last"], ts=(0, 1) if s[0] == "tile" else s[3:])
                elif s[0] == "T":
                    name, t = s[1], s[2]
                    _, _, w, n, _, _, _ = TRANSPOSES[name]
                    source_ready(name, t, at)
                    transpose_pieces(U % 2, [piece(name, i, t, at.get("norm")) for i in range(n)], w)
                elif s[0] == "scores":
                    g = s[1]
                    kind, t, h, nk = GROUPS[g]
                    if g == GROUP0[kind]:
                        units_read(pe, LAST_UNIT[LAST_T[kind], 1])
                        if kind in "MSC":
                            units_read(pe, U - 1)
                    if g:
                        pe.wait_ge(sc_read, g)
                    for i in range(2):
                        terms = score_terms(kind, h + i, t)
                        for m, (q, k) in enumerate(terms):
                            ins = pe.matmul(psS[:, i, 0:nk], q, k[:, 0:nk], start=m == 0, stop=m == len(terms) - 1)
                    ins.then_inc(sc_done, 1)
                elif s[0] == "probs_T":
                    g = s[1]
                    kind, t, h, nk = GROUPS[g]
                    pb = attention(kind)[1]
                    pe.wait_ge(exp_done, g + 1)
                    transpose_pieces(U % 2, [pb[:, g % 2, i, c * P:(c + 1) * P] for i in range(2) for c in range(nk // P)], P)
                elif s[0] == "output":
                    g = s[1]
                    kind, t, h, nk = GROUPS[g]
                    _, _, pT, _, dv = attention(kind)
                    units_read(pe, LAST_UNIT["probs", g])
                    if g:
                        pe.wait_ge(out_done, g)
                    if kind == "M" and g == GROUP0["M"]:
                        for j in range(4):
                            for tt in range(NT):
                                block_read(pe, BLOCK["mkv", 512 * j], tt)
                    if kind == "S" and g == GROUP0["S"]:
                        for j in range(6):
                            for tt in range(NT):
                                block_read(pe, BLOCK["dsa", 512 * j], tt)
                    for i in range(2):
                        for kt in range(nk // P):
                            ins = pe.matmul(psO[:, i, 0:dv], pT[:, g % 2, i * (nk // P) + kt, :], values(kind, kt, h + i),
                                            start=kt == 0, stop=kt == nk // P - 1)
                    ins.then_inc(out_acc, 1)
                elif s[0] == "bias_row":
                    pe.wait_ge(small_in, 16 * 7)
                    pe.wait_ge(const_in, 16)
                    pe.matmul(ps[0:A_HEADS, 0:C_BIASW], relb[0:33, :], cst[0:33, C_HOT:C_HOT + C_BIASW],
                              start=True, stop=True).then_inc(unit_done, 1)
                elif s[0] == "gate_z":
                    t = s[1]
                    units_read(pe, LAST_UNIT["glow", 1])
                    pe.matmul(ps[:], glowT[0:17, 0, t * P:(t + 1) * P], gup[0:17, :], start=True, stop=True).then_inc(
                        unit_done, 1)
                elif s[0] in ("gate_sum", "gate_rest"):
                    t = s[1]
                    c0 = C_TRI if s[0] == "gate_sum" else C_REST
                    pe.wait_ge(la_ready, t + 1)
                    pe.matmul(ps[:], cst[:, c0:c0 + P], la[:, t, :], start=True, stop=True).then_inc(unit_done, 1)
                elif s[0] == "gate_decay":
                    for t in range(NT):
                        for h in range(G_HEADS):
                            c0 = 4 * h + 2 * t
                            ins = pe.matmul(ps[:, c0:c0 + 2], la[:, t, h * P:(h + 1) * P], cst[:, C_IND:C_IND + 2],
                                            start=True, stop=True)
                    ins.then_inc(unit_done, 1)
                elif s[0] == "state":
                    n, h = s[1], s[2]
                    t, r = n // 2, CHUNK * (n % 2)
                    pe.wait_ge(gk_ready, t + 1)
                    for i in range(2):
                        v0 = 1024 + (h + i) * G_VAL
                        ins = pe.matmul(ps[:, i * G_VAL:(i + 1) * G_VAL], kst[r:r + CHUNK, t, (h + i) * P:(h + i + 1) * P],
                                        gla[r:r + CHUNK, t, v0:v0 + G_VAL], start=True, stop=True)
                    ins.then_inc(unit_done, 1)
                elif s[0] == "gla_att":
                    t = s[1]
                    units_read(pe, LAST_UNIT["gk", 1])
                    q = slice(t * P, (t + 1) * P)
                    for h in range(G_HEADS):
                        ins = pe.matmul(ps[:, h * P:(h + 1) * P], gkT[:, h, q], gqT[:, h, q], start=True, stop=True)
                    ins.then_inc(unit_done, 1)
                elif s[0] == "gla_out":
                    t, h = s[1], s[2]
                    if s[1:] == (0, 0):
                        units_read(pe, U - 1)
                    for i in range(2):
                        o = slice(i * G_VAL, (i + 1) * G_VAL)
                        v0 = 1024 + (h + i) * G_VAL
                        ins = pe.matmul(ps[:, o], attT[:, t, h + i, :], gla[:, t, v0:v0 + G_VAL], start=True, stop=False,
                                        skip_group_check=True)
                        for j in range(2):
                            n = 2 * t + j
                            if n:
                                r = slice(CHUNK * j, CHUNK * (j + 1))
                                ins = pe.matmul(ps[r, o], gqT[:, h + i, t * P + CHUNK * j:t * P + CHUNK * (j + 1)],
                                                state[:, n - 1, h + i, :], start=False, stop=j == 1, skip_group_check=True)
                    ins.then_inc(unit_done, 1)
                elif s[0] == "idx":
                    t, h = s[1], s[2]
                    nk = SEQ if t else P
                    if at["nth"] == 0:
                        units_read(pe, LAST_UNIT["ik", 1])
                    for i in range(2):
                        ins = pe.matmul(ps[:, i * SEQ:i * SEQ + nk], iqT[:, h + i, t * P:(t + 1) * P], ikT[:, 0, 0:nk],
                                        start=True, stop=True)
                    ins.then_inc(unit_done, 1)
                elif s[0] in ("swiglu_up", "relu2_up"):
                    glu, n = s[0] == "swiglu_up", s[2]
                    T0, B, h = at["tile"] - 16, B - 2, at["hidden"] - 4
                    U -= 0 if glu else 2

                    def pieces(j, t):
                        return [hb[:, j, t, c * P:(c + 1) * P] for c in range(4)]

                    with pe.Fori(1, n if glu else n // 2) as r:
                        for j in range(2):
                            for k in range(8):
                                dense_tile(T0 + 8 * j + k, j, B // 2 + r, xT, CK * k, CK, 512, k == 0, k == 7, r * 16)
                            for t in range(NT):
                                if j == 0:
                                    pe.wait_ge(unit_free[t], U // 2 + (r - 1 if glu else 2 * r - 1))
                                    if glu:
                                        pe.wait_ge(acc_free[1][t], B // 2 + r)
                                    else:
                                        pe.wait_ge(h2_ready, h - 2 + t + 1 + r * 4)
                                    transpose_pieces(t, pieces(0 if glu else 1, t), P)
                                elif not glu:
                                    pe.wait_ge(unit_free[t], U // 2 + 2 * r)
                                    pe.wait_ge(h2_ready, h + t + 1 + r * 4)
                                    transpose_pieces(t, pieces(0, t), P)
                elif s[0] == "down":
                    n, T0 = s[3] // CK, at["tile"]

                    def body(r):
                        for j in range(2):
                            for k in range(n):
                                if j == 0 and k in (0, n - 2):
                                    for t in range(NT):
                                        pe.wait_ge(unit_free[t], U // 2 - (k == 0))
                                dense_tile(T0 + n * j + k, j, B // 2 + r, hT, CK * k, CK, 512, k == 0, k == n - 1,
                                           r * (2 * n))

                    with pe.Fori(0, 2) as r:
                        body(r)

        @block.vector
        def _(dve):
            steps = [0]

            def after(ins):
                steps[0] += 1
                ins.then_inc(dve_step, 1)
                dve.wait_ge(dve_step, steps[0])

            def lead(i, more=0):
                if isinstance(more, int) and i + more >= TILES:
                    return
                dve.wait_ge(hi_split, i + 1 + more)
                slot = i % RING
                kc, n = SHAPES.get(i, (CK, COLS)) if isinstance(more, int) and more == 0 else (CK, COLS)
                dve.tensor_tensor(w_lo[:, slot, 0:kc, 0:n], w_raw[:, slot, 0:kc, 0:n],
                                  w_hi[:, slot, 0:kc, 0:n].bitcast(F32), ALU.subtract).then_inc(
                    lo_split, 1)

            def lo(bk, w, n, dst, i0, t):
                dve.tensor_tensor(dst[1][0:w, i0:i0 + n, t * P:(t + 1) * P],
                                  bank[bk][0:w, 0:n * P].rearrange("p (c q) -> p c q", q=P),
                                  dst[0][0:w, i0:i0 + n, t * P:(t + 1) * P].bitcast(F32), ALU.subtract).then_inc(
                    unit_free[bk], 1)

            def hidden_lo(bk, c, t):
                dve.tensor_tensor(hT[1][:, bass.ds(c, 4), t * P:(t + 1) * P],
                                  bank[bk][:].rearrange("p (c q) -> p c q", q=P),
                                  hT[0][:, bass.ds(c, 4), t * P:(t + 1) * P].bitcast(F32), ALU.subtract).then_inc(
                    unit_free[bk], 1)

            ones = stat[:, 60:64]
            after(dve.memset(ones, 1.0))

            def rstd(root, c0, n, *widths, by=1.0):
                for i, width in enumerate(widths):
                    v = stat[:, c0 + i * n:c0 + (i + 1) * n]
                    ins = dve.tensor_scalar(v, v, by / width, by * EPS, ALU.mult, ALU.add)
                ins.then_inc(mean_ready, 1)
                dve.wait_ge(rstd_ready, root + 1)

            for s, at in SCHEDULE:
                U, B = at["unit"], at["block"]
                if s[0] == "lead":
                    lead(s[1])
                elif s[0] == "tile" or s[0] == "part" and s[3] == 1:
                    lead(at["tile"] + LEAD)
                elif s[0] == "ssq":
                    _, n, j, t = s
                    c = slice(512 * j, 512 * j + 512)
                    if n == 0 and j >= 2:
                        dve.wait_ge(mem_in[t], 16)
                        dve.tensor_tensor_reduce(u_mem[:, t, c], mem_sb[:, t, c], mem_sb[:, t, c], 1.0, 0.0, ALU.mult, ALU.add,
                                                 sums[:, n, t, j:j + 1]).then_inc(mem_squares, 1)
                    elif n == 3:
                        if (j, t) == (0, 0):
                            dve.wait_ge(gain_in[3], 16)
                        block_read(dve, at["block"], t)
                        dve.wait_ge(squares, at["squares"] + 1)
                        v = x_sb[:, t, c]
                        dve.tensor_tensor(v, v, gain[:, c], ALU.mult).then_inc(x_gained, 1)
                elif s[0] == "rstd":
                    n, t = s[1], s[2]
                    c = 4 * n + t if n != 3 else 12 + 2 * t
                    dve.wait_ge(squares, at["squares"])
                    if n == 0:
                        dve.wait_ge(mem_squares, 2 * t + 2)
                    ins = dve.tensor_tensor_reduce(sums[:, n, t], sums[:, n, t], ones, 1.0 / D, EPS, ALU.mult, ALU.add,
                                                   stat[:, c:c + 1])
                    if n == 3:
                        after(ins)
                        after(dve.tensor_scalar(stat[:, 74:75], stat[:, c:c + 1], EPS, None, ALU.mult))
                        after(dve.tensor_tensor_reduce(sums[:, 8, t], sums[:, 8, t], ones, 1.0 / D, 0.0, ALU.mult, ALU.add,
                                                       stat[:, c + 1:c + 2]))
                        ins = dve.tensor_tensor(stat[:, c + 1:c + 2], stat[:, c + 1:c + 2], stat[:, 74:75], ALU.add)
                    ins.then_inc(mean_ready, 1)
                elif s[0] == "scaled":
                    _, n, j, t = s
                    c = slice(512 * j, 512 * j + 512)
                    if j == 0:
                        dve.wait_ge(rstd_ready, at["root"] + 1)
                    r = stat[:, 13 + 2 * t:14 + 2 * t] if n == 4 else stat[:, 4 * n + t:4 * n + t + 1]
                    if n == 0:
                        if (j, t) == (0, 0):
                            dve.wait_ge(gain_in[0], 16)
                        ins = dve.scalar_tensor_tensor(out=u_mem[:, t, c], in0=mem_sb[:, t, c], scalar=r, in1=gain_mem[:, c],
                                                       op0=ALU.mult, op1=ALU.mult)
                    else:
                        dve.wait_ge(gained, at["gained"] + 1)
                        v = (u_x if n == 1 else u)[:, t, c]
                        ins = dve.tensor_scalar(v, v, r, None, ALU.mult)
                    ins.then_inc(u_ready, 1)
                elif s[0] == "T":
                    name, t = s[1], s[2]
                    _, _, w, n, dst, i0, mode = TRANSPOSES[name]
                    if mode == "split":
                        dve.wait_ge(unit_hi, at["split"] + 1)
                        lo(U % 2, w, n, LHS[dst], i0, t)
                    elif mode == "dve":
                        if name == "glow" and t == 0:
                            after(dve.memset(glowT[0:32], 1.0))
                        dve.wait_ge(unit_done, U + 1)
                        dve.tensor_copy(DST[dst][0:w, i0:i0 + n, t * P:(t + 1) * P],
                                        bank[U % 2][0:w, 0:n * P].rearrange("p (c q) -> p c q", q=P)).then_inc(
                            unit_free[U % 2], 1)
                elif s[0] == "evac":
                    b, what, arg, n = B, s[1]["evac"], s[1]["arg"], s[1]["n"]
                    last = at["tile"] - 1
                    ac = acc[b % 2]
                    if what == "ckv":
                        acc_ready(dve, b, 1, last)
                        dve.tensor_copy(ckv1[:, arg, 1, :], ac[1][:]).then_inc(acc_free[b % 2][1], 1)
                    elif what in BUF:
                        acc_ready(dve, b, 1, last)
                        dve.tensor_copy(BUF[what][:, 1, arg:arg + n], ac[1][:, 0:n]).then_inc(acc_free[b % 2][1], 1)
                    elif what == "obg":
                        skip = G_RANK if arg == 0 else 0
                        for t in range(NT):
                            dve.wait_ge(obg_tanh, 2 * (b - BLOCK["obg", 0]) + t + 1)
                            v = obg[:, t, arg:arg + n - skip]
                            dve.scalar_tensor_tensor(out=v, in0=v, scalar=1.0, in1=ac[t][:, skip:n], op0=ALU.add,
                                                     op1=ALU.mult).then_inc(acc_free[b % 2][t], 1)
                    elif what == "merge":
                        c = slice(arg, arg + 512)
                        if arg == 0:
                            dve.wait_ge(sig_ready, 16)
                        for t in range(NT):
                            acc_ready(dve, b, t, last)
                            dve.tensor_tensor(sigA[:, t, c], sigA[:, t, c], acc[(b - 1) % 2][t][:], ALU.mult).then_inc(
                                acc_free[(b - 1) % 2][t], 1)
                            dve.tensor_tensor(sigB[:, t, c], sigB[:, t, c], ac[t][:], ALU.mult).then_inc(
                                acc_free[b % 2][t], 1)
                    elif what == "silu" or what == "relu2":
                        if what == "relu2":
                            for t in range(NT):
                                block_read(dve, b, t)
                                v = hb[:, arg, t, :]
                                dve.tensor_tensor(v, v, v, ALU.mult).then_inc(h2_ready, 1)
                    elif what == "glu":
                        for t in range(NT):
                            acc_ready(dve, b, t, last)
                            block_read(dve, b - 1, t)
                            dve.tensor_tensor(hb[:, 0, t, :], sil[:, t, :], ac[t][:], ALU.mult).then_inc(acc_free[b % 2][t], 1)
                    elif what == "add":
                        if arg == 0 and s[1]["w"] == "w_out":
                            dve.wait_ge(x_in[1], 16)
                        if arg == 0 and s[1]["w"] == "w_out_2" and s[1]["k0"] == 0:
                            dve.wait_ge(x_renormed, 2)
                        for t in s[2]:
                            acc_ready(dve, b, t, last)
                            v = x_sb[:, t, arg:arg + 512]
                            dve.tensor_tensor(v, v, ac[t][:], ALU.add).then_inc(acc_free[b % 2][t], 1)
                elif s[0] == "scores":
                    g = s[1]
                    kind, t, h, nk = GROUPS[g]
                    sb_, _, _, scale, _ = attention(kind)
                    if g == GROUP0["A"]:
                        dve.wait_ge(bias_in, 16)
                        dve.wait_ge(ckv_kept, 16)
                    if g >= 2:
                        dve.wait_ge(exp_done, g - 1)
                    dve.wait_ge(sc_done, g + 1)
                    dst, src = sb_[:, g % 2, :, 0:nk], psS[:, :, 0:nk]
                    if kind == "C":
                        ins = dve.tensor_scalar(dst, src, scale, None, ALU.mult)
                    else:
                        if kind == "A":
                            mask = bias[:, h:h + 2, SEQ - nk:SEQ]
                        elif kind == "M":
                            mask = cst[:, C_CMASK + P - nk:C_CMASK + P].unsqueeze(1).broadcast_to([P, 2, nk])
                        else:
                            mask = sel[:, t, 0:nk].unsqueeze(1).broadcast_to([P, 2, nk])
                        ins = dve.scalar_tensor_tensor(out=dst, in0=src, scalar=scale, in1=mask, op0=ALU.mult, op1=ALU.add)
                    ins.then_inc(sc_read, 1)
                    w = nk
                    if kind == "A":
                        after(dve.tensor_copy(sb_[:, g % 2, :, nk:nk + 1], sinks_b[:, h:h + 2].unsqueeze(2)))
                        w = nk + 1
                    dve.wait_ge(sc_read, g + 1)
                    dve.tensor_reduce(stat[:, 40 + 2 * (g % 2):42 + 2 * (g % 2)], sb_[:, g % 2, :, 0:w], X, ALU.max,
                                      negate=True).then_inc(max_done, 1)
                elif s[0] == "output":
                    g = s[1]
                    kind, t, h, nk = GROUPS[g]
                    dv = attention(kind)[4]
                    dve.wait_ge(exp_done, g + 1)
                    if g:
                        dve.wait_ge(out_done, g)
                    after(dve.reciprocal(stat[:, 118:120], stat[:, 110 + 2 * (g % 4):112 + 2 * (g % 4)]))
                    dve.wait_ge(out_acc, g + 1)
                    dve.tensor_tensor(outputs(kind, t, h, dv), psO[:, :, 0:dv],
                                      stat[:, 118:120].unsqueeze(2).broadcast_to([P, 2, dv]), ALU.mult).then_inc(out_done, 1)
                elif s[0] == "bias_row":
                    dve.wait_ge(const_in, 16)
                    dve.wait_ge(unit_done, U + 1)
                    dve.tensor_copy(brow[:], bank[U % 2][0:A_HEADS, 0:C_BIASW]).then_inc(unit_free[U % 2], 1)
                elif s[0] == "gate_z":
                    t = s[1]
                    dve.wait_ge(unit_done, U + 1)
                    after(dve.tensor_scalar(enb[:, t, :], bank[U % 2][:], 0.0, None, ALU.min))
                    dve.scalar_tensor_tensor(out=eb[:, t, :], in0=enb[:, t, :], scalar=2.0, in1=bank[U % 2][:],
                                             op0=ALU.mult, op1=ALU.subtract).then_inc(unit_free[U % 2], 1)
                elif s[0] == "state":
                    n, h = s[1], s[2]
                    dve.wait_ge(unit_done, U + 1)
                    if n:
                        units_read(dve, U - 1)
                    for i in range(2):
                        dS = bank[U % 2][:, i * G_VAL:(i + 1) * G_VAL]
                        c = 4 * (h + i) + n
                        if n == 0:
                            ins = dve.tensor_copy(state[:, n, h + i, :], dS)
                        else:
                            ins = dve.scalar_tensor_tensor(out=state[:, n, h + i, :], in0=state[:, n - 1, h + i, :],
                                                           scalar=decay[:, c:c + 1], in1=dS, op0=ALU.mult, op1=ALU.add)
                    ins.then_inc(unit_free[U % 2], 1)
                elif s[0] == "gla_att":
                    t = s[1]
                    dve.wait_ge(unit_done, U + 1)
                    dve.scalar_tensor_tensor(out=attT[:, t], in0=bank[U % 2][:].rearrange("p (h c) -> p h c", h=G_HEADS),
                                             scalar=3e38,
                                             in1=cst[:, C_CAUSAL:C_CAUSAL + P].unsqueeze(1).broadcast_to([P, G_HEADS, P]),
                                             op0=ALU.min, op1=ALU.mult).then_inc(unit_free[U % 2], 1)
                elif s[0] == "gla_out" and s[2] == 2:
                    dve.wait_ge(unit_done, U + 1)
                    dve.tensor_copy(gla[:, s[1], 512:1024], bank[U % 2][:]).then_inc(unit_free[U % 2], 1)
                elif s[0] == "gla_norm":
                    dve.wait_ge(head_squares, 8)
                    rstd(at["root"], 50, 8, G_VAL, by=4.0)
                    for t in range(NT):
                        for h in range(G_HEADS):
                            v = gla[:, t, G_VAL * h:G_VAL * (h + 1)]
                            c = 50 + 4 * t + h
                            ins = dve.scalar_tensor_tensor(out=v, in0=v, scalar=stat[:, c:c + 1], in1=glag[:],
                                                           op0=ALU.mult, op1=ALU.mult)
                        ins.then_inc(ob_normed, 1)
                elif s[0] == "angles":
                    after(dve.tensor_copy(stat[:, 88:90], pos_i[:]))
                    for t in range(NT):
                        ins = dve.tensor_scalar(ang[:, 0, t, :], cst[:, C_FREQ:C_FREQ + 32], stat[:, 88 + t:89 + t], None,
                                                ALU.mult)
                    after(ins)
                    after(dve.tensor_scalar(ang[:, 1], ang[:, 0], 1.0 / TWO_PI, 0.25, ALU.mult, ALU.add))
                    after(dve.tensor_scalar(ang[:, 2], ang[:, 1], ROUND, -ROUND, ALU.add, ALU.add))
                    after(dve.tensor_scalar(ang[:, 1], ang[:, 0], 1.0 / TWO_PI, None, ALU.mult))
                    after(dve.tensor_scalar(ang[:, 3], ang[:, 1], ROUND, -ROUND, ALU.add, ALU.add))
                    for i, shift in ((2, TWO_PI / 4), (3, 0.0)):
                        src = ang[:, 0]
                        for part in TWO_PI_PARTS:
                            after(dve.scalar_tensor_tensor(out=ang[:, 1], in0=ang[:, i], scalar=-part, in1=src,
                                                           op0=ALU.mult, op1=ALU.add))
                            src = ang[:, 1]
                        after(dve.tensor_scalar(ang[:, i], ang[:, 1], shift, PI_BELOW, ALU.add, ALU.min))
                    dve.tensor_scalar(ang[:, 2:4], ang[:, 2:4], -PI_BELOW, None, ALU.max).then_inc(angles_ready, 1)
                elif s[0] == "idx":
                    t, h, q = s[1], s[2], at["nth"]
                    nk = SEQ if t else P
                    units_read(dve, U)
                    for i in range(2):
                        w = idx[:, t, 1088 + h + i:1089 + h + i]
                        sc = score[:, t, 0:nk]
                        if h + i == 0:
                            ins = dve.tensor_scalar(sc, rel[:, q % 2, i, 0:nk], w, None, ALU.mult)
                        else:
                            ins = dve.scalar_tensor_tensor(out=sc, in0=rel[:, q % 2, i, 0:nk], scalar=w, in1=sc,
                                                           op0=ALU.mult, op1=ALU.add)
                        if i == 0:
                            after(ins)
                    ins.then_inc(rel_used, 1)
                    dve.wait_ge(rel_used, q + 1)
                elif s[0] == "topk":
                    t, r = s[1], s[2]
                    nk = SEQ if t else P
                    sc, wk = score[:, t, 0:nk], work[:, t, 0:nk]
                    if r == 0:
                        dve.wait_ge(c_normed, 4)
                        after(dve.tensor_tensor(sc, sc, cst[:, C_CMASK + P - nk:C_CMASK + P], ALU.add))
                    src = sc if r == 0 else wk
                    after(dve.max(stat[:, 80:88], src))
                    after(dve.match_replace(out=wk, in_to_replace=stat[:, 80:88], in_values=src, imm_value=-3e38))
                    if r == TOPK // 8 - 1:
                        after(dve.tensor_scalar(sel[:, t, 0:nk], wk, -2e38, NEG, ALU.is_gt, ALU.mult))
                elif s[0] == "c_norm":
                    dve.wait_ge(c_squares, 4)
                    rstd(at["root"], 66, 2, 512, 256)
                    dve.wait_ge(gcq_in, 32)
                    for i, (c0, n) in enumerate(((0, 512), (512, 256))):
                        for t in range(NT):
                            v = c_sb[:, t, c0:c0 + n]
                            dve.scalar_tensor_tensor(out=v, in0=v, scalar=stat[:, 66 + 2 * i + t:67 + 2 * i + t],
                                                     in1=gcq[:, c0:c0 + n], op0=ALU.mult, op1=ALU.mult).then_inc(c_normed, 1)
                elif s[0] in ("swiglu_up", "relu2_up"):
                    glu, n = s[0] == "swiglu_up", s[2]
                    T0, B, S0 = at["tile"] - 16, B - 2, at["split"] - (0 if glu else 2)
                    with dve.Fori(1, n if glu else n // 2) as r:
                        for k in range(8):
                            lead(T0 + k + LEAD, r * 16)
                        if not glu:
                            for t in range(NT):
                                dve.wait_ge(acc_free[0][t], B // 2 + 1 + r)
                                dve.tensor_tensor(hb[:, 0, t, :], hb[:, 0, t, :], hb[:, 0, t, :], ALU.mult).then_inc(h2_ready, 1)
                        for t in range(NT):
                            dve.wait_ge(unit_hi, S0 - 2 + t + 1 + r * (2 if glu else 4))
                            hidden_lo(t, (r - 1) * 4 if glu else (r - 1) * 8 + 4, t)
                        for k in range(8):
                            lead(T0 + 8 + k + LEAD, r * 16)
                        for t in range(NT):
                            if glu:
                                if t == 0:
                                    dve.wait_ge(acc0_done, B + 2 + r * 2)
                                else:
                                    dve.wait_ge(tile_done, T0 + 16 + r * 16)
                                dve.wait_ge(acc_free[0][t], B // 2 + 1 + r)
                                dve.tensor_tensor(hb[:, 0, t, :], sil[:, t, :], acc[1][t][:], ALU.mult).then_inc(
                                    acc_free[1][t], 1)
                            else:
                                dve.wait_ge(acc_free[1][t], B // 2 + 1 + r)
                                dve.tensor_tensor(hb[:, 1, t, :], hb[:, 1, t, :], hb[:, 1, t, :], ALU.mult).then_inc(h2_ready, 1)
                        if not glu:
                            for t in range(NT):
                                dve.wait_ge(unit_hi, S0 + t + 1 + r * 4)
                                hidden_lo(t, r * 8, t)
                elif s[0] == "down":
                    n, T0 = s[3] // CK, at["tile"]

                    def body(r):
                        for j in range(2):
                            for k in range(n):
                                lead(T0 + n * j + k + LEAD, r * (2 * n))
                            for t in range(NT):
                                if t == 0:
                                    dve.wait_ge(acc0_done, B + j + 1 + r * 2)
                                else:
                                    dve.wait_ge(tile_done, T0 + n * (j + 1) + r * (2 * n))
                                v = x_sb[:, t, bass.ds(r * 1024 + 512 * j, 512)]
                                dve.tensor_tensor(v, v, acc[j][t][:], ALU.add).then_inc(acc_free[j][t], 1)

                    with dve.Fori(0, 2) as r:
                        body(r)


def kernel(**inputs):
    import numpy as _np
    import concourse.bacc as _bacc
    from concourse import mybir as _mybir
    from concourse.bass_utils import run_bass_kernel_spmd as _run

    nc = _bacc.Bacc("TRN2", target_bir_lowering=False, num_devices=1)
    arrays, t_in = {}, {}
    for name, a in [*inputs.items(), ("const", constants())]:
        a = _np.ascontiguousarray(a)
        arrays[f"in_{name}"] = a
        t_in[name] = nc.dram_tensor(f"in_{name}", a.shape, _mybir.dt.from_np(a.dtype), kind="ExternalInput").ap()
        if name.startswith("w_"):
            t_in[name] = t_in[name][0]
    out = nc.dram_tensor("out_0", (1, SEQ, D), _mybir.dt.float32, kind="ExternalOutput").ap()
    build(nc, t_in, out)
    r = _run(nc, [arrays], core_ids=[0])
    return r.results[0]["out_0"]
```

```python
from contextlib import ExitStack

import numpy as np

import concourse.bass as bass
from concourse import mybir

F32 = mybir.dt.float32
F32R = mybir.dt.float32r
I32 = mybir.dt.int32
ALU = mybir.AluOpType
ACT = mybir.ActivationFunctionType
X = mybir.AxisListType.X

P = 128
SEQ, D = 256, 2048
NT = SEQ // P
DC = D // P
EPS = 1e-6
NEG = -1e30
RING = 4
LEAD = RING - 1
CK = 2
COLS = 512

A_HEADS, A_KV, A_DIM = 16, 4, 64
G_HEADS, G_KEY, G_VAL, G_RANK, CHUNK = 4, 128, 256, 16, 64
M_HEADS, M_NOPE, M_ROPE, M_VAL = 8, 128, 64, 128
S_HEADS, S_DIM, S_ROT = 8, 128, 32
I_HEADS, I_DIM, I_ROT = 16, 64, 16
TOPK = 64
TWO_PI = 2 * np.pi
TWO_PI_PARTS = (6.28125, float(np.float16(TWO_PI - 6.28125)), float(TWO_PI - 6.28125 - float(np.float16(TWO_PI - 6.28125))))
PI_BELOW = float(np.nextafter(np.float32(np.pi), np.float32(0)))
ROUND = 1.5 * 2.0 ** 23
C_HEADS, C_DIM = 4, 128
D_FF1, D_FF2 = 5632, 8192

IN1_GLOW = 3 * COLS + 4 * COLS
IN1_OBG = IN1_GLOW + G_RANK
IN1_GA = IN1_OBG + G_HEADS * G_VAL
IN1_GB = IN1_GA + D
IN2_CQ, IN2_CKV, IN2_QD = 0, 512, 832
IN2_QI = IN2_QD + 3 * S_HEADS * S_DIM
IN2_KI = IN2_QI + I_HEADS * I_DIM

C_IDENT, C_TRI, C_REST, C_CAUSAL, C_ZERO, C_CMASK, C_IND, C_FREQ, C_HOT = 0, 128, 256, 384, 512, 640, 768, 770, 802
C_BIASW = 384
C_END = C_HOT + C_BIASW


def constants():
    c = np.zeros((P, C_END), np.float32)
    s, t = np.arange(P)[:, None], np.arange(P)[None, :]
    same = s // CHUNK == t // CHUNK
    c[:, C_IDENT:C_IDENT + P] = s == t
    c[:, C_TRI:C_TRI + P] = (same & (s <= t)) / 16.0
    c[:, C_REST:C_REST + P] = (same & (s > t)) / 16.0
    c[:, C_CAUSAL:C_CAUSAL + P] = same & (s <= t)
    c[:, C_CMASK:C_CMASK + P] = np.where(t // CHUNK <= s // CHUNK, 0.0, NEG)
    c[:, C_IND:C_IND + 2] = (s // CHUNK == np.arange(2)[None]) / 16.0
    half = M_ROPE // 2
    c[:, C_FREQ:C_FREQ + half] = (500000.0 ** (-np.arange(half) / half)).astype(np.float32)
    dist = 255 - np.arange(C_BIASW)
    d = np.maximum(dist, 0)
    large = 16 + (np.log(np.maximum(d, 1).astype(np.float32) / 16) / np.float32(np.log(8.0)) * 16).astype(np.int32)
    bucket = np.where(d < 16, d, np.minimum(large, 31))
    seen = (dist >= 0) & (dist < 128)
    for m in range(C_BIASW):
        if seen[m]:
            c[bucket[m], C_HOT + m] = 1.0
        else:
            c[32, C_HOT + m] = NEG
    return c


TRANSPOSES = {
}


def xp(name, src, col, width, n, dst, idx, mode):
    TRANSPOSES[name] = (src, col, width, n, dst, idx, mode)


for j in range(4):
    xp(f"mem{j}", "mem", 512 * j, 128, 4, "memT", 4 * j, "gain")
    xp(f"u{j}", "u", 512 * j, 128, 4, "xT", 4 * j, "split")
    xp(f"aq{j}", "qkva", 256 * j, 64, 4, "aqT", 4 * j, "act" if j % 2 else "dve")
    xp(f"merged{j}", "merged", 512 * j, 128, 4, "xT", 4 * j, "split")
xp("ak", "qkva", 1024, 64, 4, "akT", 0, "act")
for j in range(2):
    xp(f"ya{j}", "qkva", 512 * j, 128, 4, "yT", 4 * j, "split")
    xp(f"yb{j}", "gla", 512 * j, 128, 4, "yT", 8 + 4 * j, "split")
xp("glow", "glow", 0, 16, 1, "glowT", 0, "dve")
xp("gq", "gla", 0, 128, 4, "gqT", 0, "act")
xp("gk", "gla", 512, 128, 4, "gkT", 0, "act")
for j in range(4):
    xp(f"iq{j}", "idx", 256 * j, 64, 4, "iqT", 4 * j, "act" if j % 2 else "dve")
xp("ik", "idx", 1024, 64, 1, "ikT", 0, "act")
xp("cq", "c", 0, 128, 4, "cT", 0, "split")
xp("ckv", "c", 512, 128, 2, "cT", 4, "split")
xp("kr", "c", 768, 64, 1, "krT", 0, "act")
for j in range(2):
    xp(f"mq{j}", "mq", j, 128, 4, "mqT", 4 * j, "act")
    xp(f"mr{j}", "mr", j, 64, 4, "mrT", 4 * j, "dve")
    xp(f"mk{j}", "mkv", j, 128, 4, "mkT", 4 * j, "act")
    xp(f"a{j}", "mout", 512 * j, 128, 4, "xT", 4 * j, "split")
    xp(f"sq{j}", "dsa", 512 * j, 128, 4, "sqT", 4 * j, "act")
    xp(f"sk{j}", "dsa", 1024 + 512 * j, 128, 4, "skT", 4 * j, "dve")
    xp(f"s{j}", "dsa", 512 * j, 128, 4, "xT", 8 + 4 * j, "split")
xp("ck", "ckv", 0, 128, 4, "ckT", 0, "act")
xp("cqq", "cqo", 0, 128, 4, "cqT", 0, "dve")
for name, src, i0 in (("hid0", "hb0", 0), ("glu6", "hb0", 20), ("glu5", "hb0", 16), ("relu6", "hb1", 20),
                      ("relu4", "hb1", 12)):
    xp(name, src, 0, 128, 4, "hT", i0, "split")
xp("co", "cqo", 0, 128, 4, "coT", 0, "split")


def attention_groups():
    groups = []
    for kind, heads in (("A", A_HEADS), ("M", M_HEADS), ("S", S_HEADS), ("C", C_HEADS)):
        for t in range(NT):
            for h in range(0, heads, 2):
                groups.append((kind, t, h, SEQ if t or kind == "C" else P))
    return groups


GROUPS = attention_groups()
GROUP0 = {k: [g[0] for g in GROUPS].index(k) for k in "AMSC"}
NGROUPS = {k: sum(g[0] == k for g in GROUPS) for k in "AMSC"}


def attention_slots(kind):
    a, n = GROUP0[kind], NGROUPS[kind]
    slots = []
    for j in range(n + 2):
        slot = [("scores", a + j)] if j < n else []
        if 0 <= j - 1 < n:
            slot.append(("probs_T", a + j - 1))
        if 0 <= j - 2 < n:
            slot.append(("output", a + j - 2))
        slots.append(slot)
    return slots


NORM_OF = {"w_k_cross_2": 0, "w_v_cross_2": 0, "w_in": 1, "w_ffn_gate": 2, "w_ffn_up": 2, "w_in_2": 4, "w_q_cross_2": 5,
           "w_up_2": 6}


def make_block(w, k0, kc, c0, n, lhs, l0, evac, arg=0, needs=()):
    return dict(w=w, k0=k0, kc=kc, c0=c0, n=n, lhs=lhs, l0=l0, evac=evac, arg=arg, needs=needs, norm=NORM_OF.get(w))


def tiles_in(b):
    return -(-b["kc"] // CK)


def block_steps(*args, **kw):
    b = make_block(*args, **kw)
    return [("tile", b, k) for k in range(tiles_in(b))] + [("evac", b, (0, 1))]


def both(name):
    return [("T", name, t) for t in range(NT)]


def weave(dense, slots, every):
    out, slots, n = [], list(slots), 0
    for s in dense:
        out.append(s)
        if s[0] == "tile":
            n += 1
            if n % every == 0 and slots:
                out += slots.pop(0)
    for s in slots:
        out += s
    return out


def pieces_of_norm(n, j, ts=(0, 1)):
    return [s for t in ts for s in (("ssq", n, j, t), ("gained", n, j, t))]


def after_tiles(steps, placed):
    return [x for s in steps for x in [s] + (placed.get(s[2], []) if s[0] == "tile" else [])]


def into_norm(n, blocks, turns):
    out = []
    for j, b in enumerate(blocks):
        if b is None:
            continue
        steps = [("tile", b, k) for k in range(tiles_in(b))] + [("evac", b, (0, 1))]
        out += after_tiles(steps, {k: both(f"u{i}") for (jj, k), i in turns.items() if jj == j}) + pieces_of_norm(n, j)
    return out


def out_of_norm(n, first, whole=None):
    tiles = [("tile", first, k) for k in range(whole or tiles_in(first))]
    return after_tiles(tiles, {0: [("rstd", n, 0), ("rstd", n, 1)], 2: both("u3")}) + (
        [] if whole else [("evac", first, (0, 1))])


U_NEEDS = ("u0", "u1", "u2", "u3")


def schedule():
    S = []
    mem_k = make_block("w_k_cross_2", 0, DC, 0, 512, "memT", 0, "ckv", 0, ("mem0", "mem1", "mem2", "mem3"))
    S += [("gain_T",)]
    for t in range(NT):
        T = [("T", f"mem{j}", t) for j in range(4)]
        part = [("part", mem_k, i, t) for i in range(LEAD)]
        lead = ("lead",)
        S += [T[0], T[1], lead, T[2], part[0], lead, T[3], part[1], lead, part[2]]
        S += [("ssq", 0, j, t) for j in range(4)] + [("rstd", 0, t)]
    mem_dense = [("tile", mem_k, i) for i in range(LEAD, DC // CK)] + [("evac", mem_k, (0, 1))]
    mem_dense += block_steps("w_v_cross_2", 0, DC, 0, 512, "memT", 0, "ckv", 1)
    xs = [[], pieces_of_norm(1, 0) + pieces_of_norm(1, 1),
          pieces_of_norm(1, 2) + pieces_of_norm(1, 3), [("rstd", 1, 0), ("rstd", 1, 1)]]
    xu = [(j, t) for j in range(4) for t in range(NT)]
    xs += [[("T", f"u{j}", t)] for j, t in xu]
    S += weave(mem_dense, xs, 1)
    S += [("keep_ckv",), ("bias_row",), ("half_rms",)]
    w = lambda c0, n, evac, arg=0, needs=(): block_steps("w_in", 0, DC, c0, n, "xT", 0, evac, arg, needs)
    S += w(0, 512, "qkva", 0, U_NEEDS) + w(512, 512, "qkva", 512) + w(1024, 512, "qkva", 1024)
    dense = []
    for j in range(4):
        dense += w(1536 + 512 * j, 512, "gla", 512 * j)
    for c0, n, skip in ((0, 384, G_RANK), (384, 320, 0), (704, 320, 0)):
        dense += w(IN1_OBG + c0 - skip, n + skip, "obg", c0)
    for j in range(4):
        dense += w(IN1_GA + 512 * j, 512, "sigA", 512 * j)
    for j in range(4):
        dense += w(IN1_GB + 512 * j, 512, "sigB", 512 * j)
    slots = [both(f"aq{j}") for j in range(4)] + [both("ak")] + attention_slots("A")
    slots += [both("glow"), [("gate_z", 0), ("gate_z", 1)], [], [("gate_log",)], [], [("gate_sum", 0)], [("gate_sum", 1)],
              [("gate_rest", 0)], [("gate_rest", 1)], [], [("gate_decay",)], both("gq"), both("gk")]
    slots += [[("state", n, h)] for n in range(3) for h in (0, 2)]
    slots += [[("gla_att", t)] for t in range(NT)]
    slots += [[("gla_out", t, h)] for t in range(NT) for h in (0, 2)]
    slots += [[("gla_norm",)], [], both("ya0"), both("ya1"), both("yb0"), both("yb1")]
    S += weave(dense, slots, 2)
    for j in range(4):
        S += block_steps("w_proj_a", 0, 8, 512 * j, 512, "yT", 0, "gate_a", 512 * j, ("ya0", "ya1") if not j else ())
        S += weave(block_steps("w_proj_b", 0, 8, 512 * j, 512, "yT", 8, "merge", 512 * j, ("yb0", "yb1") if not j else ()),
                   [[], both(f"merged{j - 1}")] if j else [], 1)
    S += [("load_x",), ("gain", 2)]
    merged = tuple(f"merged{j}" for j in range(4))
    blocks = [make_block("w_out", 0, DC, 512 * j, 512, "xT", 0, "add", 512 * j, () if j else merged) for j in range(4)]
    sums_ = into_norm(2, blocks, {(3, 2): 0, (3, 4): 1, (3, 6): 2})
    S += sums_[:3] + both("merged3") + sums_[3:]
    gate = lambda j, needs=(): ("w_ffn_gate", 0, DC, 512 * j, 512, "xT", 0, "silu", 0, needs)
    up = lambda j: block_steps("w_ffn_up", 0, DC, 512 * j, 512, "xT", 0, "glu", 0)
    S += out_of_norm(2, make_block(*gate(0, U_NEEDS)))
    S += [("gain", 3), ("gain", 4)] + up(0) + [("swiglu_up", 0, 6)] + both("glu6") + [("down", "w_ffn_down", 0, 24)]
    S += block_steps(*gate(6)) + up(6) + [("swiglu_up", 6, 5)]
    blocks = [make_block("w_ffn_down", 24, 20, 512 * j, 512, "hT", 0, "add", 512 * j, () if j else hidden_needs("glu5", 5))
              for j in range(4)]
    sums_ = into_norm(3, blocks, {(3, 2): 0, (3, 4): 1, (3, 6): 2})
    S += sums_[:2] + both("glu5") + sums_[2:]
    w = lambda c0, n, evac, arg=0: block_steps("w_in_2", 0, DC, c0, n, "xT", 0, evac, arg)
    S += out_of_norm(3, make_block("w_in_2", 0, DC, IN2_CQ, 416, "xT", 0, "c", 0, U_NEEDS))
    S += weave(w(IN2_CQ + 416, 416, "c", 416), [[("norm_x", j, t)] for j in range(4) for t in range(NT)], 1)
    S += [("c_squares",)]
    dense = []
    for j in range(3):
        dense += w(IN2_QI + 368 * j, 368, "idx", 368 * j)
    S += weave(dense, [[], [("c_norm",)], [("angles",)], [("rope", "kr")], both("cq"), both("ckv"), both("kr")], 2)
    S += [("rope", "idx")]
    dense = []
    for j in range(4):
        dense += block_steps("w_qb_2", 0, 4, 384 * j, 384, "cT", 0, "mq", 384 * j, () if j else ("cq",))
    for j in range(4):
        dense += block_steps("w_kvb_2", 0, 2, 512 * j, 512, "cT", 4, "mkv", 512 * j, () if j else ("ckv",))
    dense += [("rope", "mq")]
    for j in range(5):
        dense += w(IN2_QD + 512 * j, 512, "dsa", 512 * j)
        dense += [("rope", "dsa")] * (j == 3)
    slots = [[], [], []] + [both(f"iq{j}") for j in range(4)] + [both("ik")]
    slots += [[("idx", t, h)] for t in range(NT) for h in range(0, I_HEADS, 2)]
    slots += [both(f"mk{j}") for j in range(2)] + [both(f"mq{j}") for j in range(2)] + [both(f"mr{j}") for j in range(2)]
    rounds = [("topk", t, r) for t in range(NT) for r in range(TOPK // 8)]
    slots += [m + rounds[2 * i:2 * i + 2] for i, m in enumerate(attention_slots("M"))]
    S += weave(dense, slots, 1)
    S += weave(w(IN2_QD + 2560, 512, "dsa", 2560), [[], [], [], [], both("a0"), both("a1")], 1)
    dense = []
    for j in range(4):
        dense += block_steps("w_out_2", 0, 8, 512 * j, 512, "xT", 0, "add", 512 * j, () if j else ("a0", "a1"))
    slots = [both("sq0") + both("sk0")] + [both("sq1") + both("sk1")] + attention_slots("S") + [both("s0"), both("s1")]
    S += weave(dense, slots, 1)
    S += [("gain", 5)]
    S += into_norm(5, [make_block("w_out_2", 8, 8, 512 * j, 512, "xT", 8, "add", 512 * j, () if j else ("s0", "s1"))
                       for j in range(4)], {(2, 1): 0, (2, 3): 1, (3, 2): 2})
    q = make_block("w_q_cross_2", 0, DC, 0, 512, "xT", 0, "cqo", 0, U_NEEDS)
    S += out_of_norm(5, q, whole=5)
    S += both("ck") + [("gain", 6)]
    g = GROUP0["C"]
    S += [("part", q, k, 0) for k in range(5, 8)] + [("evac", q, (0,)), ("part", q, 5, 1), ("T", "cqq", 0), ("lead",)]
    S += [("part", q, 6, 1), ("scores", g), ("part", q, 7, 1), ("evac", q, (1,)), ("scores", g + 1), ("T", "cqq", 1)]
    S += [("probs_T", g), ("scores", g + 2), ("output", g), ("probs_T", g + 1), ("scores", g + 3)]
    S += [("output", g + 1), ("lead",), ("probs_T", g + 2), ("T", "co", 0), ("lead",), ("output", g + 2),
          ("probs_T", g + 3)]
    o = make_block("w_o_cross_2", 0, 4, 0, 512, "coT", 0, "add", 0, ("co",))
    S += [("part", o, 0, 0), ("output", g + 3), ("part", o, 1, 0), ("T", "co", 1), ("part", o, 0, 1), ("part", o, 1, 1)]
    S += [("lead",), ("lead",), ("evac", o, (0, 1))] + pieces_of_norm(6, 0)
    blocks = [None] + [make_block("w_o_cross_2", 0, 4, 512 * j, 512, "coT", 0, "add", 512 * j) for j in (1, 2, 3)]
    S += into_norm(6, blocks, {(2, 0): 0, (3, 0): 1, (3, 1): 2})
    relu = lambda j, needs=(): ("w_up_2", 0, DC, 512 * j, 512, "xT", 0, "relu2", j % 2, needs)
    S += out_of_norm(6, make_block(*relu(0, U_NEEDS)))
    S += [("gain", 7)] + block_steps(*relu(1)) + both("hid0")
    S += [("relu2_up", 0, 6)] + both("relu6") + [("down", "w_down_2", 0, 24)]
    S += block_steps(*relu(6)) + block_steps(*relu(7)) + both("hid0")
    S += [("relu2_up", 6, 6)] + both("relu6") + [("down", "w_down_2", 24, 24)]
    S += block_steps(*relu(12)) + block_steps(*relu(13)) + both("hid0") + [("relu2_up", 12, 4)]
    for j in range(3):
        b = block_steps("w_down_2", 48, 16, 512 * j, 512, "hT", 0, "add", 512 * j, hidden_needs("relu4", 4) if not j else ())
        S += (weave(b, [[], both("relu4")], 1) if not j else b) + pieces_of_norm(7, j)
    last = make_block("w_down_2", 48, 16, 1536, 512, "hT", 0, "add", 1536)
    S += [("tile", last, k) for k in range(8 - LEAD)]
    for t in range(NT):
        S += [("part", last, k, t) for k in range(8 - LEAD, 8)]
        S += [("evac", last, (t,)), ("ssq", 7, 3, t), ("rstd", 7, t)]
        S += [s for j in (0, 2, 1, 3) for s in (("scaled", 7, j, t), ("store", 7, j, t))]
    return number(S)


def hidden_needs(name, n):
    return (None,) * (n - 1) + (name,)


UNIT_STEPS = ("T", "probs_T", "bias_row", "gate_z", "gate_sum", "gate_rest", "gate_decay", "state", "gla_att",
              "gla_out", "idx")


def number(steps):
    out, shapes, wrote, seen = [], {}, {}, {}
    c = dict(tile=0, lead=0, block=0, unit=0, split=0, hidden=0, squares=0, root=0, gained=0)
    ahead = 0
    for s in steps:
        kind = s[0]
        at = dict(c, nth=seen.get(kind, 0))
        seen[kind] = at["nth"] + 1
        if kind in ("tile", "part"):
            b, k = s[1], s[2]
            name = b["needs"][CK * k // 4] if b["needs"] and k % 2 == 0 else None
            ts = (0, 1) if kind == "tile" else (s[3],)
            at["need"] = max(wrote[name, t] for t in ts) if name else None
            at["last"] = k == tiles_in(b) - 1
            c["lead"] += kind == "tile"
            if ts == (0,):
                at["tile"] += ahead
                ahead += 1
            else:
                ahead -= kind == "part"
                c["tile"] += 1
            shapes[at["tile"]] = (min(CK, b["kc"] - CK * k), b["n"])
        elif kind == "lead":
            c["lead"] += 1
        elif kind == "evac":
            what = s[1]["evac"]
            at["root"] = wrote.get(("root", 1))
            for t in s[2]:
                wrote[what, s[1]["arg"], t] = c["block"]
            c["block"] += 1 in s[2]
            c["hidden"] += 2 * (what == "relu2")
        elif kind == "ssq":
            at["block"] = wrote.get(("add", 512 * s[2], s[3]))
            c["squares"] += 2 if s[1] == 3 else 1
        elif kind == "gained":
            at["block"] = wrote.get(("add", 512 * s[2], s[3]))
            at["u3"] = wrote.get(("u3", 1))
            wrote["norm"] = s[1]
            wrote["gained", s[2], s[3]] = c["gained"]
            c["gained"] += 1
        elif kind in ("rstd", "c_norm", "gla_norm"):
            wrote["root", s[-1]] = c["root"]
            c["root"] += 1
        elif kind == "scaled":
            at["root"] = wrote["root", s[3]]
            at["gained"] = wrote.get(("gained", s[2], s[3]))
        elif kind in UNIT_STEPS:
            if kind == "probs_T":
                wrote["probs", s[1]] = c["unit"]
            if kind == "T":
                if TRANSPOSES[s[1]][0] == "u":
                    j = TRANSPOSES[s[1]][1] // 512
                    at["gained"] = wrote.get(("gained", j, s[2]))
                    at["norm"] = wrote["norm"]
                wrote[s[1], s[2]] = c["unit"]
                if s[1] == "u3":
                    wrote[f"u3 of {wrote['norm']}"] = c["unit"]
                c["split"] += TRANSPOSES[s[1]][6] in ("split", "gain")
            c["unit"] += 1
        elif kind in ("swiglu_up", "relu2_up"):
            n = s[2] - 1 if kind == "swiglu_up" else s[2] // 2 - 1
            assert c["unit"] % 2 == 0 and c["block"] % 2 == 0, s
            per = 2 if kind == "swiglu_up" else 4
            assert c["lead"] == c["tile"] + LEAD
            c["tile"] += 16 * n
            c["lead"] += 16 * n
            c["block"] += 2 * n
            c["unit"] += per * n
            c["split"] += per * n
            c["hidden"] += 4 * n if per == 4 else 0
            assert c["tile"] % RING == 0
        elif kind == "down":
            assert c["block"] % 2 == 0
            assert c["lead"] == c["tile"] + LEAD
            c["tile"] += 4 * (s[3] // CK)
            c["lead"] += 4 * (s[3] // CK)
            c["block"] += 4
        out.append((s, at))
    return out, c["tile"], wrote, shapes


def build(nc, t_in, out):
    SCHEDULE, TILES, LAST_UNIT, SHAPES = schedule()
    ctx = ExitStack()
    with ctx:
        def sem(name):
            return ctx.enter_context(nc.semaphore(name))

        base = (nc.sbuf_base + 63) // 64 * 64
        top = [base]

        def put(name, shape, dt=F32, at=None):
            size = 4 * int(np.prod(shape[1:]))
            off = top[0] if at is None else at
            if at is None:
                top[0] += (size + 63) // 64 * 64
            assert off + size <= nc.sbuf_usable_end, (name, off + size - nc.sbuf_usable_end)
            return nc.alloc_sbuf_tensor_at(name, shape, dt, offset=off)

        w_raw = put("w_raw", [P, RING, CK, COLS])
        w_hi = put("w_hi", [P, RING, CK, COLS], F32R)
        w_lo = put("w_lo", [P, RING, CK, COLS], F32R)
        xT = (put("xT_hi", [P, DC, SEQ], F32R), put("xT_lo", [P, DC, SEQ], F32R))
        cst = put("cst", [P, C_END])
        stat = put("stat", [P, 128])
        sums = put("sums", [P, 9, NT, 4])
        unwanted = put("unwanted", [P, 512], mybir.dt.bfloat16)
        X0 = top[0]
        x_sb = put("x_sb", [P, NT, D])
        ARENA = top[0]
        K = 1024

        def arena(name, shape, at, dt=F32):
            return put(name, shape, dt, at=ARENA + int(at * K))

        sigB = put("sigB", [P, NT, D], at=X0)
        sigA = arena("sigA", [P, NT, D], 0)
        obg = arena("obg", [P, NT, 1024], 16)
        gain_rows = arena("gain_rows", [DC, P], 16)
        gain_T = arena("gain_T", [P, DC], 17)
        gain_x = arena("gain_x", [P, D], 40)
        qkva = arena("qkva", [P, NT, 1536], 24)
        gla = arena("gla", [P, NT, 2048], 36)
        SH = 52
        mem_sb = arena("mem_sb", [P, NT, D], 24)
        u_x = arena("u_x", [P, NT, D], 24)
        ckv1 = arena("ckv1", [P, 2, NT, 512], SH + 32)
        memT = (arena("memT_hi", [P, DC, SEQ], SH, F32R), arena("memT_lo", [P, DC, SEQ], SH + 16, F32R))
        bias = arena("bias", [P, A_HEADS, SEQ], SH)
        aqT = arena("aqT", [64, A_HEADS, SEQ], SH + 16)
        akT = arena("akT", [64, A_KV, SEQ], SH + 32)
        s1 = arena("s1", [P, 2, 2, 258], SH + 36)
        p1 = arena("p1", [P, 2, 2, 258], SH + 40.25)
        pT1 = arena("pT1", [P, 2, 4, P], SH + 44.5)
        la = arena("la", [P, NT, 512], SH)
        eb = arena("eb", [P, NT, 512], SH + 4)
        enb = arena("enb", [P, NT, 512], SH + 8)
        kst = arena("kst", [P, NT, 512], SH + 12)
        gqT = arena("gqT", [P, G_HEADS, SEQ], SH + 16)
        gkT = arena("gkT", [P, G_HEADS, SEQ], SH + 20)
        attT = arena("attT", [P, NT, G_HEADS, P], SH + 24)
        state = arena("state", [P, 3, G_HEADS, G_VAL], SH + 28)
        glowT = arena("glowT", [32, 1, SEQ], SH + 40)
        decay = arena("decay", [P, 16], SH + 41)
        yT = (arena("yT_hi", [P, DC, SEQ], SH, F32R), arena("yT_lo", [P, DC, SEQ], SH + 16, F32R))
        SH2 = SH + 49
        gup = arena("gup", [17, 512], SH2)
        glow = arena("glow", [P, NT, G_RANK], SH2 + 2)
        glag = arena("glag", [P, G_VAL], SH2 + 2.125)
        sinks_b = arena("sinks_b", [P, A_HEADS], SH2 + 3.125)
        relb = arena("relb", [33, A_HEADS], SH2 + 3.1875)
        brow = arena("brow", [A_HEADS, C_BIASW], SH + 46)
        hT = (arena("hT_hi", [P, 24, SEQ], 0, F32R), arena("hT_lo", [P, 24, SEQ], 24, F32R))
        hb = arena("hb", [P, 2, NT, 512], 48)
        sil = arena("sil", [P, NT, 512], 56)
        u = arena("u", [P, NT, D], 64)
        gain = arena("gain", [P, D], 96)
        gain4 = arena("gain4", [P, D], 80)
        idx = arena("idx", [P, NT, 1104], 0)
        iqT = arena("iqT", [64, I_HEADS, SEQ], 9)
        ikT = arena("ikT", [64, 1, SEQ], 25)
        mqT = arena("mqT", [P, M_HEADS, SEQ], 0)
        mrT = arena("mrT", [64, M_HEADS, SEQ], 8)
        mkT = arena("mkT", [P, M_HEADS, SEQ], 16)
        krT = arena("krT", [64, 1, SEQ], 26)
        sqT = arena("sqT", [P, S_HEADS, SEQ], 0)
        skT = arena("skT", [P, S_HEADS, SEQ], 8)
        mq = arena("mq", [P, NT, 1536], 27)
        mout = arena("mout", [P, NT, 1024], 27)
        mkv = arena("mkv", [P, NT, 2048], 39)
        s2 = arena("s2", [P, 2, 2, 258], 55)
        p2 = arena("p2", [P, 2, 2, 258], 59.25)
        pT2 = arena("pT2", [P, 2, 4, P], 63.5)
        rel = arena("rel", [P, 2, 2, SEQ], 55)
        work = arena("work", [P, 2, SEQ], 101)
        dsa = arena("dsa", [P, NT, 3072], 68)
        c_sb = arena("c_sb", [P, NT, 832], 68)
        cT = (arena("cT_hi", [P, 6, SEQ], 75, F32R), arena("cT_lo", [P, 6, SEQ], 81, F32R))
        gcq = arena("gcq", [P, 768], 101)
        SM = 92
        score = arena("score", [P, NT, SEQ], SM)
        sel = arena("sel", [P, NT, SEQ], SM)
        trig = arena("trig", [P, 2, NT, 32], 94)
        rtmp = arena("rtmp", [P, 4, 256], 96)
        pos_i = arena("pos_i", [P, NT], 104.25, I32)
        ang = arena("ang", [P, 4, NT, 32], 100)
        ckv = arena("ckv", [P, 2, NT, 512], 0)
        ckT = arena("ckT", [P, C_HEADS, SEQ], 8)
        cqo = arena("cqo", [P, NT, 512], 12)
        cqT = arena("cqT", [P, C_HEADS, SEQ], 16)
        coT = (arena("coT_hi", [P, 4, SEQ], 20, F32R), arena("coT_lo", [P, 4, SEQ], 24, F32R))

        acc = [[ctx.enter_context(nc.psum_tensor(f"acc{p}{t}", [P, 512], F32)) for t in range(NT)] for p in range(2)]
        bank = [ctx.enter_context(nc.psum_tensor(f"unit{i}", [P, 512], F32)) for i in range(2)]
        psS = ctx.enter_context(nc.psum_tensor("psS", [P, 2, 256], F32))
        psO = ctx.enter_context(nc.psum_tensor("psO", [P, 2, 256], F32))

        keep_kv = nc.dram_tensor("keep_kv", [2, SEQ, 512], F32, kind="Internal")
        keep_bias = nc.dram_tensor("keep_bias", [A_HEADS, P, C_BIASW], F32, kind="Internal")

        w_landed = [sem(f"w_landed{i}") for i in range(RING)]
        hi_split = sem("hi_split")
        lo_split = sem("lo_split")
        tile_done = sem("tile_done")
        acc0_done = sem("acc0_done")
        acc_free = [[sem(f"acc{p}{t}_free") for t in range(NT)] for p in range(2)]
        unit_done = sem("unit_done")
        unit_hi = sem("unit_hi")
        unit_free = [sem(f"unit{i}_free") for i in range(2)]
        sc_done = sem("scores_done")
        sc_read = sem("scores_read")
        max_done = sem("max_done")
        exp_done = sem("exp_done")
        out_acc = sem("attention_out_acc")
        out_done = sem("attention_out_done")
        ident_in, const_in = sem("ident_in"), sem("const_in")
        mem0_in = [sem(f"mem0_in{j}") for j in range(4)]
        mem1_in = sem("mem1_in")
        gain_mem_in = sem("gain_mem_in")
        x_in = [sem("x_in"), sem("x_again_in")]
        gain_in = [None] + [sem(f"gain_in{i}") for i in range(1, 8)]
        small_in, gcq_in = sem("small_in"), sem("gcq_in")
        ckv_kept, ckv_back = sem("ckv_kept"), sem("ckv_back")
        bias_kept, bias_in = sem("bias_kept"), sem("bias_in")
        out_stored = sem("out_stored")
        gain_turned, gain_T_ready = sem("gain_turned"), sem("gain_T_ready")
        squares = sem("squares")
        gained = sem("gained")
        x_gained = sem("x_gained")
        mean_ready, rstd_ready = sem("mean_ready"), sem("rstd_ready")
        half_known = sem("half_known")
        x_normed = sem("x_normed")
        result_ready = [sem("result01_ready"), sem("result23_ready")]
        z_exp, z_log = sem("z_exp"), sem("z_log")
        la_ready = sem("la_ready")
        decay_exp = sem("decay_exp")
        gq_ready, gk_ready = sem("gq_ready"), sem("gk_ready")
        obg_tanh = sem("obg_tanh")
        head_squares = sem("head_squares")
        ob_normed, ob_ready = sem("ob_normed"), sem("ob_ready")
        sig_ready, merged_ready = sem("sig_ready"), sem("merged_ready")
        h2_ready = sem("h2_ready")
        angles_ready, trig_ready = sem("angles_ready"), sem("trig_ready")
        roped = {k: sem(f"roped_{k}") for k in ("idx", "kr", "mq", "dsa")}
        c_squares, c_normed = sem("c_squares"), sem("c_normed")
        rel_used = sem("rel_used")
        dve_step, pool_step = sem("dve_step"), sem("pool_step")

        def acc_ready(eng, b, t, last_tile):
            if t == 0:
                eng.wait_ge(acc0_done, b + 1)
            else:
                eng.wait_ge(tile_done, last_tile + 1)

        def block_read(eng, b, t):
            eng.wait_ge(acc_free[b % 2][t], b // 2 + 1)

        def units_read(eng, n):
            for i in range(2):
                if n >= i:
                    eng.wait_ge(unit_free[i], (n - i) // 2 + 1)

        def over_rms(norm, t):
            if norm is None:
                return 1.0
            c = 13 + 2 * t if norm == 4 else 4 * norm + t
            return stat[:, c:c + 1]

        def norm_known(eng, norm, root):
            if norm is not None:
                eng.wait_ge(rstd_ready, root + 1)

        BLOCK = {}
        for s, at in SCHEDULE:
            if s[0] == "evac":
                BLOCK[s[1]["evac"], s[1]["arg"]] = at["block"]

        BUF = dict(qkva=qkva, gla=gla, glow=glow, idx=idx, c=c_sb, mq=mq, mkv=mkv, dsa=dsa, cqo=cqo)
        SRC = dict(mem=mem_sb, qkva=qkva, gla=gla, glow=glow, merged=sigA, idx=idx, c=c_sb, mout=mout, dsa=dsa, cqo=cqo)
        LHS = dict(memT=memT, xT=xT, yT=yT, cT=cT, coT=coT, hT=hT)
        DST = dict(aqT=aqT, akT=akT, glowT=glowT, gqT=gqT, gkT=gkT, iqT=iqT, ikT=ikT, krT=krT, mqT=mqT, mrT=mrT,
                   mkT=mkT, sqT=sqT, skT=skT, ckT=ckT, cqT=cqT)
        SRC.update(hb0=hb[:, 0], hb1=hb[:, 1])

        def piece(name, i, t, norm):
            src, col, width, _, _, _, _ = TRANSPOSES[name]
            if src == "u":
                return (u_x if norm == 1 else u)[:, t, col + i * width:col + (i + 1) * width]
            if src == "mq":
                return mq[:, t, (4 * col + i) * 192:(4 * col + i) * 192 + 128]
            if src == "mr":
                return mq[:, t, (4 * col + i) * 192 + 128:(4 * col + i + 1) * 192]
            if src == "mkv":
                return mkv[:, t, (4 * col + i) * 256:(4 * col + i) * 256 + 128]
            if src == "ckv":
                return ckv[:, 0, t, i * 128:(i + 1) * 128]
            return SRC[src][:, t, col + i * width:col + (i + 1) * width]

        def heads_view(which, t):
            if which == "idx":
                return idx[:, t, 0:1088].rearrange("p (h d) -> p h d", d=I_DIM), I_ROT // 2
            if which == "kr":
                return c_sb[:, t, 768:832].rearrange("p (h d) -> p h d", d=M_ROPE), M_ROPE // 2
            if which == "mq":
                return mq[:, t, :].rearrange("p (h d) -> p h d", d=M_NOPE + M_ROPE)[:, :, M_NOPE:], M_ROPE // 2
            return dsa[:, t, 0:2048].rearrange("p (h d) -> p h d", d=S_DIM), S_ROT // 2

        def attention(kind):
            if kind == "A":
                return s1, p1, pT1, A_DIM ** -0.5, A_DIM
            scale = {"M": (M_NOPE + M_ROPE) ** -0.5, "S": S_DIM ** -0.5, "C": C_DIM ** -0.5}[kind]
            return s2, p2, pT2, scale, 128

        def values(kind, kt, h):
            if kind == "A":
                return qkva[:, kt, 1280 + (h // 4) * 64:1280 + (h // 4 + 1) * 64]
            if kind == "M":
                return mkv[:, kt, h * 256 + 128:(h + 1) * 256]
            if kind == "S":
                return dsa[:, kt, 2048 + h * 128:2048 + (h + 1) * 128]
            return ckv[:, 1, kt, h * 128:(h + 1) * 128]

        def outputs(kind, t, h, dv):
            to = {"A": qkva, "M": mout, "S": dsa, "C": cqo}[kind]
            return to[:, t, h * dv:(h + 2) * dv].rearrange("p (i v) -> p i v", i=2)

        ident = cst[:, C_IDENT:C_IDENT + P]
        block = ctx.enter_context(nc.Block())

        @block.sync
        def _(sp):
            tok = lambda a: a.rearrange("(t p) d -> p t d", p=P)
            sp.dma_start(cst[:, C_IDENT:C_IDENT + P], t_in["const"][:, C_IDENT:C_IDENT + P]).then_inc(ident_in, 16)
            for j in range(4):
                c = slice(512 * j, 512 * j + 512)
                sp.dma_start(mem_sb[:, 0, c], t_in["mem_2"][0, 0:P, c]).then_inc(mem0_in[j], 16)

            def tile(slot, free, src, kc, n):
                if free is not None:
                    sp.wait_ge(lo_split, free)
                sp.dma_start(w_raw[:, slot, 0:kc, 0:n], src.rearrange("(c p) n -> p c n", p=P)).then_inc(
                    w_landed[slot], 16)

            for s, at in SCHEDULE:
                i = at["tile"]
                if s[0] == "tile" or s[0] == "part" and s[3] == 0:
                    b, k = s[1], s[2]
                    kc = min(CK, b["kc"] - k * CK)
                    if i == LEAD:
                        sp.dma_start(mem_sb[:, 1], t_in["mem_2"][0, P:2 * P]).then_inc(mem1_in, 16)
                    r = (b["k0"] + k * CK) * P
                    tile(i % RING, i - RING + 1 if i >= RING else None,
                         t_in[b["w"]][r:r + kc * P, b["c0"]:b["c0"] + b["n"]], kc, b["n"])
                    if i == RING - 1:
                        sp.dma_start(x_sb[:], tok(t_in["x"][0])).then_inc(x_in[0], 16)
                        sp.dma_start(cst[:, P:], t_in["const"][:, P:]).then_inc(const_in, 16)
                elif s[0] == "swiglu_up":
                    with sp.Fori(1, s[2]) as r:
                        for j, w in enumerate(("w_ffn_gate", "w_ffn_up")):
                            for k in range(8):
                                tile(k % RING, i - 16 + 8 * j + k - RING + 1 + r * 16,
                                     t_in[w][2 * k * P:(2 * k + 2) * P, bass.ds(r * 512 + s[1] * 512, 512)], 2, 512)
                elif s[0] == "relu2_up":
                    with sp.Fori(1, s[2] // 2) as r:
                        for j in range(2):
                            for k in range(8):
                                tile(k % RING, i - 16 + 8 * j + k - RING + 1 + r * 16,
                                     t_in["w_up_2"][2 * k * P:(2 * k + 2) * P,
                                                    bass.ds(r * 1024 + (s[1] + j) * 512, 512)], 2, 512)
                elif s[0] == "down":
                    n = s[3] // CK
                    with sp.Fori(0, 2) as r:
                        for j in range(2):
                            for k in range(n):
                                o = i + n * j + k
                                row = (s[2] + 2 * k) * P
                                tile(o % RING, o - RING + 1 + r * (2 * n),
                                     t_in[s[1]][row:row + 2 * P, bass.ds(r * 1024 + j * 512, 512)], 2, 512)
                elif s[0] == "store":
                    _, n, j, t = s
                    c = slice(512 * j, 512 * j + 512)
                    sp.wait_ge(result_ready[j // 2], 2 * t + j % 2 + 1)
                    sp.dma_start(out[0, t * P:(t + 1) * P, c], u[:, t, c]).then_inc(out_stored, 16)
            sp.wait_ge(out_stored, 16 * NT * 4)

        @block.gpsimd
        def _(pool):
            steps = [0]

            def after(ins):
                steps[0] += 1
                ins.then_inc(pool_step, 1)
                pool.wait_ge(pool_step, steps[0])

            def rows(dst, vec, sm):
                pool.dma_start(dst, vec.unsqueeze(0).broadcast_to([P, vec.shape[0]])).then_inc(sm, 16)

            after(pool.memset(relb[32:33, :], 1.0))
            pool.dma_start(relb[0:32, :], t_in["rel_bias"]).then_inc(small_in, 16)
            pool.dma_start(gup[0:G_RANK, :], t_in["w_gate_up"]).then_inc(small_in, 16)
            pool.dma_start(gup[G_RANK:G_RANK + 1, :], t_in["b_gate"]).then_inc(small_in, 16)
            rows(glag[:], t_in["gla_norm_g"][0], small_in)
            rows(sinks_b[:], t_in["sinks"][0], small_in)
            for t in range(NT):
                pool.dma_start(pos_i[:, t:t + 1], t_in["positions_2"][0, t * P:(t + 1) * P].unsqueeze(1)).then_inc(small_in, 16)

            roots = [0]

            after(pool.memset(stat[:, 100:108], -0.5))

            def rstd(c0, n):
                roots[0] += 1
                pool.wait_ge(mean_ready, roots[0])
                v = stat[:, c0:c0 + n]
                pool.tensor_tensor(v, v, stat[:, 100:100 + n], ALU.pow).then_inc(rstd_ready, 1)

            def rotate(which, t):
                v, half = heads_view(which, t)
                n = v.shape[1]
                x1, x2 = v[:, :, 0:half], v[:, :, half:2 * half]
                cos, sin = (trig[:, i, t, 0:32:32 // half].unsqueeze(1).broadcast_to([P, n, half]) for i in range(2))
                tmp = [rtmp[:, i, 0:n * half].rearrange("p (h f) -> p h f", f=half) for i in range(4)]
                for dst, a, b in zip(tmp, (x1, x2, x2, x1), (cos, sin, cos, sin)):
                    last = pool.tensor_tensor(dst, a, b, ALU.mult)
                after(last)
                pool.tensor_tensor(x1, tmp[0], tmp[1], ALU.subtract)
                last = pool.tensor_tensor(x2, tmp[2], tmp[3], ALU.add)
                last.then_inc(roped[which], 1)
                pool.wait_ge(roped[which], t + 1)

            for s, at in SCHEDULE:
                if s[0] == "ssq" and s[1:] == (0, 0, 0):
                    pool.wait_ge(mem1_in, 16)
                    rows(gain_x[:], t_in["norm_mix_g"][0], gain_in[1])
                elif s[0] == "gain":
                    n = s[1]
                    if n == 2:
                        pool.wait_ge(merged_ready, 8)
                    elif n != 4:
                        pool.wait_ge(gained, at["gained"])
                    if n == 5:
                        pool.wait_ge(c_normed, 4)
                        pool.wait_ge(out_done, GROUP0["S"] + NGROUPS["S"])
                        pool.dma_start(ckv[:], keep_kv.ap().rearrange("a (t p) d -> p a t d", p=P)).then_inc(ckv_back, 16)
                    name = ["", "", "norm_ffn_g", "norm_final_g", "g_mix_2", "g_cross_2", "g_mlp_2", "g_final_2"][n]
                    vec = t_in[name]
                    rows((gain4 if n == 4 else gain)[:], vec if len(vec.shape) == 1 else vec[0], gain_in[n])
                elif s[0] == "gained":
                    _, n, j, t = s
                    c = slice(512 * j, 512 * j + 512)
                    if (j, t) == (0, 0):
                        pool.wait_ge(gain_in[n + (n == 3)], 16)
                        if n == 1:
                            pool.wait_ge(x_in[0], 16)
                            pool.wait_ge(squares, 8)
                            pool.wait_ge(unit_done, LAST_UNIT["mem3", 1] + 1)
                        elif n > 2:
                            pool.wait_ge(unit_done, at["u3"] + 1)
                    if n == 3:
                        pool.wait_ge(squares, at["squares"])
                    elif n > 1:
                        block_read(pool, at["block"], t)
                    dst, g = (u_x, gain_x) if n == 1 else (u, gain4 if n == 3 else gain)
                    src = u if n == 3 else x_sb
                    pool.tensor_tensor(dst[:, t, c], src[:, t, c], g[:, c], ALU.mult).then_inc(gained, 1)
                elif s[0] == "rstd":
                    n, t = s[1], s[2]
                    if n == 3:
                        rstd(12 + 2 * t, 2)
                    else:
                        rstd(4 * n + t, 1)
                elif s[0] == "c_norm":
                    rstd(66, 4)
                elif s[0] == "keep_ckv":
                    for i in range(2):
                        for t in range(NT):
                            block_read(pool, BLOCK["ckv", i], t)
                    pool.dma_start(keep_kv.ap().rearrange("a (t p) d -> p a t d", p=P), ckv1[:]).then_inc(ckv_kept, 16)
                elif s[0] == "bias_row":
                    units_read(pool, at["unit"])
                    pool.dma_start(keep_bias[:, :, :], brow[:].unsqueeze(1).broadcast_to([A_HEADS, P, C_BIASW])).then_inc(
                        bias_kept, 16)
                    pool.wait_ge(bias_kept, 16)
                    pool.dma_start(bias[:], bass.AP(tensor=keep_bias, offset=P - 1,
                                                    ap=[[C_BIASW - 1, P], [P * C_BIASW, A_HEADS], [1, SEQ]])).then_inc(bias_in, 16)
                elif s[0] == "gate_log":
                    for t in range(NT):
                        pool.wait_ge(z_log, t + 1)
                        pool.tensor_tensor(la[:, t, :], enb[:, t, :], eb[:, t, :], ALU.subtract).then_inc(la_ready, 1)
                elif s[0] == "gate_sum":
                    t = s[1]
                    pool.wait_ge(decay_exp, t + 1)
                    pool.tensor_tensor(gla[:, t, 0:512], gla[:, t, 0:512], eb[:, t, :], ALU.mult).then_inc(gq_ready, 1)
                elif s[0] == "gate_rest":
                    t = s[1]
                    units_read(pool, at["unit"])
                    after(pool.tensor_tensor(kst[:, t, :], kst[:, t, :], gla[:, t, 512:1024], ALU.mult))
                    pool.tensor_tensor(gla[:, t, 512:1024], gla[:, t, 512:1024], enb[:, t, :], ALU.mult).then_inc(
                        gk_ready, 1)
                elif s[0] == "evac" and s[1]["evac"] in ("sigA", "sigB"):
                    buf, col = (sigA if s[1]["evac"] == "sigA" else sigB), s[1]["arg"]
                    for t in range(NT):
                        block_read(pool, at["block"], t)
                        v = buf[:, t, col:col + 512]
                        pool.tensor_scalar(v, v, 0.5, 0.5, ALU.mult, ALU.add).then_inc(sig_ready, 1)
                elif s[0] == "gla_norm":
                    rstd(50, 8)
                    for t in range(NT):
                        pool.wait_ge(ob_normed, t + 1)
                        v = gla[:, t, 0:1024]
                        pool.tensor_tensor(v, v, obg[:, t, :], ALU.mult).then_inc(ob_ready, 1)
                elif s[0] == "evac" and s[1]["evac"] == "merge":
                    j = s[1]["arg"] // 512
                    for t in range(NT):
                        block_read(pool, at["block"] - 1, t)
                        block_read(pool, at["block"], t)
                        c = slice(512 * j, 512 * j + 512)
                        pool.tensor_tensor(sigA[:, t, c], sigA[:, t, c], sigB[:, t, c], ALU.add).then_inc(
                            merged_ready, 1)
                elif s[0] == "load_x":
                    pool.wait_ge(merged_ready, 8)
                    pool.dma_start(x_sb[:], t_in["x"][0].rearrange("(t p) d -> p t d", p=P)).then_inc(x_in[1], 16)
                elif s[0] == "c_squares":
                    pool.wait_ge(x_normed, 8)
                    rows(gcq[:, 0:512], t_in["g_cq_2"][0], gcq_in)
                    rows(gcq[:, 512:768], t_in["g_ckv_2"][0], gcq_in)
                elif s[0] == "angles":
                    pool.wait_ge(trig_ready, 2)
                elif s[0] == "rope":
                    which = s[1]
                    blocks = {"idx": [("idx", 368 * j) for j in range(3)], "kr": [("c", 416)],
                              "mq": [("mq", 384 * j) for j in range(4)],
                              "dsa": [("dsa", 512 * j) for j in range(4)]}[which]
                    for t in range(NT):
                        for b in blocks:
                            block_read(pool, BLOCK[b], t)
                        rotate(which, t)

        @block.scalar
        def _(act):
            act.dma_start(gain_rows[:], t_in["g_mem_2"][0].rearrange("(c p) -> c p", p=P)).then_inc(gain_mem_in, 16)

            def split_hi(i, slot, uses, free, kc=CK, n=COLS):
                act.wait_ge(w_landed[slot], uses)
                if free is not None:
                    act.wait_ge(tile_done, free)
                act.activation(w_hi[:, slot, 0:kc, 0:n], w_raw[:, slot, 0:kc, 0:n], ACT.Copy).then_inc(hi_split, 1)

            def lead(i, more=0):
                if isinstance(more, int) and i + more >= TILES:
                    return
                static = isinstance(more, int) and more == 0
                split_hi(i, i % RING, 16 * (i // RING + 1) + (0 if static else more * (16 // RING)),
                         (i - RING + 1 if i >= RING else None) if static else i - RING + 1 + more,
                         *(SHAPES.get(i, (CK, COLS)) if static else (CK, COLS)))

            def hi(bk, w, n, dst, i0, t):
                act.activation(dst[0][0:w, i0:i0 + n, t * P:(t + 1) * P],
                               bank[bk][0:w, 0:n * P].rearrange("p (c q) -> p c q", q=P), ACT.Copy).then_inc(unit_hi, 1)

            def hidden_hi(c, t, unit):
                act.wait_ge(unit_done, unit)
                act.activation(hT[0][:, bass.ds(c, 4), t * P:(t + 1) * P],
                               bank[t][:].rearrange("p (c q) -> p c q", q=P), ACT.Copy).then_inc(unit_hi, 1)

            for s, at in SCHEDULE:
                U, B = at["unit"], at["block"]
                if s[0] == "lead" or s[0] == "tile":
                    lead(at["lead"])
                elif s[0] == "scaled" and s[2] < 2:
                    _, n, j, t = s
                    c = slice(512 * j, 512 * j + 512)
                    act.wait_ge(rstd_ready, at["root"] + 1)
                    act.wait_ge(gained, at["gained"] + 1)
                    act.activation(u[:, t, c], u[:, t, c], ACT.Copy, scale=stat[:, 4 * n + t:4 * n + t + 1]).then_inc(
                        result_ready[0], 1)
                elif s[0] == "gain_T":
                    act.wait_ge(gain_turned, 1)
                    act.activation(gain_T[:], psO[:, 0, 0:DC], ACT.Copy).then_inc(gain_T_ready, 1)
                elif s[0] == "ssq":
                    _, n, j, t = s
                    c = slice(512 * j, 512 * j + 512)
                    if n == 0:
                        act.wait_ge(mem1_in if t else mem0_in[j], 16)
                    elif n == 1:
                        act.wait_ge(x_in[0], 16)
                    else:
                        block_read(act, at["block"], t)
                    src = mem_sb if n == 0 else x_sb
                    if at["squares"]:
                        act.wait_ge(squares, at["squares"])
                    act.activation(unwanted[:], src[:, t, c], ACT.Square, accum_out=sums[:, n, t, j:j + 1]).then_inc(squares, 1)
                    if n == 3:
                        act.wait_ge(x_gained, 2 * j + t + 1)
                        act.wait_ge(squares, at["squares"] + 1)
                        act.activation(unwanted[:], u[:, t, c], ACT.Square, accum_out=sums[:, 8, t, j:j + 1]).then_inc(
                            squares, 1)
                elif s[0] == "T":
                    name, t = s[1], s[2]
                    _, _, w, n, dst, i0, mode = TRANSPOSES[name]
                    if mode == "split":
                        act.wait_ge(unit_done, U + 1)
                        hi(U % 2, w, n, LHS[dst], i0, t)
                    elif mode == "gain":
                        act.wait_ge(gain_T_ready, 1)
                        act.wait_ge(unit_done, U + 1)
                        for c in range(i0, i0 + n):
                            ins = act.activation(memT[0][:, c, t * P:(t + 1) * P], bank[U % 2][:, (c - i0) * P:(c - i0 + 1) * P],
                                                 ACT.Copy, scale=gain_T[:, c:c + 1])
                        ins.then_inc(unit_hi, 1)
                    elif mode == "act":
                        if name == "ak" and t == 0:
                            act.wait_ge(ckv_kept, 16)
                        act.wait_ge(unit_done, U + 1)
                        scale = G_KEY ** -0.5 if name == "gq" else 1.0
                        act.activation(DST[dst][0:w, i0:i0 + n, t * P:(t + 1) * P],
                                       bank[U % 2][0:w, 0:n * P].rearrange("p (c q) -> p c q", q=P),
                                       ACT.Copy, scale=scale).then_inc(unit_free[U % 2], 1)
                elif s[0] == "evac":
                    b, what, arg, n = B, s[1]["evac"], s[1]["arg"], s[1]["n"]
                    last = at["tile"] - 1
                    ac = acc[b % 2]
                    if what == "ckv":
                        acc_ready(act, b, 0, last)
                        norm_known(act, 0, 1)
                        act.activation(ckv1[:, arg, 0, :], ac[0][:], ACT.Copy, scale=over_rms(0, 0)).then_inc(
                            acc_free[b % 2][0], 1)
                    elif what in BUF and 0 in s[2]:
                        if what == "gla" and arg == 0:
                            act.wait_ge(gained, 8)
                        acc_ready(act, b, 0, last)
                        norm_known(act, s[1]["norm"], at["root"])
                        act.activation(BUF[what][:, 0, arg:arg + n], ac[0][:, 0:n], ACT.Copy,
                                       scale=over_rms(s[1]["norm"], 0)).then_inc(acc_free[b % 2][0], 1)
                    elif what == "obg":
                        skip = G_RANK if arg == 0 else 0
                        for t in range(NT):
                            acc_ready(act, b, t, last)
                            if skip:
                                act.activation(glow[:, t, :], ac[t][:, 0:skip], ACT.Copy, scale=over_rms(1, t))
                            act.wait_ge(half_known, 1)
                            act.activation(obg[:, t, arg:arg + n - skip], ac[t][:, skip:n], ACT.Tanh,
                                           scale=stat[:, 6 + t:7 + t]).then_inc(
                                obg_tanh, 1)
                    elif what in ("silu", "relu2"):
                        for t in range(NT):
                            acc_ready(act, b, t, last)
                            norm_known(act, s[1]["norm"], at["root"])
                            act.activation(sil[:, t, :] if what == "silu" else hb[:, arg, t, :], ac[t][:],
                                           ACT.Silu if what == "silu" else ACT.Relu,
                                           scale=over_rms(s[1]["norm"], t)).then_inc(acc_free[b % 2][t], 1)
                    elif what in ("sigA", "sigB"):
                        buf = sigA if what == "sigA" else sigB
                        for t in range(NT):
                            acc_ready(act, b, t, last)
                            act.activation(buf[:, t, arg:arg + 512], ac[t][:], ACT.Tanh, scale=stat[:, 6 + t:7 + t]).then_inc(
                                acc_free[b % 2][t], 1)
                elif s[0] == "scores":
                    g = s[1]
                    kind, t, h, nk = GROUPS[g]
                    _, pb, _, _, _ = attention(kind)
                    sb_ = attention(kind)[0]
                    act.wait_ge(max_done, g + 1)
                    w = nk + 1 if kind == "A" else nk
                    for i in range(2):
                        ins = act.activation(pb[:, g % 2, i, 0:w], sb_[:, g % 2, i, 0:w], ACT.Exp,
                                             bias=stat[:, 40 + 2 * (g % 2) + i:41 + 2 * (g % 2) + i],
                                             accum_out=stat[:, 110 + 2 * (g % 4) + i:111 + 2 * (g % 4) + i])
                    ins.then_inc(exp_done, 1)
                elif s[0] == "probs_T":
                    g = s[1]
                    kind, t, h, nk = GROUPS[g]
                    n = 2 * nk // P
                    act.wait_ge(unit_done, U + 1)
                    act.activation(attention(kind)[2][:, g % 2, 0:n, :],
                                   bank[U % 2][:, 0:n * P].rearrange("p (c q) -> p c q", q=P), ACT.Copy).then_inc(
                        unit_free[U % 2], 1)
                elif s[0] == "gate_z":
                    t = s[1]
                    units_read(act, U)
                    act.activation(eb[:, t, :], eb[:, t, :], ACT.Exp).then_inc(z_exp, 1)
                elif s[0] == "gate_log":
                    for t in range(NT):
                        act.wait_ge(z_exp, t + 1)
                        act.activation(eb[:, t, :], eb[:, t, :], ACT.Ln, bias=1.0).then_inc(z_log, 1)
                elif s[0] == "gate_sum":
                    t = s[1]
                    act.wait_ge(unit_done, U + 1)
                    act.activation(eb[:, t, :], bank[U % 2][:], ACT.Exp).then_inc(decay_exp, 1)
                    act.activation(enb[:, t, :], bank[U % 2][:], ACT.Exp, scale=-1.0).then_inc(unit_free[U % 2], 1)
                elif s[0] == "gate_rest":
                    t = s[1]
                    act.wait_ge(unit_done, U + 1)
                    ins = act.activation(kst[:, t, :], bank[U % 2][:], ACT.Exp)
                    ins.then_inc(unit_free[U % 2], 1)
                elif s[0] == "gate_decay":
                    act.wait_ge(unit_done, U + 1)
                    act.activation(decay[:], bank[U % 2][:, 0:16], ACT.Exp).then_inc(unit_free[U % 2], 1)
                elif s[0] == "gla_out" and s[2] == 0:
                    act.wait_ge(unit_done, U + 1)
                    act.activation(gla[:, s[1], 0:512], bank[U % 2][:], ACT.Copy).then_inc(unit_free[U % 2], 1)
                elif s[0] == "gla_norm":
                    units_read(act, U - 1)
                    for t in range(NT):
                        for h in range(G_HEADS):
                            junk = (eb, enb)[t][:, h // 2, 256 * (h % 2):256 * (h % 2) + 256]
                            act.activation(junk, gla[:, t, 256 * h:256 * h + 256], ACT.Square,
                                           accum_out=stat[:, 50 + 4 * t + h:51 + 4 * t + h]).then_inc(head_squares, 1)
                elif s[0] == "angles":
                    act.wait_ge(angles_ready, 1)
                    for i in range(2):
                        act.activation(trig[:, i], ang[:, 2 + i], ACT.Sin).then_inc(trig_ready, 1)
                elif s[0] == "idx":
                    t, n = s[1], at["nth"]
                    nk = SEQ if t else P
                    if n >= 2:
                        act.wait_ge(rel_used, n - 1)
                    act.wait_ge(unit_done, U + 1)
                    act.activation(rel[:, n % 2, :, 0:nk], bank[U % 2][:].rearrange("p (i k) -> p i k", i=2)[:, :, 0:nk],
                                   ACT.Relu, scale=1.0 / 32).then_inc(unit_free[U % 2], 1)
                elif s[0] == "c_squares":
                    for i, (c0, n) in enumerate(((0, 512), (512, 256))):
                        for t in range(NT):
                            block_read(act, BLOCK["c", 0], t)
                            block_read(act, BLOCK["c", 416], t)
                            act.activation(mkv[:, t, c0:c0 + n], c_sb[:, t, c0:c0 + n], ACT.Square,
                                           accum_out=stat[:, 66 + 2 * i + t:67 + 2 * i + t]).then_inc(c_squares, 1)
                elif s[0] in ("swiglu_up", "relu2_up"):
                    glu = s[0] == "swiglu_up"
                    T0, B = at["tile"] - 16, B - 2
                    U -= 0 if glu else 2

                    with act.Fori(1, s[2] if glu else s[2] // 2) as r:
                        m = r * 16
                        for k in range(8):
                            lead(T0 + k + LEAD, m)
                        for t in range(NT):
                            if t == 0:
                                act.wait_ge(acc0_done, B + 1 + r * 2)
                            else:
                                act.wait_ge(tile_done, T0 + 8 + m)
                            if glu:
                                act.wait_ge(acc_free[1][t], B // 2 + r)
                            act.activation(sil[:, t, :] if glu else hb[:, 0, t, :], acc[0][t][:],
                                           ACT.Silu if glu else ACT.Relu,
                                           scale=over_rms(2 if glu else 6, t)).then_inc(acc_free[0][t], 1)
                        for t in range(NT):
                            hidden_hi((r - 1) * 4 if glu else (r - 1) * 8 + 4, t, U - 2 + t + 1 + r * (2 if glu else 4))
                        for k in range(8):
                            lead(T0 + 8 + k + LEAD, m)
                        if not glu:
                            for t in range(NT):
                                if t == 0:
                                    act.wait_ge(acc0_done, B + 2 + r * 2)
                                else:
                                    act.wait_ge(tile_done, T0 + 16 + m)
                                act.activation(hb[:, 1, t, :], acc[1][t][:], ACT.Relu,
                                               scale=over_rms(6, t)).then_inc(acc_free[1][t], 1)
                            for t in range(NT):
                                hidden_hi(r * 8, t, U + t + 1 + r * 4)
                elif s[0] == "down":
                    n, T0 = s[3] // CK, at["tile"]
                    with act.Fori(0, 2) as r:
                        for k in range(2 * n):
                            lead(T0 + k + LEAD, r * (2 * n))

        @block.tensor
        def _(pe):
            def products(ac, b_lhs, l0, kc, slot, n, t, start, stop):
                hi_, lo_ = b_lhs
                for c in range(kc):
                    for m, (a, w) in enumerate(((hi_, w_hi), (lo_, w_hi), (hi_, w_lo))):
                        ins = pe.matmul(ac[t][:, 0:n], a[:, l0 + c, t * P:(t + 1) * P], w[:, slot, c, 0:n],
                                        start=start and c == 0 and m == 0, stop=stop and c == kc - 1 and m == 2)
                return ins

            def dense_tile(i, p, free, lhs, l0, kc, n, first, last, more=0, ts=(0, 1)):
                pe.wait_ge(lo_split, i + 1 + more)
                for t in ts:
                    if first and free is not None:
                        pe.wait_ge(acc_free[p][t], free)
                    ins = products(acc[p], lhs, l0, kc, i % RING, n, t, first, last)
                    if t == 0 and last:
                        ins.then_inc(acc0_done, 1)
                if 1 in ts:
                    ins.then_inc(tile_done, 1)

            def bank_free(n):
                if n >= 2:
                    pe.wait_ge(unit_free[n % 2], n // 2)

            def transpose_pieces(bk, pieces, w):
                for i, a in enumerate(pieces):
                    ins = pe.transpose(bank[bk][0:w, i * P:(i + 1) * P], a, ident)
                ins.then_inc(unit_done, 1)

            def source_ready(name, t, at):
                src, col, w, _, _, _, _ = TRANSPOSES[name]
                if src == "mem":
                    pe.wait_ge(mem1_in if t else mem0_in[col // 512], 16)
                elif src == "u":
                    pe.wait_ge(gained, at["gained"] + 1)
                elif name[:3] == "glu":
                    block_read(pe, at["block"] - 1, t)
                elif name == "hid0" or name[:4] == "relu":
                    pe.wait_ge(h2_ready, at["hidden"] - (4 if name == "hid0" else 2) + t + 1)
                elif name[:2] in ("aq", "ak"):
                    block_read(pe, BLOCK["qkva", col // 512 * 512], t)
                elif name == "glow":
                    block_read(pe, BLOCK["obg", 0], t)
                elif name in ("gq", "gk"):
                    pe.wait_ge(gq_ready if name == "gq" else gk_ready, t + 1)
                elif name[:2] == "ya":
                    pe.wait_ge(out_done, GROUP0["A"] + NGROUPS["A"])
                elif name[:2] == "yb":
                    pe.wait_ge(ob_ready, t + 1)
                elif src == "merged":
                    pe.wait_ge(merged_ready, 2 * (col // 512) + t + 1)
                elif src == "idx":
                    pe.wait_ge(roped["idx"], t + 1)
                elif name in ("cq", "ckv"):
                    pe.wait_ge(c_normed, t + 1 if name == "cq" else t + 3)
                elif name == "kr":
                    pe.wait_ge(roped["kr"], t + 1)
                elif src == "mq":
                    for j in range(4):
                        block_read(pe, BLOCK["mq", 384 * j], t)
                    pe.wait_ge(roped["mq"], t + 1)
                elif src == "mr":
                    pe.wait_ge(roped["mq"], t + 1)
                elif src == "mkv":
                    for j in range(4):
                        block_read(pe, BLOCK["mkv", 512 * j], t)
                elif src == "mout":
                    pe.wait_ge(out_done, GROUP0["M"] + NGROUPS["M"])
                elif name[:2] in ("sq", "sk"):
                    pe.wait_ge(roped["dsa"], t + 1)
                elif name in ("s0", "s1"):
                    pe.wait_ge(out_done, GROUP0["S"] + NGROUPS["S"])
                elif name == "ck":
                    pe.wait_ge(ckv_back, 16)
                elif name == "cqq":
                    block_read(pe, BLOCK["cqo", 0], t)
                elif name == "co":
                    pe.wait_ge(out_done, GROUP0["C"] + C_HEADS // 2 * (t + 1))

            def score_terms(kind, h, t):
                q = slice(t * P, (t + 1) * P)
                if kind == "A":
                    return [(aqT[:, h, q], akT[:, h // 4])]
                if kind == "M":
                    return [(mqT[:, h, q], mkT[:, h]), (mrT[:, h, q], krT[:, 0])]
                if kind == "S":
                    return [(sqT[:, h, q], skT[:, h])]
                return [(cqT[:, h, q], ckT[:, h])]

            LAST_T = {"A": "ak", "M": "mr1", "S": "sk1", "C": "cqq"}
            for s, at in SCHEDULE:
                U, B = at["unit"], at["block"]
                if s[0] in UNIT_STEPS:
                    bank_free(U)
                    ps = bank[U % 2]
                if s[0] in ("tile", "part"):
                    b, k = s[1], s[2]
                    if at["need"] is not None:
                        units_read(pe, at["need"])
                    dense_tile(at["tile"], B % 2, B // 2 if B >= 2 else None, LHS[b["lhs"]], b["l0"] + CK * k,
                               min(CK, b["kc"] - CK * k), b["n"], k == 0, at["last"], ts=(0, 1) if s[0] == "tile" else s[3:])
                elif s[0] == "gain_T":
                    pe.wait_ge(ident_in, 16)
                    pe.wait_ge(gain_mem_in, 16)
                    pe.transpose(psO[:, 0, 0:DC], gain_rows[:], ident[0:DC, 0:DC]).then_inc(gain_turned, 1)
                elif s[0] == "T":
                    name, t = s[1], s[2]
                    _, _, w, n, _, _, _ = TRANSPOSES[name]
                    source_ready(name, t, at)
                    transpose_pieces(U % 2, [piece(name, i, t, at.get("norm")) for i in range(n)], w)
                elif s[0] == "scores":
                    g = s[1]
                    kind, t, h, nk = GROUPS[g]
                    if g == GROUP0[kind] and kind != "C":
                        units_read(pe, LAST_UNIT[LAST_T[kind], 1])
                    if kind == "C" and (g - GROUP0["C"]) % (C_HEADS // 2) == 0:
                        units_read(pe, LAST_UNIT["cqq", t])
                    if g:
                        pe.wait_ge(sc_read, g)
                    for i in range(2):
                        terms = score_terms(kind, h + i, t)
                        for m, (q, k) in enumerate(terms):
                            ins = pe.matmul(psS[:, i, 0:nk], q, k[:, 0:nk], start=m == 0, stop=m == len(terms) - 1)
                    ins.then_inc(sc_done, 1)
                elif s[0] == "probs_T":
                    g = s[1]
                    kind, t, h, nk = GROUPS[g]
                    pb = attention(kind)[1]
                    pe.wait_ge(exp_done, g + 1)
                    transpose_pieces(U % 2, [pb[:, g % 2, i, c * P:(c + 1) * P] for i in range(2) for c in range(nk // P)], P)
                elif s[0] == "output":
                    g = s[1]
                    kind, t, h, nk = GROUPS[g]
                    _, _, pT, _, dv = attention(kind)
                    units_read(pe, LAST_UNIT["probs", g])
                    if g:
                        pe.wait_ge(out_done, g)
                    if kind == "M" and g == GROUP0["M"]:
                        for j in range(4):
                            for tt in range(NT):
                                block_read(pe, BLOCK["mkv", 512 * j], tt)
                    if kind == "S" and g == GROUP0["S"]:
                        for j in range(6):
                            for tt in range(NT):
                                block_read(pe, BLOCK["dsa", 512 * j], tt)
                    for i in range(2):
                        for kt in range(nk // P):
                            ins = pe.matmul(psO[:, i, 0:dv], pT[:, g % 2, i * (nk // P) + kt, :], values(kind, kt, h + i),
                                            start=kt == 0, stop=kt == nk // P - 1)
                    ins.then_inc(out_acc, 1)
                elif s[0] == "bias_row":
                    pe.wait_ge(small_in, 16 * 7)
                    pe.wait_ge(const_in, 16)
                    pe.matmul(ps[0:A_HEADS, 0:C_BIASW], relb[0:33, :], cst[0:33, C_HOT:C_HOT + C_BIASW],
                              start=True, stop=True).then_inc(unit_done, 1)
                elif s[0] == "gate_z":
                    t = s[1]
                    units_read(pe, LAST_UNIT["glow", 1])
                    pe.matmul(ps[:], glowT[0:17, 0, t * P:(t + 1) * P], gup[0:17, :], start=True, stop=True).then_inc(
                        unit_done, 1)
                elif s[0] in ("gate_sum", "gate_rest"):
                    t = s[1]
                    c0 = C_TRI if s[0] == "gate_sum" else C_REST
                    pe.wait_ge(la_ready, t + 1)
                    pe.matmul(ps[:], cst[:, c0:c0 + P], la[:, t, :], start=True, stop=True).then_inc(unit_done, 1)
                elif s[0] == "gate_decay":
                    for t in range(NT):
                        for h in range(G_HEADS):
                            c0 = 4 * h + 2 * t
                            ins = pe.matmul(ps[:, c0:c0 + 2], la[:, t, h * P:(h + 1) * P], cst[:, C_IND:C_IND + 2],
                                            start=True, stop=True)
                    ins.then_inc(unit_done, 1)
                elif s[0] == "state":
                    n, h = s[1], s[2]
                    t, r = n // 2, CHUNK * (n % 2)
                    pe.wait_ge(gk_ready, t + 1)
                    for i in range(2):
                        v0 = 1024 + (h + i) * G_VAL
                        ins = pe.matmul(ps[:, i * G_VAL:(i + 1) * G_VAL], kst[r:r + CHUNK, t, (h + i) * P:(h + i + 1) * P],
                                        gla[r:r + CHUNK, t, v0:v0 + G_VAL], start=True, stop=True)
                    ins.then_inc(unit_done, 1)
                elif s[0] == "gla_att":
                    t = s[1]
                    units_read(pe, LAST_UNIT["gk", 1])
                    q = slice(t * P, (t + 1) * P)
                    for h in range(G_HEADS):
                        ins = pe.matmul(ps[:, h * P:(h + 1) * P], gkT[:, h, q], gqT[:, h, q], start=True, stop=True)
                    ins.then_inc(unit_done, 1)
                elif s[0] == "gla_out":
                    t, h = s[1], s[2]
                    if s[1:] == (0, 0):
                        units_read(pe, U - 1)
                    for i in range(2):
                        o = slice(i * G_VAL, (i + 1) * G_VAL)
                        v0 = 1024 + (h + i) * G_VAL
                        ins = pe.matmul(ps[:, o], attT[:, t, h + i, :], gla[:, t, v0:v0 + G_VAL], start=True, stop=False,
                                        skip_group_check=True)
                        for j in range(2):
                            n = 2 * t + j
                            if n:
                                r = slice(CHUNK * j, CHUNK * (j + 1))
                                ins = pe.matmul(ps[r, o], gqT[:, h + i, t * P + CHUNK * j:t * P + CHUNK * (j + 1)],
                                                state[:, n - 1, h + i, :], start=False, stop=j == 1, skip_group_check=True)
                    ins.then_inc(unit_done, 1)
                elif s[0] == "idx":
                    t, h = s[1], s[2]
                    nk = SEQ if t else P
                    if at["nth"] == 0:
                        units_read(pe, LAST_UNIT["ik", 1])
                    for i in range(2):
                        ins = pe.matmul(ps[:, i * SEQ:i * SEQ + nk], iqT[:, h + i, t * P:(t + 1) * P], ikT[:, 0, 0:nk],
                                        start=True, stop=True)
                    ins.then_inc(unit_done, 1)
                elif s[0] in ("swiglu_up", "relu2_up"):
                    glu, n = s[0] == "swiglu_up", s[2]
                    T0, B, h = at["tile"] - 16, B - 2, at["hidden"] - 4
                    U -= 0 if glu else 2

                    def pieces(j, t):
                        return [hb[:, j, t, c * P:(c + 1) * P] for c in range(4)]

                    with pe.Fori(1, n if glu else n // 2) as r:
                        for j in range(2):
                            for k in range(8):
                                dense_tile(T0 + 8 * j + k, j, B // 2 + r, xT, CK * k, CK, 512, k == 0, k == 7, r * 16)
                            for t in range(NT):
                                if j == 0:
                                    pe.wait_ge(unit_free[t], U // 2 + (r - 1 if glu else 2 * r - 1))
                                    if glu:
                                        pe.wait_ge(acc_free[1][t], B // 2 + r)
                                    else:
                                        pe.wait_ge(h2_ready, h - 2 + t + 1 + r * 4)
                                    transpose_pieces(t, pieces(0 if glu else 1, t), P)
                                elif not glu:
                                    pe.wait_ge(unit_free[t], U // 2 + 2 * r)
                                    pe.wait_ge(h2_ready, h + t + 1 + r * 4)
                                    transpose_pieces(t, pieces(0, t), P)
                elif s[0] == "down":
                    n, T0 = s[3] // CK, at["tile"]

                    with pe.Fori(0, 2) as r:
                        for j in range(2):
                            for k in range(n):
                                if j == 0 and k in (0, n - 2):
                                    for t in range(NT):
                                        pe.wait_ge(unit_free[t], U // 2 - (k == 0))
                                dense_tile(T0 + n * j + k, j, B // 2 + r, hT, CK * k, CK, 512, k == 0, k == n - 1,
                                           r * (2 * n))

        @block.vector
        def _(dve):
            steps = [0]

            def after(ins):
                steps[0] += 1
                ins.then_inc(dve_step, 1)
                dve.wait_ge(dve_step, steps[0])

            def lead(i, more=0):
                if isinstance(more, int) and i + more >= TILES:
                    return
                dve.wait_ge(hi_split, i + 1 + more)
                slot = i % RING
                kc, n = SHAPES.get(i, (CK, COLS)) if isinstance(more, int) and more == 0 else (CK, COLS)
                dve.tensor_tensor(w_lo[:, slot, 0:kc, 0:n], w_raw[:, slot, 0:kc, 0:n],
                                  w_hi[:, slot, 0:kc, 0:n].bitcast(F32), ALU.subtract).then_inc(
                    lo_split, 1)

            def lo(bk, w, n, dst, i0, t):
                dve.tensor_tensor(dst[1][0:w, i0:i0 + n, t * P:(t + 1) * P],
                                  bank[bk][0:w, 0:n * P].rearrange("p (c q) -> p c q", q=P),
                                  dst[0][0:w, i0:i0 + n, t * P:(t + 1) * P].bitcast(F32), ALU.subtract).then_inc(
                    unit_free[bk], 1)

            def hidden_lo(bk, c, t):
                dve.tensor_tensor(hT[1][:, bass.ds(c, 4), t * P:(t + 1) * P],
                                  bank[bk][:].rearrange("p (c q) -> p c q", q=P),
                                  hT[0][:, bass.ds(c, 4), t * P:(t + 1) * P].bitcast(F32), ALU.subtract).then_inc(
                    unit_free[bk], 1)

            ones = stat[:, 60:64]
            after(dve.memset(ones, 1.0))

            def rstd(root, c0, n, *widths, by=1.0):
                for i, width in enumerate(widths):
                    v = stat[:, c0 + i * n:c0 + (i + 1) * n]
                    ins = dve.tensor_scalar(v, v, by / width, by * EPS, ALU.mult, ALU.add)
                ins.then_inc(mean_ready, 1)
                dve.wait_ge(rstd_ready, root + 1)

            for s, at in SCHEDULE:
                U, B = at["unit"], at["block"]
                if s[0] == "lead" or s[0] == "tile":
                    lead(at["lead"])
                elif s[0] == "ssq":
                    _, n, j, t = s
                    c = slice(512 * j, 512 * j + 512)
                    if n == 3:
                        if (j, t) == (0, 0):
                            dve.wait_ge(gain_in[3], 16)
                        block_read(dve, at["block"], t)
                        if (j, t) == (0, 0):
                            dve.wait_ge(unit_done, LAST_UNIT["u3 of 2"] + 1)
                        dve.tensor_tensor(u[:, t, c], x_sb[:, t, c], gain[:, c], ALU.mult).then_inc(x_gained, 1)
                elif s[0] == "rstd":
                    n, t = s[1], s[2]
                    c = 4 * n + t if n != 3 else 12 + 2 * t
                    dve.wait_ge(squares, at["squares"])
                    ins = dve.tensor_tensor_reduce(sums[:, n, t], sums[:, n, t], ones, 1.0 / D, EPS, ALU.mult, ALU.add,
                                                   stat[:, c:c + 1])
                    if n == 3:
                        after(dve.tensor_tensor_reduce(sums[:, 8, t], sums[:, 8, t], ones, 1.0 / D, 0.0, ALU.mult, ALU.add,
                                                       stat[:, c + 1:c + 2]))
                        ins = dve.scalar_tensor_tensor(out=stat[:, c + 1:c + 2], in0=stat[:, c:c + 1], scalar=EPS,
                                                       in1=stat[:, c + 1:c + 2], op0=ALU.mult, op1=ALU.add)
                    ins.then_inc(mean_ready, 1)
                elif s[0] == "half_rms":
                    dve.wait_ge(rstd_ready, at["root"])
                    dve.tensor_scalar(stat[:, 6:8], stat[:, 4:6], 0.5, None, ALU.mult).then_inc(half_known, 1)
                elif s[0] == "norm_x":
                    _, j, t = s
                    v = x_sb[:, t, 512 * j:512 * j + 512]
                    dve.wait_ge(squares, at["squares"])
                    dve.scalar_tensor_tensor(out=v, in0=v, scalar=stat[:, 12 + 2 * t:13 + 2 * t],
                                             in1=gain[:, 512 * j:512 * j + 512], op0=ALU.mult,
                                             op1=ALU.mult).then_inc(x_normed, 1)
                elif s[0] == "scaled":
                    _, n, j, t = s
                    c = slice(512 * j, 512 * j + 512)
                    r = stat[:, 4 * n + t:4 * n + t + 1]
                    if j < 2:
                        continue
                    dve.wait_ge(rstd_ready, at["root"] + 1)
                    if j == 2:
                        dve.wait_ge(gained, at["gained"] + 1)
                        ins = dve.tensor_scalar(u[:, t, c], u[:, t, c], r, None, ALU.mult)
                    else:
                        dve.wait_ge(gain_in[n], 16)
                        ins = dve.scalar_tensor_tensor(out=u[:, t, c], in0=x_sb[:, t, c], scalar=r, in1=gain[:, c],
                                                       op0=ALU.mult, op1=ALU.mult)
                    ins.then_inc(result_ready[1], 1)
                elif s[0] == "T":
                    name, t = s[1], s[2]
                    _, _, w, n, dst, i0, mode = TRANSPOSES[name]
                    if mode == "split":
                        dve.wait_ge(unit_hi, at["split"] + 1)
                        lo(U % 2, w, n, LHS[dst], i0, t)
                    elif mode == "gain":
                        dve.wait_ge(unit_hi, at["split"] + 1)
                        for c in range(i0, i0 + n):
                            q = slice(t * P, (t + 1) * P)
                            ins = dve.scalar_tensor_tensor(out=memT[1][:, c, q], in0=bank[U % 2][:, (c - i0) * P:(c - i0 + 1) * P],
                                                           scalar=gain_T[:, c:c + 1], in1=memT[0][:, c, q].bitcast(F32),
                                                           op0=ALU.mult, op1=ALU.subtract)
                        ins.then_inc(unit_free[U % 2], 1)
                    elif mode == "dve":
                        if name == "glow" and t == 0:
                            after(dve.memset(glowT[0:32], 1.0))
                        dve.wait_ge(unit_done, U + 1)
                        dve.tensor_copy(DST[dst][0:w, i0:i0 + n, t * P:(t + 1) * P],
                                        bank[U % 2][0:w, 0:n * P].rearrange("p (c q) -> p c q", q=P)).then_inc(
                            unit_free[U % 2], 1)
                elif s[0] == "evac":
                    b, what, arg, n = B, s[1]["evac"], s[1]["arg"], s[1]["n"]
                    last = at["tile"] - 1
                    ac = acc[b % 2]
                    if what == "ckv":
                        acc_ready(dve, b, 1, last)
                        norm_known(dve, 0, 1)
                        dve.tensor_scalar(ckv1[:, arg, 1, :], ac[1][:], over_rms(0, 1), None, ALU.mult).then_inc(
                            acc_free[b % 2][1], 1)
                    elif what in BUF and 1 in s[2]:
                        acc_ready(dve, b, 1, last)
                        norm_known(dve, s[1]["norm"], at["root"])
                        dve.tensor_scalar(BUF[what][:, 1, arg:arg + n], ac[1][:, 0:n], over_rms(s[1]["norm"], 1), None,
                                          ALU.mult).then_inc(acc_free[b % 2][1], 1)
                    elif what == "obg":
                        skip = G_RANK if arg == 0 else 0
                        for t in range(NT):
                            dve.wait_ge(obg_tanh, 2 * (b - BLOCK["obg", 0]) + t + 1)
                            v = obg[:, t, arg:arg + n - skip]
                            dve.scalar_tensor_tensor(out=v, in0=v, scalar=1.0, in1=ac[t][:, skip:n], op0=ALU.add,
                                                     op1=ALU.mult).then_inc(acc_free[b % 2][t], 1)
                    elif what in ("gate_a", "merge"):
                        c = slice(arg, arg + 512)
                        if arg == 0:
                            dve.wait_ge(sig_ready, 16)
                        for t in range(NT):
                            acc_ready(dve, b, t, last)
                            sig = sigA if what == "gate_a" else sigB
                            dve.tensor_tensor(sig[:, t, c], sig[:, t, c], ac[t][:], ALU.mult).then_inc(acc_free[b % 2][t], 1)
                    elif what == "relu2":
                        for t in range(NT):
                            block_read(dve, b, t)
                            v = hb[:, arg, t, :]
                            dve.tensor_tensor(v, v, v, ALU.mult).then_inc(h2_ready, 1)
                    elif what == "glu":
                        for t in range(NT):
                            acc_ready(dve, b, t, last)
                            block_read(dve, b - 1, t)
                            norm_known(dve, s[1]["norm"], at["root"])
                            dve.scalar_tensor_tensor(out=hb[:, 0, t, :], in0=ac[t][:], scalar=over_rms(2, t), in1=sil[:, t, :],
                                                     op0=ALU.mult, op1=ALU.mult).then_inc(acc_free[b % 2][t], 1)
                    elif what == "add":
                        if arg == 0 and s[1]["w"] == "w_out":
                            dve.wait_ge(x_in[1], 16)
                        if arg == 0 and s[1]["w"] == "w_out_2" and s[1]["k0"] == 0:
                            dve.wait_ge(x_normed, 8)
                        for t in s[2]:
                            acc_ready(dve, b, t, last)
                            v = x_sb[:, t, arg:arg + 512]
                            dve.tensor_tensor(v, v, ac[t][:], ALU.add).then_inc(acc_free[b % 2][t], 1)
                elif s[0] == "scores":
                    g = s[1]
                    kind, t, h, nk = GROUPS[g]
                    sb_, _, _, scale, _ = attention(kind)
                    if g == GROUP0["A"]:
                        dve.wait_ge(bias_in, 16)
                        dve.wait_ge(ckv_kept, 16)
                    if g >= 2:
                        dve.wait_ge(exp_done, g - 1)
                    dve.wait_ge(sc_done, g + 1)
                    dst, src = sb_[:, g % 2, :, 0:nk], psS[:, :, 0:nk]
                    if kind == "C":
                        ins = dve.tensor_scalar(dst, src, scale, None, ALU.mult)
                    else:
                        if kind == "A":
                            mask = bias[:, h:h + 2, SEQ - nk:SEQ]
                        elif kind == "M":
                            mask = cst[:, C_CMASK + P - nk:C_CMASK + P].unsqueeze(1).broadcast_to([P, 2, nk])
                        else:
                            mask = sel[:, t, 0:nk].unsqueeze(1).broadcast_to([P, 2, nk])
                        ins = dve.scalar_tensor_tensor(out=dst, in0=src, scalar=scale, in1=mask, op0=ALU.mult, op1=ALU.add)
                    ins.then_inc(sc_read, 1)
                    w = nk
                    if kind == "A":
                        after(dve.tensor_copy(sb_[:, g % 2, :, nk:nk + 1], sinks_b[:, h:h + 2].unsqueeze(2)))
                        w = nk + 1
                    dve.wait_ge(sc_read, g + 1)
                    dve.tensor_reduce(stat[:, 40 + 2 * (g % 2):42 + 2 * (g % 2)], sb_[:, g % 2, :, 0:w], X, ALU.max,
                                      negate=True).then_inc(max_done, 1)
                elif s[0] == "output":
                    g = s[1]
                    kind, t, h, nk = GROUPS[g]
                    dv = attention(kind)[4]
                    dve.wait_ge(exp_done, g + 1)
                    if g:
                        dve.wait_ge(out_done, g)
                    after(dve.reciprocal(stat[:, 118:120], stat[:, 110 + 2 * (g % 4):112 + 2 * (g % 4)]))
                    dve.wait_ge(out_acc, g + 1)
                    dve.tensor_tensor(outputs(kind, t, h, dv), psO[:, :, 0:dv],
                                      stat[:, 118:120].unsqueeze(2).broadcast_to([P, 2, dv]), ALU.mult).then_inc(out_done, 1)
                elif s[0] == "bias_row":
                    dve.wait_ge(const_in, 16)
                    dve.wait_ge(unit_done, U + 1)
                    dve.tensor_copy(brow[:], bank[U % 2][0:A_HEADS, 0:C_BIASW]).then_inc(unit_free[U % 2], 1)
                elif s[0] == "gate_z":
                    t = s[1]
                    dve.wait_ge(unit_done, U + 1)
                    after(dve.tensor_scalar(enb[:, t, :], bank[U % 2][:], 0.0, None, ALU.min))
                    dve.scalar_tensor_tensor(out=eb[:, t, :], in0=enb[:, t, :], scalar=2.0, in1=bank[U % 2][:],
                                             op0=ALU.mult, op1=ALU.subtract).then_inc(unit_free[U % 2], 1)
                elif s[0] == "state":
                    n, h = s[1], s[2]
                    dve.wait_ge(unit_done, U + 1)
                    if n:
                        units_read(dve, U - 1)
                    for i in range(2):
                        dS = bank[U % 2][:, i * G_VAL:(i + 1) * G_VAL]
                        c = 4 * (h + i) + n
                        if n == 0:
                            ins = dve.tensor_copy(state[:, n, h + i, :], dS)
                        else:
                            ins = dve.scalar_tensor_tensor(out=state[:, n, h + i, :], in0=state[:, n - 1, h + i, :],
                                                           scalar=decay[:, c:c + 1], in1=dS, op0=ALU.mult, op1=ALU.add)
                    ins.then_inc(unit_free[U % 2], 1)
                elif s[0] == "gla_att":
                    t = s[1]
                    dve.wait_ge(unit_done, U + 1)
                    dve.scalar_tensor_tensor(out=attT[:, t], in0=bank[U % 2][:].rearrange("p (h c) -> p h c", h=G_HEADS),
                                             scalar=3e38,
                                             in1=cst[:, C_CAUSAL:C_CAUSAL + P].unsqueeze(1).broadcast_to([P, G_HEADS, P]),
                                             op0=ALU.min, op1=ALU.mult).then_inc(unit_free[U % 2], 1)
                elif s[0] == "gla_out" and s[2] == 2:
                    dve.wait_ge(unit_done, U + 1)
                    dve.tensor_copy(gla[:, s[1], 512:1024], bank[U % 2][:]).then_inc(unit_free[U % 2], 1)
                elif s[0] == "gla_norm":
                    dve.wait_ge(head_squares, 8)
                    rstd(at["root"], 50, 8, G_VAL, by=4.0)
                    for t in range(NT):
                        c = 50 + G_HEADS * t
                        after(dve.tensor_scalar(stat[:, c:c + G_HEADS], stat[:, c:c + G_HEADS], over_rms(1, t), None, ALU.mult))
                        for h in range(G_HEADS):
                            v = gla[:, t, G_VAL * h:G_VAL * (h + 1)]
                            c = 50 + 4 * t + h
                            ins = dve.scalar_tensor_tensor(out=v, in0=v, scalar=stat[:, c:c + 1], in1=glag[:],
                                                           op0=ALU.mult, op1=ALU.mult)
                        ins.then_inc(ob_normed, 1)
                elif s[0] == "angles":
                    after(dve.tensor_copy(stat[:, 88:90], pos_i[:]))
                    for t in range(NT):
                        ins = dve.tensor_scalar(ang[:, 0, t, :], cst[:, C_FREQ:C_FREQ + 32], stat[:, 88 + t:89 + t], None,
                                                ALU.mult)
                    after(ins)
                    after(dve.tensor_scalar(ang[:, 1], ang[:, 0], 1.0 / TWO_PI, 0.25, ALU.mult, ALU.add))
                    after(dve.tensor_scalar(ang[:, 2], ang[:, 1], ROUND, -ROUND, ALU.add, ALU.add))
                    after(dve.tensor_scalar(ang[:, 1], ang[:, 0], 1.0 / TWO_PI, None, ALU.mult))
                    after(dve.tensor_scalar(ang[:, 3], ang[:, 1], ROUND, -ROUND, ALU.add, ALU.add))
                    for i, shift in ((2, TWO_PI / 4), (3, 0.0)):
                        src = ang[:, 0]
                        for part in TWO_PI_PARTS:
                            after(dve.scalar_tensor_tensor(out=ang[:, 1], in0=ang[:, i], scalar=-part, in1=src,
                                                           op0=ALU.mult, op1=ALU.add))
                            src = ang[:, 1]
                        after(dve.tensor_scalar(ang[:, i], ang[:, 1], shift, PI_BELOW, ALU.add, ALU.min))
                    dve.tensor_scalar(ang[:, 2:4], ang[:, 2:4], -PI_BELOW, None, ALU.max).then_inc(angles_ready, 1)
                elif s[0] == "idx":
                    t, h, q = s[1], s[2], at["nth"]
                    nk = SEQ if t else P
                    units_read(dve, U)
                    for i in range(2):
                        w = idx[:, t, 1088 + h + i:1089 + h + i]
                        sc = score[:, t, 0:nk]
                        if h + i == 0:
                            ins = dve.tensor_scalar(sc, rel[:, q % 2, i, 0:nk], w, None, ALU.mult)
                        else:
                            ins = dve.scalar_tensor_tensor(out=sc, in0=rel[:, q % 2, i, 0:nk], scalar=w, in1=sc,
                                                           op0=ALU.mult, op1=ALU.add)
                        if i == 0:
                            after(ins)
                    ins.then_inc(rel_used, 1)
                    dve.wait_ge(rel_used, q + 1)
                elif s[0] == "topk":
                    t, r = s[1], s[2]
                    nk = SEQ if t else P
                    sc, wk = score[:, t, 0:nk], work[:, t, 0:nk]
                    if r == 0:
                        dve.wait_ge(c_normed, 4)
                        after(dve.tensor_tensor(sc, sc, cst[:, C_CMASK + P - nk:C_CMASK + P], ALU.add))
                    src = sc if r == 0 else wk
                    after(dve.max(stat[:, 80:88], src))
                    after(dve.match_replace(out=wk, in_to_replace=stat[:, 80:88], in_values=src, imm_value=-3e38))
                    if r == TOPK // 8 - 1:
                        after(dve.tensor_scalar(sel[:, t, 0:nk], wk, -2e38, NEG, ALU.is_gt, ALU.mult))
                elif s[0] == "c_norm":
                    dve.wait_ge(c_squares, 4)
                    rstd(at["root"], 66, 2, 512, 256)
                    dve.wait_ge(gcq_in, 32)
                    for i, (c0, n) in enumerate(((0, 512), (512, 256))):
                        for t in range(NT):
                            v = c_sb[:, t, c0:c0 + n]
                            dve.scalar_tensor_tensor(out=v, in0=v, scalar=stat[:, 66 + 2 * i + t:67 + 2 * i + t],
                                                     in1=gcq[:, c0:c0 + n], op0=ALU.mult, op1=ALU.mult).then_inc(c_normed, 1)
                elif s[0] in ("swiglu_up", "relu2_up"):
                    glu, n = s[0] == "swiglu_up", s[2]
                    T0, B, S0 = at["tile"] - 16, B - 2, at["split"] - (0 if glu else 2)
                    with dve.Fori(1, n if glu else n // 2) as r:
                        for k in range(8):
                            lead(T0 + k + LEAD, r * 16)
                        if not glu:
                            for t in range(NT):
                                dve.wait_ge(acc_free[0][t], B // 2 + 1 + r)
                                dve.tensor_tensor(hb[:, 0, t, :], hb[:, 0, t, :], hb[:, 0, t, :], ALU.mult).then_inc(h2_ready, 1)
                        for t in range(NT):
                            dve.wait_ge(unit_hi, S0 - 2 + t + 1 + r * (2 if glu else 4))
                            hidden_lo(t, (r - 1) * 4 if glu else (r - 1) * 8 + 4, t)
                        for k in range(8):
                            lead(T0 + 8 + k + LEAD, r * 16)
                        for t in range(NT):
                            if glu:
                                if t == 0:
                                    dve.wait_ge(acc0_done, B + 2 + r * 2)
                                else:
                                    dve.wait_ge(tile_done, T0 + 16 + r * 16)
                                dve.wait_ge(acc_free[0][t], B // 2 + 1 + r)
                                dve.scalar_tensor_tensor(out=hb[:, 0, t, :], in0=acc[1][t][:], scalar=over_rms(2, t),
                                                         in1=sil[:, t, :], op0=ALU.mult, op1=ALU.mult).then_inc(
                                    acc_free[1][t], 1)
                            else:
                                dve.wait_ge(acc_free[1][t], B // 2 + 1 + r)
                                dve.tensor_tensor(hb[:, 1, t, :], hb[:, 1, t, :], hb[:, 1, t, :], ALU.mult).then_inc(h2_ready, 1)
                        if not glu:
                            for t in range(NT):
                                dve.wait_ge(unit_hi, S0 + t + 1 + r * 4)
                                hidden_lo(t, r * 8, t)
                elif s[0] == "down":
                    n, T0 = s[3] // CK, at["tile"]

                    with dve.Fori(0, 2) as r:
                        for j in range(2):
                            for k in range(n):
                                lead(T0 + n * j + k + LEAD, r * (2 * n))
                            for t in range(NT):
                                if t == 0:
                                    dve.wait_ge(acc0_done, B + j + 1 + r * 2)
                                else:
                                    dve.wait_ge(tile_done, T0 + n * (j + 1) + r * (2 * n))
                                v = x_sb[:, t, bass.ds(r * 1024 + 512 * j, 512)]
                                dve.tensor_tensor(v, v, acc[j][t][:], ALU.add).then_inc(acc_free[j][t], 1)


def kernel(**inputs):
    import numpy as _np
    import concourse.bacc as _bacc
    from concourse import mybir as _mybir
    from concourse.bass_utils import run_bass_kernel_spmd as _run

    nc = _bacc.Bacc("TRN2", target_bir_lowering=False, num_devices=1)
    arrays, t_in = {}, {}
    for name, a in [*inputs.items(), ("const", constants())]:
        a = _np.ascontiguousarray(a)
        arrays[f"in_{name}"] = a
        t_in[name] = nc.dram_tensor(f"in_{name}", a.shape, _mybir.dt.from_np(a.dtype), kind="ExternalInput").ap()
        if name.startswith("w_"):
            t_in[name] = t_in[name][0]
    out = nc.dram_tensor("out_0", (1, SEQ, D), _mybir.dt.float32, kind="ExternalOutput").ap()
    build(nc, t_in, out)
    r = _run(nc, [arrays], core_ids=[0])
    return r.results[0]["out_0"]
```
